# Optimizing a Trainium2 kernel written in Bass

```python
import jax, jax.numpy as jnp
from jax import lax
import numpy as np

D_MODEL = 1024
BATCH = 1
SEQ = 512
DEPTH = 2

CHUNK = 64
SUB = 8
EPS = 1e-6
D_FF = 4 * D_MODEL
HALF_MIX = D_MODEL // 2

HG_DK = 128
HG_HEADS = HALF_MIX // 128
HG_DV = HALF_MIX // HG_HEADS
HG_KD = HG_HEADS * HG_DK
HG_VD = HG_HEADS * HG_DV

GLA_HEADS = HALF_MIX // 128
GLA_DV = HALF_MIX // GLA_HEADS
GLA_DK = GLA_DV // 2
GLA_KD = GLA_HEADS * GLA_DK
GLA_VD = GLA_HEADS * GLA_DV
GLA_GATE_RANK = 16
GLA_GATE_TEMP = 16.0

EVEN_SPLITS = (HG_KD, HG_KD, HG_VD, HG_VD, GLA_KD, GLA_KD, GLA_VD, GLA_VD, GLA_GATE_RANK)
EVEN_IN = 2 * HG_KD + 2 * HG_VD + 2 * GLA_KD + 2 * GLA_VD + GLA_GATE_RANK
EVEN_MIX = HG_VD + GLA_VD

MLA_HEADS = D_MODEL // 128
MLA_Q_RANK = 3 * D_MODEL // 8
MLA_KV_RANK = D_MODEL // 4
MLA_NOPE = 128
MLA_ROPE = 64
MLA_V = 128
ODD_SPLITS = (MLA_Q_RANK, MLA_KV_RANK, MLA_ROPE)
ODD_IN = MLA_Q_RANK + MLA_KV_RANK + MLA_ROPE
ROPE_THETA = 10000.0
Q_BLOCK = 128
MAX_POS_OFFSET = 8192

N_EVEN = (DEPTH + 1) // 2
N_ODD = DEPTH // 2

kernel_name = 'hybrid_hgrn2_gla_mla_trunk'

def split_cols(a, sizes):
    parts, start = [], 0
    for size in sizes:
        parts.append(a[..., start:start + size])
        start += size
    return parts

def rmsnorm(x, g):
    xf = x.astype(jnp.float32)
    y = xf * lax.rsqrt(jnp.mean(xf * xf, axis=-1, keepdims=True) + EPS)
    return (y * g.astype(jnp.float32)).astype(x.dtype)

def chunk_gated_linear_attention(q, k, v, log_g):
    B, T, H, DK = q.shape
    DV = v.shape[-1]
    NC, NS = T // CHUNK, CHUNK // SUB
    out_dtype = v.dtype
    f32 = jnp.float32

    def blocks(a):
        return a.astype(f32).reshape(B, NC, NS, SUB, H, a.shape[-1]).transpose(0, 4, 1, 2, 3, 5)

    q, k, v, lg = blocks(q), blocks(k), blocks(v), blocks(log_g)
    b = jnp.cumsum(lg.reshape(B, H, NC, CHUNK, DK), axis=3).reshape(B, H, NC, NS, SUB, DK)
    r = b[..., -1, :]

    tri = jnp.tril(jnp.ones((SUB, SUB), dtype=bool))[:, :, None]
    dd = b[..., :, None, :] - b[..., None, :, :]
    decay_diag = jnp.exp(jnp.where(tri, dd, -jnp.inf))
    a_diag = jnp.einsum('bhcitsd,bhcisd->bhcits', q[..., :, None, :] * decay_diag, k)

    qo = q[..., None, :] * jnp.exp(jnp.minimum(b[..., None, :] - r[:, :, :, None, None, :, :], 0.0))
    ko = k * jnp.exp(r[..., None, :] - b)
    before = (jnp.arange(NS)[None, :] < jnp.arange(NS)[:, None]).astype(f32)
    a_off = jnp.einsum('bhcitjd,bhcjsd->bhcitjs', qo, ko) * before[:, None, :, None]
    eye = jnp.eye(NS, dtype=f32)[:, None, :, None]
    a_full = (a_off + a_diag[..., :, :, None, :] * eye).reshape(B, H, NC, CHUNK, CHUNK)

    qc, kc, vc, bc = (a.reshape(B, H, NC, CHUNK, a.shape[-1]) for a in (q, k, v, b))
    o_intra = jnp.einsum('bhcts,bhcsv->bhctv', a_full, vc)
    last = bc[..., -1, :]
    kv = jnp.einsum('bhcsd,bhcsv->bhcdv', kc * jnp.exp(last[..., None, :] - bc), vc)

    def carry_state(state, inp):
        decay, kv_c = inp
        return decay[..., None] * state + kv_c, state

    _, s_prev = lax.scan(carry_state, jnp.zeros((B, H, DK, DV), f32),
                         (jnp.moveaxis(jnp.exp(last), 2, 0), jnp.moveaxis(kv, 2, 0)))
    s_prev = jnp.moveaxis(s_prev, 0, 2)
    o_inter = jnp.einsum('bhctd,bhcdv->bhctv', qc * jnp.exp(bc), s_prev)
    o = (o_intra + o_inter).transpose(0, 2, 3, 1, 4).reshape(B, T, H, DV)
    return o.astype(out_dtype)

def hgrn2_gla_mixer(h, w_in, lb, w_gate, b_gate, hg_norm, gla_norm, w_out):
    B, T, _ = h.shape
    f32 = jnp.float32
    hq, hf, hi, hg, gq, gk, gv, gr, ga = split_cols(h @ w_in, EVEN_SPLITS)

    def heads(a, n):
        return a.reshape(B, T, n, -1)

    forget = lb + (1.0 - lb) * jax.nn.sigmoid(hf.astype(f32))
    o_a = chunk_gated_linear_attention(heads(hq, HG_HEADS), heads(1.0 - forget, HG_HEADS),
                                       heads(hi, HG_HEADS), heads(jnp.log(forget), HG_HEADS))
    o_a = rmsnorm(o_a, hg_norm).reshape(B, T, HG_VD) * jax.nn.silu(hg)

    log_alpha = jax.nn.log_sigmoid((ga @ w_gate + b_gate).astype(f32)) / GLA_GATE_TEMP
    o_b = chunk_gated_linear_attention(heads(gq * GLA_DK ** -0.5, GLA_HEADS), heads(gk, GLA_HEADS),
                                       heads(gv, GLA_HEADS), heads(log_alpha, GLA_HEADS))
    o_b = rmsnorm(o_b, gla_norm).reshape(B, T, GLA_VD) * jax.nn.silu(gr)

    return jnp.concatenate([o_a, o_b], axis=-1) @ w_out

def rope(x, cos, sin):
    half = x.shape[-1] // 2
    x1 = x[..., :half].astype(jnp.float32)
    x2 = x[..., half:].astype(jnp.float32)
    return jnp.concatenate([x1 * cos - x2 * sin, x2 * cos + x1 * sin], axis=-1).astype(x.dtype)

def chunk_causal_attention(q_nope, q_rope, k_nope, k_rope, v):
    B, T, H, _ = q_nope.shape
    NB = T // Q_BLOCK
    scale = (MLA_NOPE + MLA_ROPE) ** -0.5
    key_chunk = jnp.arange(T) // CHUNK

    def one_block(inp):
        qn, qr, blk = inp
        s = (jnp.einsum('bqhd,bkhd->bhqk', qn, k_nope)
             + jnp.einsum('bqhd,bkd->bhqk', qr, k_rope)).astype(jnp.float32) * scale
        q_chunk = (blk * Q_BLOCK + jnp.arange(Q_BLOCK)) // CHUNK
        s = jnp.where(key_chunk[None, :] <= q_chunk[:, None], s, -jnp.inf)
        p = jax.nn.softmax(s, axis=-1).astype(v.dtype)
        return jnp.einsum('bhqk,bkhv->bqhv', p, v)

    def qblocks(a):
        return a.reshape(B, NB, Q_BLOCK, H, a.shape[-1]).transpose(1, 0, 2, 3, 4)

    out = lax.map(one_block, (qblocks(q_nope), qblocks(q_rope), jnp.arange(NB)))
    return out.transpose(1, 0, 2, 3, 4).reshape(B, T, H * MLA_V)

def mla_mixer(h, positions, w_in, q_norm, w_uq, kv_norm, w_ukv, w_out):
    B, T, _ = h.shape
    c_q, c_kv, k_rope = split_cols(h @ w_in, ODD_SPLITS)
    q = (rmsnorm(c_q, q_norm) @ w_uq).reshape(B, T, MLA_HEADS, MLA_NOPE + MLA_ROPE)
    kv = (rmsnorm(c_kv, kv_norm) @ w_ukv).reshape(B, T, MLA_HEADS, MLA_NOPE + MLA_V)
    q_nope, q_rope = q[..., :MLA_NOPE], q[..., MLA_NOPE:]
    k_nope, v = kv[..., :MLA_NOPE], kv[..., MLA_NOPE:]
    inv_freq = ROPE_THETA ** (-jnp.arange(0, MLA_ROPE, 2, dtype=jnp.float32) / MLA_ROPE)
    ang = positions.astype(jnp.float32)[..., None] * inv_freq
    cos, sin = jnp.cos(ang), jnp.sin(ang)
    q_rope = rope(q_rope, cos[:, :, None, :], sin[:, :, None, :])
    k_rope = rope(k_rope, cos, sin)
    return chunk_causal_attention(q_nope, q_rope, k_nope, k_rope, v) @ w_out

def sq_relu_mlp(h, w1, w2):
    return jnp.square(jax.nn.relu(h @ w1)) @ w2

def setup_inputs(seed: int = 0) -> dict:
    key = jax.random.key(seed)
    ks = jax.random.split(key, 18)
    f32 = jnp.float32

    def dense(k, shape):
        return jax.random.normal(k, shape, f32) * shape[-2] ** -0.5

    def gain(k, shape):
        return 1.0 + 0.02 * jax.random.normal(k, shape, f32)

    x = jax.random.normal(ks[0], (BATCH, SEQ, D_MODEL), f32)
    offset = jax.random.randint(ks[1], (BATCH, 1), 0, MAX_POS_OFFSET, dtype=jnp.int32)
    positions = offset + jnp.arange(SEQ, dtype=jnp.int32)[None, :]
    return {
        'x': x,
        'positions': positions,
        'norm_gains': gain(ks[2], (DEPTH, 4, D_MODEL)),
        'ev_w_in': dense(ks[3], (N_EVEN, D_MODEL, EVEN_IN)),
        'hg_lb_table': 0.5 * jax.random.normal(ks[4], (N_EVEN + 1, HG_KD), f32),
        'gla_w_gate': dense(ks[5], (N_EVEN, GLA_GATE_RANK, GLA_KD)),
        'gla_b_gate': 0.1 * jax.random.normal(ks[6], (N_EVEN, GLA_KD), f32),
        'hg_out_norm': gain(ks[7], (N_EVEN, HG_DV)),
        'gla_out_norm': gain(ks[8], (N_EVEN, GLA_DV)),
        'ev_w_out': dense(ks[9], (N_EVEN, EVEN_MIX, D_MODEL)),
        'od_w_in': dense(ks[10], (N_ODD, D_MODEL, ODD_IN)),
        'mla_q_norm': gain(ks[11], (N_ODD, MLA_Q_RANK)),
        'mla_w_uq': dense(ks[12], (N_ODD, MLA_Q_RANK, MLA_HEADS * (MLA_NOPE + MLA_ROPE))),
        'mla_kv_norm': gain(ks[13], (N_ODD, MLA_KV_RANK)),
        'mla_w_ukv': dense(ks[14], (N_ODD, MLA_KV_RANK, MLA_HEADS * (MLA_NOPE + MLA_V))),
        'od_w_out': dense(ks[15], (N_ODD, MLA_HEADS * MLA_V, D_MODEL)),
        'mlp_w1': dense(ks[16], (DEPTH, D_MODEL, D_FF)),
        'mlp_w2': dense(ks[17], (DEPTH, D_FF, D_MODEL)),
    }

def reference(x, positions, norm_gains, ev_w_in, hg_lb_table, gla_w_gate, gla_b_gate,
              hg_out_norm, gla_out_norm, ev_w_out, od_w_in, mla_q_norm, mla_w_uq,
              mla_kv_norm, mla_w_ukv, od_w_out, mlp_w1, mlp_w2):
    lb_all = jnp.cumsum(jax.nn.softmax(hg_lb_table.astype(jnp.float32), axis=0), axis=0)[:N_EVEN]
    for l in range(DEPTH):
        h = rmsnorm(x, norm_gains[l, 0])
        if l % 2 == 0:
            e = l // 2
            m = hgrn2_gla_mixer(h, ev_w_in[e], lb_all[e], gla_w_gate[e], gla_b_gate[e],
                                hg_out_norm[e], gla_out_norm[e], ev_w_out[e])
        else:
            o = l // 2
            m = mla_mixer(h, positions, od_w_in[o], mla_q_norm[o], mla_w_uq[o],
                          mla_kv_norm[o], mla_w_ukv[o], od_w_out[o])
        x = x + rmsnorm(m, norm_gains[l, 1])
        h = rmsnorm(x, norm_gains[l, 2])
        x = x + rmsnorm(sq_relu_mlp(h, mlp_w1[l], mlp_w2[l]), norm_gains[l, 3])
    return x


_drawn_inputs = setup_inputs


def setup_inputs(seed=0):
    import zlib

    import numpy as np

    out = dict(_drawn_inputs(seed))
    spreads = {}
    factors = {'hg_out_norm': 5.228, 'gla_out_norm': 5.345, 'mla_q_norm': 8.0, 'mla_kv_norm': 4.675}
    for name, (base, spread) in spreads.items():
        noise = np.random.default_rng([zlib.crc32(name.encode()), seed]).standard_normal(out[name].shape)
        drawn = base * np.exp(spread * noise) if base else spread * noise
        out[name] = __import__('jax').numpy.asarray(drawn.astype(out[name].dtype))
    for name, factor in factors.items():
        out[name] = (out[name] * factor).astype(out[name].dtype)
    return out
```

```python
from contextlib import ExitStack

import concourse.bass as bass
from concourse import mybir

ALU = mybir.AluOpType
ACT = mybir.ActivationFunctionType
F32 = mybir.dt.float32
F32R = mybir.dt.float32r
I32 = mybir.dt.int32
AX_X = mybir.AxisListType.X

P = 128
T = 512
D = 1024
KD = D // P
NT = T // P
F = 4 * D
GROUPS = F // D
EPS = 1e-6
HEADS = 4
GLA_DK = 64
GATE_RANK = 16
GATE_TEMP = 16.0
LEVELS = 7
Q_RANK_T, KV_RANK_T = 3, 2
MLA_HEADS = 8
NOPE, ROPE, VDIM = 128, 64, 128
SCALE = float(NOPE + ROPE) ** -0.5
MASKED = -1e30

HQ, HF, HI, HG, GQ, GK, GV, GR, GA = 0, 512, 1024, 1536, 2048, 2304, 2560, 3072, 3584
V_LB, V_BG, V_HGN, V_GLN, V_QN, V_KVN, V_ROWS = 64, 72, 74, 75, 76, 79, 81

STAGE, SPLIT = 2, 4
UNIT = KD * P

TWO_PI_A, TWO_PI_B, TWO_PI_C = 6.28125, 0.0019350051879882812, 3.0199159819567e-07
MAGIC = 12582912.0
PI_IN = 3.1415925


def trunk(nc, x, positions, norm_gains, ev_w_in, hg_lb_table, gla_w_gate, gla_b_gate, hg_out_norm,
          gla_out_norm, ev_w_out, od_w_in, mla_q_norm, mla_w_uq, mla_kv_norm, mla_w_ukv, od_w_out,
          mlp_w1, mlp_w2, rope_const, out):

    PACKS = [("hg", 0), ("hg", 1), ("hg", 2), ("hg", 3), ("gla", 0), ("gla", 1)]

    def pack_tiles(p):
        kind, a = PACKS[p]
        if kind == "hg":
            return [("f", a, HF + a * P), ("g", a, HG + a * P), ("q", a, HQ + a * P), ("v", a, HI + a * P)]
        return [("g", 4 + 2 * a, GR + 2 * a * P), ("g", 5 + 2 * a, GR + (2 * a + 1) * P),
                ("k", a, GK + a * P), ("q", a, GQ + a * P), ("z", a, None),
                ("v", 2 * a, GV + 2 * a * P), ("v", 2 * a + 1, GV + (2 * a + 1) * P)]

    def rows(w, c0, c1):
        return w[:, c0:c1].rearrange("(k p) c -> p k c", p=P)

    units = []
    tile_of_unit = []
    tile_no = {}
    unit_no = {}

    def add_tile(name, unit=None):
        tile_no[name] = len(tile_no)
        if unit is not None:
            tile_of_unit[unit] = tile_no[name]

    def add_unit(name, loads):
        unit_no[name] = len(units)
        units.append(loads)
        tile_of_unit.append(None)
        return unit_no[name]

    for k in range(KD):
        add_tile(("x", k))
    w = ev_w_in[0]
    add_tile(("ga", 0), add_unit(("ga", 0), [((KD, GATE_RANK), 0, GATE_RANK, rows(w, GA, GA + GATE_RANK))]))
    for p in range(len(PACKS)):
        for what, a, col in pack_tiles(p):
            add_tile((p, what, a), None if col is None else add_unit(
                (p, what, a), [((KD, P), 0, P, rows(w, col, col + P))]))
    for m in range(KD):
        add_tile(("eo", m), add_unit(("eo", m), [((KD, P), 0, P, rows(ev_w_out[0], m * P, (m + 1) * P))]))

    def add_mlp(layer):
        for g in range(GROUPS):
            for m in range(2 * KD):
                add_tile(("mlp", layer, g, m), add_unit(("mlp", layer, g, m), None))

    add_mlp(0)
    w = od_w_in[0]
    for m in range(5):
        add_tile(("oi", m), add_unit(("oi", m), [((KD, P), 0, P, rows(w, m * P, (m + 1) * P))]))
    R0, RH = 5 * P, ROPE // 2
    add_tile(("oi", 5), add_unit(("oi", 5), [((KD, P), c, c + ROPE, rows(w, R0, R0 + ROPE)) for c in (0, ROPE)]))
    add_tile(("oi", 6), add_unit(("oi", 6), [((KD, P), c + d, c + d + RH, rows(w, R0 + RH - d, R0 + 2 * RH - d))
                                             for c in (0, ROPE) for d in (0, RH)]))
    w = mla_w_ukv[0].rearrange("(k p) (h c) -> k p h c", p=P, c=NOPE + VDIM)
    for what, c0 in (("mv", NOPE), ("mk", 0)):
        for g in range(2):
            u = add_unit((what, g), [((KV_RANK_T, 4 * P), None, k, w[k, :, 4 * g:4 * g + 4, c0:c0 + P])
                                     for k in range(KV_RANK_T)])
            for j in range(4):
                add_tile((what, g, j), u)
    w = mla_w_uq[0]
    for a in range(MLA_HEADS // 2):
        c = 2 * a * (NOPE + ROPE)
        u = add_unit(("qn", a), [((Q_RANK_T, 2 * P), hh * P, (hh + 1) * P, rows(w, c + hh * 192, c + hh * 192 + NOPE))
                                 for hh in range(2)])
        add_tile(("qn", a, 0), u)
        add_tile(("qn", a, 1), u)
        loads = [((Q_RANK_T, 2 * P), hh * ROPE, (hh + 1) * ROPE, rows(w, c + hh * 192 + NOPE, c + (hh + 1) * 192))
                 for hh in range(2)]
        for hh in range(2):
            r0 = c + hh * 192 + NOPE
            loads += [((Q_RANK_T, 2 * P), P + hh * ROPE + d, P + hh * ROPE + d + RH,
                       rows(w, r0 + RH - d, r0 + 2 * RH - d)) for d in (0, RH)]
        u = add_unit(("qr", a), loads)
        add_tile(("qr", a, 0), u)
        add_tile(("qr", a, 1), u)
    for m in range(KD):
        add_tile(("oo", m), add_unit(("oo", m), [((KD, P), 0, P, rows(od_w_out[0], m * P, (m + 1) * P))]))
    add_mlp(1)
    for m in range(2 * NT):
        add_tile(("out", m))
    n_units = len(units)
    loaded = []
    for u, loads in enumerate(units):
        loaded.append((loaded[u - STAGE] if u >= STAGE else 0) + 16 * (1 if loads is None else len(loads)))

    def unit_size(u):
        return UNIT if units[u] is None else units[u][0][0][0] * units[u][0][0][1]

    with ExitStack() as ctx:
        def sb(name, shape, dt=F32, scope=ctx):
            return scope.enter_context(nc.sbuf_tensor(name, shape, dt))

        def sem(name):
            return ctx.enter_context(nc.semaphore(name))

        xT = sb("xT", [P, KD, T])
        h_hi = sb("h_hi", [P, KD, T], F32R)
        h_lo = sb("h_lo", [P, KD, T], F32R)
        a_hi = sb("a_hi", [P, KD, T], F32R)
        a_lo = sb("a_lo", [P, KD, T], F32R)
        y = sb("y", [P, KD, T])
        stage = sb("stage", [P, STAGE, UNIT])
        w_hi = sb("w_hi", [P, SPLIT, UNIT], F32R)
        w_lo = sb("w_lo", [P, SPLIT, UNIT], F32R)
        ident = sb("ident", [P, P])
        ones = sb("ones", [P, P])
        eps = sb("eps", [P, 1])
        masks = sb("masks", [P, LEVELS + 1, P])
        vec = sb("vec", [P, V_ROWS])
        lbt = sb("lbt", [P, 6, HEADS])
        w_gate = sb("w_gate", [GATE_RANK, HEADS * GLA_DK])
        ropec = sb("ropec", [P, 2])
        sq = sb("sq", [P, 2, T])
        tmp = sb("tmp", [P, 2, T])
        rinv = sb("rinv", [P, 2, T])

        with ExitStack() as s1:
            x_tok = sb("x_tok", [P, NT, D], F32, s1)
            vrows = sb("vrows", [V_ROWS, P], F32, s1)
        with ExitStack() as s2:
            vbuf = sb("vbuf", [P, 4, T], F32, s2)
            xl = sb("xl", [P, LEVELS, T], F32, s2)
            dec = sb("dec", [P, 3, T], F32, s2)
            q_sb = sb("q_sb", [P, 2, T], F32, s2)
            k_sb = sb("k_sb", [P, 2, T], F32, s2)
            b_sb = sb("b_sb", [P, T], F32, s2)
            qe = sb("qe", [P, T], F32, s2)
            ke = sb("ke", [P, T], F32, s2)
            e_last = sb("e_last", [P, NT], F32, s2)
            a_sb = sb("a_sb", [P, 4, P], F32, s2)
            ke_t = sb("ke_t", [P, NT - 1, P], F32, s2)
            state = sb("state", [P, NT - 1, P], F32, s2)
            t_f = sb("t_f", [P, T], F32, s2)
            t_g = sb("t_g", [P, T], F32, s2)
            ga_t = sb("ga_t", [GATE_RANK, T], F32, s2)
        with ExitStack() as s3:
            v_tok = sb("v_tok", [P, NT, D], F32, s3)
            kr = sb("kr", [P, T], F32, s3)
            cosd = sb("cosd", [P, T], F32, s3)
            sind = sb("sind", [P, T], F32, s3)
            ang = sb("ang", [P, T], F32, s3)
            qn = sb("qn", [P, 2, 2, T], F32, s3)
            qr = sb("qr", [P, 2, T], F32, s3)
            prob = sb("prob", [P, 3, T], F32, s3)
            p_t = sb("p_t", [P, NT, T], F32, s3)
            pos_i = p_t[:, 0, :].bitcast(I32)
            mask_q = sb("mask_q", [P, P], F32, s3)
            mask_k = sb("mask_k", [P, P], F32, s3)
            stat = sb("stat", [P, 3, 4 * MLA_HEADS], F32, s3)

        bank = [ctx.enter_context(nc.psum_tensor(f"bank{b}", [P, T], F32)) for b in range(2)]
        pp = [ctx.enter_context(nc.psum_tensor(f"pp{b}", [P, LEVELS + 1, P], F32)) for b in range(2)]
        po = ctx.enter_context(nc.psum_tensor("po", [P, T], F32))
        misc = ctx.enter_context(nc.psum_tensor("misc", [P, T], F32))
        s_bank = [pp[0][:, 0:4, :], pp[0][:, 4:8, :], pp[1][:, 0:4, :]]
        s_bank = [v.rearrange("p a b -> p (a b)") for v in s_bank]
        t_bank = [pp[1][:, 4:8, :], misc[:, :].rearrange("p (a b) -> p a b", a=4)]

        x_in = [sem(f"x_in{i}") for i in range(4)]
        vec_in, consts_ready, vec_done = sem("vec_in"), sem("consts_ready"), sem("vec_done")
        vec_ready, pos_in, out_stored = sem("vec_ready"), sem("pos_in"), sem("out_stored")
        stage_in = [sem(f"stage_in{s}") for s in range(STAGE)]
        hi_ready, lo_ready = sem("hi_ready"), sem("lo_ready")
        tile_done = sem("tile_done")
        act_chain, dve_chain, pool_chain = sem("act_chain"), sem("dve_chain"), sem("pool_chain")
        x_ready = sem("x_ready")
        y_ready = {j: sem(f"y_ready{j}") for j in (1, 3, 5, 7)}
        sq_ready = [sem(f"sq_ready{j}") for j in range(9)]
        sq_used = [sem(f"sq_used{j}") for j in range(9)]
        r_ready = [sem(f"r_ready{j}") for j in range(9)]
        h_f32, h_high, h_ready = sem("h_f32"), sem("h_high"), sem("h_ready")
        f_sig, f_gate, f_log, b_ready = sem("f_sig"), sem("f_gate"), sem("f_log"), sem("b_ready")
        g_sig, gate_ready, q_ready, k_ready = sem("g_sig"), sem("gate_ready"), sem("q_ready"), sem("k_ready")
        v_ready, ga_ready, d_ready, e_ready = sem("v_ready"), sem("ga_ready"), sem("d_ready"), sem("e_ready")
        xl_ready, ket_done, ket_ready = sem("xl_ready"), sem("ket_done"), sem("ket_ready")
        kv_done, state_ready, p_done, p_read = sem("kv_done"), sem("state_ready"), sem("p_done"), sem("p_read")
        a_ready, o_done, o_sq, o_sum = sem("a_ready"), sem("o_done"), sem("o_sq"), sem("o_sum")
        o_rinv, o_read, mix_f32, mix_high, mix_ready = (sem("o_rinv"), sem("o_read"), sem("mix_f32"),
                                                        sem("mix_high"), sem("mix_ready"))
        c_ready, rope_ready, vt_ready, kt_ready = sem("c_ready"), sem("rope_ready"), sem("vt_ready"), sem("kt_ready")
        sin_arg, sin_ready, qn_ready, qr_ready = sem("sin_arg"), sem("sin_ready"), sem("qn_ready"), sem("qr_ready")
        s_done, nmax_ready, prob_exp, prob_ready = sem("s_done"), sem("nmax_ready"), sem("prob_exp"), sem("prob_ready")
        pt_done, pt_ready, pv_done, att_high, att_ready = (sem("pt_done"), sem("pt_ready"), sem("pv_done"),
                                                           sem("att_high"), sem("att_ready"))
        relu_ready = [sem(f"relu_ready{l}") for l in range(2)]
        hid_f32 = [sem(f"hid_f32_{l}") for l in range(2)]
        hid_high = [sem(f"hid_high{l}") for l in range(2)]
        hid_ready = [sem(f"hid_ready{l}") for l in range(2)]
        y_zero = [sem(f"y_zero{l}") for l in range(2)]
        z_read, kr_read, rot_read = sem("z_read"), sem("kr_read"), sem("rot_read")
        out_ready = sem("out_ready")

        read = {}

        def says(name, s, value):
            read[tile_no[name]] = (s, value)

        for k in range(KD):
            says(("x", k), x_ready, k + 1)
            says(("eo", k), y_ready[1], k + 1)
            says(("oo", k), y_ready[5], k + 1)
            says(("out", k), out_ready, k + 1)
            for layer, j in ((0, 3), (1, 7)):
                for g in range(GROUPS):
                    says(("mlp", layer, g, k), hid_f32[layer], g * KD + k + 1)
                    says(("mlp", layer, g, KD + k), y_ready[j], g * KD + k + 1)
            if k < 7:
                says(("oi", k), c_ready if k < 5 else kr_read, k + 1 if k < 5 else k - 4)
            says(("mv", k // 4, k % 4), vt_ready, k + 1)
            says(("mk", k // 4, k % 4), kt_ready, k + 1)
            says(("qn", k // 2, k % 2), qn_ready, k + 1)
            says(("qr", k // 2, k % 2), rot_read, k + 1)
        says(("ga", 0), ga_ready, 1)
        for p in range(len(PACKS)):
            for what, a, _ in pack_tiles(p):
                s_, v_ = {"f": (f_sig, p + 1), "g": (gate_ready, a + 1), "q": (q_ready, p + 1), "k": (k_ready, a + 1),
                          "z": (z_read, a + 1), "v": (v_ready, (a if p < 4 else 4 + a) + 1)}[what]
                says((p, what, a), s_, v_)

        def wait_read(eng, n):
            eng.wait_ge(*read[n])

        def wait_bank(eng, n, i=None):
            if i is None:
                if n >= 2:
                    wait_read(eng, n - 2)
            else:
                s, value = read[n - 2]
                eng.wait_ge(s, value + KD * (i - 1))

        def wait_tile(eng, n, i=0):
            eng.wait_ge(tile_done, n + 1 + 16 * i)

        def split_high(act, u, i=0):
            if u >= n_units:
                return
            act.wait_ge(stage_in[u % STAGE], loaded[u] + 16 * (16 // STAGE) * i)
            if u >= SPLIT:
                act.wait_ge(tile_done, tile_of_unit[u - SPLIT] + 1 + 16 * i)
            n = unit_size(u)
            nc.scalar.copy(w_hi[:, u % SPLIT, 0:n], stage[:, u % STAGE, 0:n]).then_inc(hi_ready, 1)

        def split_low(dve, u, i=0):
            if u >= n_units:
                return
            dve.wait_ge(hi_ready, u + 1 + 16 * i)
            n = unit_size(u)
            nc.vector.tensor_tensor(w_lo[:, u % SPLIT, 0:n], stage[:, u % STAGE, 0:n],
                                    w_hi[:, u % SPLIT, 0:n].bitcast(F32), ALU.subtract).then_inc(lo_ready, 1)

        AHEAD_HI, AHEAD_LO = SPLIT, SPLIT - 1

        class Chain:
            def __init__(self, eng, s):
                self.eng, self.sem, self.n = eng, s, 0

            def link(self, ins, i=0, per=0):
                self.n += 1
                ins.then_inc(self.sem, 1)
                self.eng.wait_ge(self.sem, self.n + per * i)

        def halves(ap, L):
            return ap.rearrange("p (b h j) -> p b h j", h=2, j=L)

        def gain(layer, n, k):
            c = (layer * 4 + n) * KD + k
            return vec[:, c:c + 1]

        block = ctx.enter_context(nc.Block())

        @block.sync
        def _(sp):
            for i in range(4):
                c = slice(i * 2 * P, (i + 1) * 2 * P)
                sp.dma_start(x_tok[:, :, c], x[0].rearrange("(t p) d -> p t d", p=P)[:, :, c]).then_inc(x_in[i], 16)

            def stage_free(u, i=0):
                if u >= STAGE:
                    sp.wait_ge(hi_ready, u - STAGE + 1 + 16 * i)
                    sp.wait_ge(lo_ready, u - STAGE + 1 + 16 * i)

            def load(u):
                stage_free(u)
                for shape, c0, c1, src in units[u]:
                    size = shape[0] * shape[1]
                    slot = stage[:, u % STAGE, 0:size].rearrange("p (k c) -> p k c", k=shape[0])
                    if c0 is None:
                        dst = slot[:, c1, :].rearrange("p (h c) -> p h c", c=P)
                    else:
                        dst = slot[:, :, c0:c1]
                    sp.dma_start(dst, src).then_inc(stage_in[u % STAGE], 16)

            def load_mlp(layer):
                u0 = unit_no[("mlp", layer, 0, 0)]
                w1 = mlp_w1[layer].rearrange("(k p) n -> p k n", p=P)
                w2 = mlp_w2[layer].rearrange("(g k p) n -> p (g k) n", p=P, k=KD)
                with sp.Fori(0, GROUPS) as i:
                    for m in range(2 * KD):
                        u = u0 + m
                        stage_free(u, i)
                        dst = stage[:, u % STAGE, :].rearrange("p (k c) -> p k c", k=KD)
                        if m < KD:
                            src = w1[:, :, bass.ds(i * D + m * P, P)]
                        else:
                            src = w2[:, bass.ds(i * KD, KD), (m - KD) * P:(m - KD + 1) * P]
                        sp.dma_start(dst, src).then_inc(stage_in[u % STAGE], 16)

            for u in range(unit_no[("mlp", 0, 0, 0)]):
                load(u)
            load_mlp(0)
            sp.dma_start(pos_i, positions.partition_broadcast(P)).then_inc(pos_in, 16)
            for u in range(unit_no[("oi", 0)], unit_no[("mlp", 1, 0, 0)]):
                load(u)
            load_mlp(1)
            for m in range(2 * NT):
                t, half = divmod(m, 2)
                sp.wait_ge(out_ready, m + 1)
                sp.dma_start(out[0, t * P:(t + 1) * P, half * T:(half + 1) * T], y[:, m, :]).then_inc(out_stored, 16)
            sp.wait_ge(out_stored, 16 * 2 * NT)

        @block.gpsimd
        def _(pool):
            nc.gpsimd.memset(ones[:, :], 1.0).then_inc(consts_ready, 1)
            nc.gpsimd.memset(eps[:, :], EPS).then_inc(consts_ready, 1)
            ch = Chain(pool, pool_chain)
            ch.link(nc.gpsimd.memset(ident[:, :], 0.0))
            nc.gpsimd.affine_select(out=ident[:, :], in_=ident[:, :], compare_op=ALU.not_equal, fill=1.0, base=0,
                                    pattern=[[-1, P]], channel_multiplier=1).then_inc(consts_ready, 1)
            ch.link(nc.gpsimd.memset(masks[:, :, :], 0.0))
            for lv in range(LEVELS):
                L = 64 >> lv
                right = masks[:, lv, :].rearrange("p (b h j) -> p b h j", h=2, j=L)[:, :, 1, :]
                ch.link(nc.gpsimd.memset(right, 1.0))
                ch.link(nc.gpsimd.affine_select(out=right, in_=right, compare_op=ALU.is_ge, fill=0.0, base=0,
                                                pattern=[[-2 * L, P // (2 * L)], [0, L]], channel_multiplier=1))
                ch.link(nc.gpsimd.affine_select(out=right, in_=right, compare_op=ALU.is_ge, fill=0.0, base=L - 1,
                                                pattern=[[2 * L, P // (2 * L)], [0, L]], channel_multiplier=-1))
            nc.gpsimd.affine_select(out=masks[:, LEVELS, :], in_=masks[:, LEVELS, :], compare_op=ALU.not_equal,
                                    fill=1.0, base=0, pattern=[[-1, P]], channel_multiplier=1).then_inc(consts_ready, 1)

            for p in range(len(PACKS)):
                pool.wait_ge(b_ready, p + 1)
                for lv in range(LEVELS + 1):
                    item = p * (LEVELS + 2) + lv
                    if item >= 3:
                        pool.wait_ge(xl_ready, item - 2)
                    L = 64 >> lv
                    if lv < LEVELS:
                        ref = halves(b_sb[:, :], L)[:, :, 0, L - 1:L]
                    else:
                        L = P // 2
                        ref = halves(b_sb[:, :], L)[:, :, 1, L - 1:L]
                    shape = [P, T // (2 * L), 2 * L]
                    nc.gpsimd.tensor_tensor(dec[:, item % 3, :].rearrange("p (b j) -> p b j", j=2 * L),
                                            b_sb[:, :].rearrange("p (b j) -> p b j", j=2 * L),
                                            ref.to_broadcast(shape), ALU.subtract).then_inc(d_ready, 1)
            pool.wait_ge(y_zero[0], 1)
            ch.link(nc.gpsimd.memset(mask_q[:, :], 0.0))
            ch.link(nc.gpsimd.memset(mask_k[:, :], 0.0))
            nc.gpsimd.memset(mask_q[0:1, 0:P // 2], MASKED).then_inc(consts_ready, 1)
            nc.gpsimd.memset(mask_k[0:1, P // 2:P], 1.0).then_inc(consts_ready, 1)

        @block.scalar
        def _(act):
            ch = Chain(act, act_chain)
            small = [(0, norm_gains.rearrange("l n (k p) -> (l n k) p", p=P)),
                     (V_LB, hg_lb_table.rearrange("r (h p) -> (r h) p", p=P)),
                     (V_BG, gla_b_gate.rearrange("e (k p) -> (e k) p", p=P)),
                     (V_HGN, hg_out_norm), (V_GLN, gla_out_norm),
                     (V_QN, mla_q_norm.rearrange("e (k p) -> (e k) p", p=P)),
                     (V_KVN, mla_kv_norm.rearrange("e (k p) -> (e k) p", p=P))]
            for r, src in small:
                act.dma_start(vrows[r:r + src.shape[0], :], src).then_inc(vec_in, 16)
            act.dma_start(w_gate[:, :], gla_w_gate[0]).then_inc(vec_in, 16)
            act.dma_start(ropec[:, :], rope_const).then_inc(vec_in, 16)

            def inv_rms(src, width, slot, ready):
                ch.link(nc.scalar.activation(rinv[:, slot, :], src, ACT.Ln, bias=eps[:, 0:1], scale=1.0 / width))
                nc.scalar.activation(rinv[:, slot, :], rinv[:, slot, :], ACT.Exp, scale=-0.5).then_inc(ready, 1)

            def pre_norm(j, xs, hs):
                for k in range(KD):
                    act.wait_ge(x_ready, xs + k + 1)
                    if k >= 2:
                        act.wait_ge(sq_used[j], k - 1)
                    nc.scalar.activation(sq[:, k % 2, :], xT[:, k, :], ACT.Square).then_inc(sq_ready[j], 1)
                act.wait_ge(sq_used[j], KD)
                inv_rms(misc[:, :], D, 0, r_ready[j])
                for k in range(KD):
                    act.wait_ge(h_f32, hs + k + 1)
                    nc.scalar.copy(h_hi[:, k, :], tmp[:, k % 2, :]).then_inc(h_high, 1)

            def y_square(j, ys, m):
                act.wait_ge(y_ready[j], ys + m + 1)
                if m >= 2:
                    act.wait_ge(sq_used[j], m - 1)
                nc.scalar.activation(sq[:, m % 2, :], y[:, m, :], ACT.Square).then_inc(sq_ready[j], 1)

            def post_norm(j):
                act.wait_ge(sq_used[j], KD)
                inv_rms(misc[:, :], D, 1, r_ready[j])

            def pump(u, i=0):
                split_high(act, u + AHEAD_HI, i)

            act.wait_ge(consts_ready, 4)
            act.wait_ge(vec_ready, 2)
            nc.scalar.activation(lbt[:, 1:3, :], lbt[:, 1:3, :], ACT.Exp).then_inc(vec_ready, 1)
            for u in range(AHEAD_HI):
                split_high(act, u)
            pre_norm(0, 0, 0)

            n = tile_no[("ga", 0)]
            wait_tile(act, n)
            nc.scalar.copy(ga_t[:, :], bank[n % 2][0:GATE_RANK, :]).then_inc(ga_ready, 1)
            pump(unit_no[("ga", 0)])

            def decay(p, items):
                s = 1.0 if PACKS[p][0] == "hg" else 1.0 / GATE_TEMP
                for lv in items:
                    item = p * (LEVELS + 2) + lv
                    d = dec[:, item % 3, :]
                    if lv <= LEVELS:
                        act.wait_ge(d_ready, p * (LEVELS + 1) + lv + 1)
                    if lv < LEVELS:
                        v = halves(d, 64 >> lv)
                        nc.scalar.activation(v[:, :, 0, :], v[:, :, 0, :], ACT.Exp, scale=-s).then_inc(e_ready, 1)
                        nc.scalar.activation(v[:, :, 1, :], v[:, :, 1, :], ACT.Exp, scale=s).then_inc(e_ready, 1)
                    elif lv == LEVELS:
                        nc.scalar.activation(d, d, ACT.Exp, scale=-s).then_inc(e_ready, 1)
                        last = b_sb[:, :].rearrange("p (c j) -> p c j", j=P)[:, :, P - 1]
                        nc.scalar.activation(e_last[:, :], last, ACT.Exp, scale=s).then_inc(e_ready, 1)
                    else:
                        act.wait_ge(xl_ready, item - 2)
                        nc.scalar.activation(d, b_sb[:, :], ACT.Exp, scale=s).then_inc(e_ready, 1)

            def evacuate(p, what, a):
                n = tile_no[(p, what, a)]
                ps = bank[n % 2][:, :]
                wait_tile(act, n)
                if what == "f":
                    if p >= 1:
                        act.wait_ge(b_ready, p)
                    nc.scalar.activation(t_f[:, :], ps, ACT.Sigmoid).then_inc(f_sig, 1)
                elif what == "g":
                    if a >= 1:
                        act.wait_ge(gate_ready, a)
                    if p > 4:
                        act.wait_ge(f_gate, p)
                    nc.scalar.activation(t_g[:, :], ps, ACT.Sigmoid).then_inc(g_sig, 1)
                elif what == "q":
                    scale = 1.0 if PACKS[p][0] == "hg" else GLA_DK ** -0.5
                    nc.scalar.activation(q_sb[:, p % 2, :], ps, ACT.Copy, scale=scale).then_inc(q_ready, 1)
                elif what == "k":
                    nc.scalar.activation(k_sb[:, p % 2, :], ps, ACT.Copy).then_inc(k_ready, 1)
                elif what == "v":
                    nc.scalar.activation(vbuf[:, a % 4, :], ps, ACT.Copy).then_inc(v_ready, 1)
                elif what == "z":
                    act.wait_ge(b_ready, p)
                    bg = vec[:, V_BG + a:V_BG + a + 1]
                    nc.scalar.activation(t_f[:, :], ps, ACT.Identity, bias=bg).then_inc(z_read, 1)
                    act.wait_ge(z_read, a + 1)
                    act.wait_ge(gate_ready, 4 + 2 * (a + 1))
                    ch.link(nc.scalar.activation(t_g[:, :], t_f[:, :], ACT.Abs))
                    ch.link(nc.scalar.activation(t_g[:, :], t_g[:, :], ACT.Exp, scale=-1.0))
                    nc.scalar.activation(t_g[:, :], t_g[:, :], ACT.Ln, bias=1.0).then_inc(f_log, 1)

            def attend_act(p):
                kind, a = PACKS[p]
                act.wait_ge(ket_done, p + 1)
                nc.scalar.activation(ke_t[:, :, :].rearrange("p c d -> p (c d)"), misc[:, 0:(NT - 1) * P],
                                     ACT.Copy).then_inc(ket_ready, 1)
                for head in ([a] if kind == "hg" else [4 + 2 * a, 5 + 2 * a]):
                    act.wait_ge(o_done, head + 1)
                    nc.scalar.activation(sq[:, 0, :], po[:, :], ACT.Square).then_inc(o_sq, 1)
                    act.wait_ge(o_sum, head + 1)
                    if head >= 1:
                        act.wait_ge(o_read, head)
                    inv_rms(misc[:, :], P, 0, o_rinv)
                    act.wait_ge(mix_f32, head + 1)
                    nc.scalar.copy(a_hi[:, head, :], tmp[:, 1, :]).then_inc(mix_high, 1)

            for p in range(len(PACKS) + 1):
                if p >= 1:
                    decay(p - 1, range(0, 3))
                if p < len(PACKS):
                    tiles = pack_tiles(p)
                    for j, (what, a, col) in enumerate(tiles):
                        evacuate(p, what, a)
                        if what == "q" and PACKS[p][0] == "hg":
                            act.wait_ge(f_gate, p + 1)
                            nc.scalar.activation(t_f[:, :], t_f[:, :], ACT.Ln).then_inc(f_log, 1)
                        if col is not None:
                            pump(unit_no[(p, what, a)])
                        if what == "q" and p >= 1:
                            decay(p - 1, range(3, LEVELS))
                    if p >= 1:
                        decay(p - 1, (LEVELS, LEVELS + 1))
                else:
                    decay(p - 1, range(3, LEVELS + 2))
                if p >= 1:
                    attend_act(p - 1)

            def linear_out(name, j):
                for m in range(KD):
                    if m >= 1:
                        y_square(j, 0, m - 1)
                    wait_tile(act, tile_no[(name, m)])
                    pump(unit_no[(name, m)])
                y_square(j, 0, KD - 1)
                post_norm(j)

            linear_out("eo", 1)
            pre_norm(2, KD, KD)

            def mlp(layer, j):
                n0, u0 = tile_no[("mlp", layer, 0, 0)], unit_no[("mlp", layer, 0, 0)]

                def group(i, last):
                    for m in range(2 * KD):
                        n = n0 + m
                        wait_tile(act, n, i)
                        if m < KD:
                            if m >= 2:
                                act.wait_ge(hid_f32[layer], m - 1 + KD * i)
                            nc.scalar.activation(sq[:, m % 2, :], bank[n % 2][:, :], ACT.Relu).then_inc(relu_ready[layer], 1)
                        if not last or m < 2 * KD - AHEAD_HI or layer == 0:
                            pump(u0 + m, i)
                        if m < KD:
                            act.wait_ge(hid_f32[layer], m + 1 + KD * i)
                            nc.scalar.copy(a_hi[:, m, :], tmp[:, m % 2, :]).then_inc(hid_high[layer], 1)
                        elif last and m > KD:
                            y_square(j, (GROUPS - 1) * KD, m - KD - 1)

                with act.Fori(0, GROUPS - 1) as i:
                    group(i, False)
                group(GROUPS - 1, True)
                y_square(j, (GROUPS - 1) * KD, KD - 1)
                post_norm(j)

            mlp(0, 3)

            pre_norm(4, 2 * KD, 2 * KD)
            for m in range(5):
                n = tile_no[("oi", m)]
                wait_tile(act, n)
                nc.scalar.activation(y[:, m, :], bank[n % 2][:, :], ACT.Copy).then_inc(c_ready, 1)
                act.wait_ge(c_ready, m + 1)
                if m >= 2:
                    act.wait_ge(sq_used[8], m - 1)
                nc.scalar.activation(sq[:, m % 2, :], y[:, m, :], ACT.Square).then_inc(sq_ready[8], 1)
                pump(unit_no[("oi", m)])
            for m in (5, 6):
                wait_tile(act, tile_no[("oi", m)])
                pump(unit_no[("oi", m)])
            act.wait_ge(sq_used[8], 5)
            inv_rms(po[:, :], KV_RANK_T * P, 1, r_ready[8])
            inv_rms(misc[:, :], Q_RANK_T * P, 0, r_ready[8])
            for j, k in enumerate((3, 4, 0, 1, 2)):
                act.wait_ge(h_f32, 3 * KD + j + 1)
                nc.scalar.copy(h_hi[:, k, :], tmp[:, j % 2, :]).then_inc(h_high, 1)
            act.wait_ge(sin_arg, 1)
            nc.scalar.activation(sind[:, :], sind[:, :], ACT.Sin).then_inc(sin_ready, 1)
            nc.scalar.activation(cosd[:, :], cosd[:, :], ACT.Sin).then_inc(sin_ready, 1)
            for what in ("mv", "mk"):
                for g in range(2):
                    for j in range(4):
                        n = tile_no[(what, g, j)]
                        wait_tile(act, n)
                        dst = v_tok[:, j, g * T:(g + 1) * T] if what == "mv" else y[:, 4 * g + j, :]
                        nc.scalar.activation(dst, bank[n % 2][:, :], ACT.Copy).then_inc(
                            vt_ready if what == "mv" else kt_ready, 1)
                    pump(unit_no[(what, g)])

            def q_evacuate(a):
                if a == 1:
                    act.wait_ge(rope_ready, 1)
                for hh in range(2):
                    n = tile_no[("qn", a, hh)]
                    wait_tile(act, n)
                    nc.scalar.activation(qn[:, a % 2, hh, :], bank[n % 2][:, :], ACT.Copy,
                                         scale=SCALE).then_inc(qn_ready, 1)
                pump(unit_no[("qn", a)])
                wait_tile(act, tile_no[("qr", a, 1)])
                pump(unit_no[("qr", a)])

            def att_out(h):
                act.wait_ge(pv_done, h + 1)
                nc.scalar.copy(a_hi[:, h, :], po[:, :]).then_inc(att_high, 1)

            q_evacuate(0)
            for j in range(4 * MLA_HEADS + 2):
                if j % 8 == 0 and j // 8 + 1 < MLA_HEADS // 2:
                    q_evacuate(j // 8 + 1)
                if j < 4 * MLA_HEADS:
                    width = (j % 4 + 1) * P
                    act.wait_ge(nmax_ready, j + 1)
                    nc.scalar.activation(prob[:, j % 3, 0:width], s_bank[j % 3][:, 0:width], ACT.Exp,
                                         bias=stat[:, 0, j:j + 1], accum_out=stat[:, 1, j:j + 1]).then_inc(prob_exp, 1)
                if j >= 6 and j % 4 == 2:
                    att_out(j // 4 - 1)
            att_out(MLA_HEADS - 1)
            linear_out("oo", 5)
            pre_norm(6, 3 * KD, 3 * KD + 5)
            mlp(1, 7)

        @block.vector
        def _(dve):
            ch = Chain(dve, dve_chain)

            def pump(u, i=0):
                split_low(dve, u + AHEAD_LO, i)

            def pre_norm(j, layer, which, hs):
                dve.wait_ge(r_ready[j], 1)
                for k in range(KD + 1):
                    if 2 <= k < KD:
                        dve.wait_ge(h_ready, hs + k - 1)
                    if k < KD:
                        nc.vector.scalar_tensor_tensor(out=tmp[:, k % 2, :], in0=xT[:, k, :], scalar=gain(layer, which, k),
                                                       in1=rinv[:, 0, :], op0=ALU.mult, op1=ALU.mult).then_inc(h_f32, 1)
                    if k >= 1:
                        dve.wait_ge(h_high, hs + k)
                        nc.vector.tensor_tensor(h_lo[:, k - 1, :], tmp[:, (k - 1) % 2, :],
                                                h_hi[:, k - 1, :].bitcast(F32), ALU.subtract).then_inc(h_ready, 1)
                dve.wait_ge(h_ready, hs + KD)

            def post_norm(j, layer, which):
                dve.wait_ge(r_ready[j], 1)
                for k in range(KD):
                    ch.link(nc.vector.scalar_tensor_tensor(out=y[:, k, :], in0=y[:, k, :], scalar=gain(layer, which, k),
                                                           in1=rinv[:, 1, :], op0=ALU.mult, op1=ALU.mult))
                    nc.vector.tensor_tensor(xT[:, k, :], xT[:, k, :], y[:, k, :], ALU.add).then_inc(x_ready, 1)

            dve.wait_ge(vec_done, 1)
            nc.vector.tensor_copy(vec[:, :], misc[:, 0:V_ROWS]).then_inc(vec_ready, 1)
            dve.wait_ge(vec_ready, 1)
            t0, t1 = vec[:, V_LB:V_LB + HEADS], vec[:, V_LB + HEADS:V_LB + 2 * HEADS]
            ch.link(nc.vector.tensor_tensor(lbt[:, 0, :], t0, t1, ALU.max))
            ch.link(nc.vector.tensor_tensor(lbt[:, 1, :], t0, lbt[:, 0, :], ALU.subtract))
            nc.vector.tensor_tensor(lbt[:, 2, :], t1, lbt[:, 0, :], ALU.subtract).then_inc(vec_ready, 1)
            dve.wait_ge(vec_ready, 3)
            ch.link(nc.vector.tensor_tensor(lbt[:, 0, :], lbt[:, 1, :], lbt[:, 2, :], ALU.add))
            ch.link(nc.vector.reciprocal(lbt[:, 3, :], lbt[:, 0, :]))
            ch.link(nc.vector.tensor_tensor(lbt[:, 4, :], lbt[:, 1, :], lbt[:, 3, :], ALU.mult))
            ch.link(nc.vector.tensor_scalar(lbt[:, 5, :], lbt[:, 4, :], -1.0, 1.0, ALU.mult, ALU.add))

            for k in range(KD):
                n = tile_no[("x", k)]
                wait_tile(dve, n)
                nc.vector.tensor_copy(xT[:, k, :], bank[n % 2][:, :]).then_inc(x_ready, 1)
            for u in range(AHEAD_LO):
                split_low(dve, u)
            pre_norm(0, 0, 0, 0)
            wait_tile(dve, tile_no[("ga", 0)])
            pump(unit_no[("ga", 0)])

            def decayed(p, items):
                q, k = q_sb[:, p % 2, :], k_sb[:, p % 2, :]
                for lv in items:
                    item = p * (LEVELS + 2) + lv
                    e = dec[:, item % 3, :]
                    done = p * (2 * LEVELS + 3) + 2 * lv
                    dve.wait_ge(e_ready, done + 2 if lv <= LEVELS else done + 1)
                    if lv < LEVELS:
                        L = 64 >> lv
                        nc.vector.tensor_tensor(halves(xl[:, lv, :], L)[:, :, 0, :], halves(k, L)[:, :, 0, :],
                                                halves(e, L)[:, :, 0, :], ALU.mult)
                        nc.vector.tensor_tensor(halves(xl[:, lv, :], L)[:, :, 1, :], halves(q, L)[:, :, 1, :],
                                                halves(e, L)[:, :, 1, :], ALU.mult).then_inc(xl_ready, 1)
                    elif lv == LEVELS:
                        nc.vector.tensor_tensor(ke[:, :], k, e, ALU.mult).then_inc(xl_ready, 1)
                    else:
                        nc.vector.tensor_tensor(qe[:, :], q, e, ALU.mult).then_inc(xl_ready, 1)

            def evacuate(p, what, a):
                n = tile_no[(p, what, a)]
                if what == "f":
                    dve.wait_ge(f_sig, p + 1)
                    ch.link(nc.vector.tensor_scalar(t_f[:, :], t_f[:, :], lbt[:, 5, a:a + 1], lbt[:, 4, a:a + 1],
                                                    ALU.mult, ALU.add))
                    nc.vector.tensor_scalar(k_sb[:, p % 2, :], t_f[:, :], -1.0, 1.0, ALU.mult,
                                            ALU.add).then_inc(f_gate, 1)
                elif what == "g":
                    dve.wait_ge(g_sig, a + 1)
                    nc.vector.tensor_tensor(y[:, a, :], bank[n % 2][:, :], t_g[:, :], ALU.mult).then_inc(gate_ready, 1)
                elif what == "z":
                    dve.wait_ge(f_log, p + 1)
                    nc.vector.scalar_tensor_tensor(out=t_f[:, :], in0=t_f[:, :], scalar=0.0, in1=t_g[:, :],
                                                   op0=ALU.min, op1=ALU.subtract).then_inc(f_gate, 1)
                else:
                    wait_tile(dve, n)

            def cumulate(p):
                dve.wait_ge(f_log, p + 1)
                dve.wait_ge(f_gate, p + 1)
                for c in range(NT):
                    s = slice(c * P, (c + 1) * P)
                    ins = nc.vector.tensor_tensor_scan(b_sb[:, s], ones[:, :], t_f[:, s], 0.0, ALU.mult, ALU.add)
                ins.then_inc(b_ready, 1)

            def attend_dve(p):
                kind, a = PACKS[p]
                heads = [a] if kind == "hg" else [4 + 2 * a, 5 + 2 * a]
                pm = tmp[:, :, :].rearrange("p a t -> p (a t)")
                for head in heads:
                    for c in range(NT):
                        idx = head * NT + c
                        dve.wait_ge(p_done, idx + 1)
                        if idx >= 1:
                            dve.wait_ge(a_ready, idx)
                        if c == 0 and head >= 1:
                            dve.wait_ge(mix_ready, head)
                        nc.vector.tensor_tensor(pm, pp[idx % 2][:, :, :].rearrange("p l t -> p (l t)"),
                                                masks[:, :, :].rearrange("p l t -> p (l t)"),
                                                ALU.mult).then_inc(p_read, 1)
                        dve.wait_ge(p_read, idx + 1)
                        nc.vector.tensor_reduce(a_sb[:, idx % 4, :], pm.rearrange("p (l t) -> p t l", l=LEVELS + 1),
                                                AX_X, ALU.add).then_inc(a_ready, 1)
                        if c == 1 and head == heads[0]:
                            dve.wait_ge(kv_done, p + 1)
                            kv = misc[:, 0:(NT - 1) * P].rearrange("p (c d) -> p c d", c=NT - 1)
                            ch.link(nc.vector.tensor_copy(state[:, 0, :], kv[:, 0, :]))
                            for cc in range(1, NT - 1):
                                ins = nc.vector.scalar_tensor_tensor(
                                    out=state[:, cc, :], in0=state[:, cc - 1, :], scalar=e_last[:, cc:cc + 1],
                                    in1=kv[:, cc, :], op0=ALU.mult, op1=ALU.add)
                                if cc < NT - 2:
                                    ch.link(ins)
                            ins.then_inc(state_ready, 1)
                    dve.wait_ge(a_ready, (head + 1) * NT)
                    dve.wait_ge(o_rinv, head + 1)
                    g = V_HGN if kind == "hg" else V_GLN
                    nc.vector.scalar_tensor_tensor(out=tmp[:, 0, :], in0=po[:, :], scalar=vec[:, g:g + 1],
                                                   in1=rinv[:, 0, :], op0=ALU.mult, op1=ALU.mult).then_inc(o_read, 1)
                    dve.wait_ge(o_read, head + 1)
                    nc.vector.tensor_tensor(tmp[:, 1, :], tmp[:, 0, :], y[:, head, :], ALU.mult).then_inc(mix_f32, 1)
                    dve.wait_ge(mix_high, head + 1)
                    nc.vector.tensor_tensor(a_lo[:, head, :], tmp[:, 1, :], a_hi[:, head, :].bitcast(F32),
                                            ALU.subtract).then_inc(mix_ready, 1)

            for p in range(len(PACKS) + 1):
                if p >= 1:
                    decayed(p - 1, range(0, 3))
                if p < len(PACKS):
                    for what, a, col in pack_tiles(p):
                        evacuate(p, what, a)
                        if col is not None:
                            pump(unit_no[(p, what, a)])
                        if what == "q" and p >= 1:
                            decayed(p - 1, range(3, LEVELS))
                    if p >= 1:
                        decayed(p - 1, (LEVELS, LEVELS + 1))
                    cumulate(p)
                else:
                    decayed(p - 1, range(3, LEVELS + 2))
                if p >= 1:
                    attend_dve(p - 1)

            def linear_out(name, j):
                for m in range(KD):
                    n = tile_no[(name, m)]
                    wait_tile(dve, n)
                    nc.vector.tensor_copy(y[:, m, :], bank[n % 2][:, :]).then_inc(y_ready[j], 1)
                    pump(unit_no[(name, m)])

            def mlp(layer, j):
                n0, u0 = tile_no[("mlp", layer, 0, 0)], unit_no[("mlp", layer, 0, 0)]
                nc.vector.memset(y[:, :, :], 0.0).then_inc(y_zero[layer], 1)
                dve.wait_ge(y_zero[layer], 1)

                def group(i, last):
                    for m in range(2 * KD):
                        n = n0 + m
                        if m < KD:
                            dve.wait_ge(relu_ready[layer], m + 1 + KD * i)
                            if m >= 2:
                                dve.wait_ge(hid_ready[layer], m - 1 + KD * i)
                            nc.vector.tensor_tensor(tmp[:, m % 2, :], sq[:, m % 2, :], bank[n % 2][:, :],
                                                    ALU.mult).then_inc(hid_f32[layer], 1)
                        else:
                            wait_tile(dve, n, i)
                            nc.vector.tensor_tensor(y[:, m - KD, :], y[:, m - KD, :], bank[n % 2][:, :],
                                                    ALU.add).then_inc(y_ready[j], 1)
                        if not last or m < 2 * KD - AHEAD_LO or layer == 0:
                            pump(u0 + m, i)
                        if m < KD:
                            dve.wait_ge(hid_high[layer], m + 1 + KD * i)
                            nc.vector.tensor_tensor(a_lo[:, m, :], tmp[:, m % 2, :], a_hi[:, m, :].bitcast(F32),
                                                    ALU.subtract).then_inc(hid_ready[layer], 1)

                with dve.Fori(0, GROUPS - 1) as i:
                    group(i, False)
                group(GROUPS - 1, True)

            linear_out("eo", 1)
            post_norm(1, 0, 1)
            pre_norm(2, 0, 2, KD)
            mlp(0, 3)
            post_norm(3, 0, 3)
            pre_norm(4, 1, 0, 2 * KD)

            dve.wait_ge(pos_in, 16)
            ch.link(nc.vector.tensor_copy(ang[:, :], pos_i))
            ch.link(nc.vector.tensor_scalar(ang[:, :], ang[:, :], ropec[:, 0:1], None, ALU.mult))
            for dst, turn in ((sind, 0.0), (cosd, 0.25)):
                n_, r_ = tmp[:, 0, :], dst[:, :]
                ch.link(nc.vector.tensor_scalar(n_, ang[:, :], 0.15915494309189535, turn, ALU.mult, ALU.add))
                ch.link(nc.vector.tensor_scalar(n_, n_, MAGIC, None, ALU.add))
                ch.link(nc.vector.tensor_scalar(n_, n_, MAGIC, None, ALU.subtract))
                ch.link(nc.vector.scalar_tensor_tensor(out=r_, in0=n_, scalar=-TWO_PI_A, in1=ang[:, :],
                                                       op0=ALU.mult, op1=ALU.add))
                ch.link(nc.vector.scalar_tensor_tensor(out=r_, in0=n_, scalar=-TWO_PI_B, in1=r_,
                                                       op0=ALU.mult, op1=ALU.add))
                ch.link(nc.vector.scalar_tensor_tensor(out=r_, in0=n_, scalar=-TWO_PI_C, in1=r_,
                                                       op0=ALU.mult, op1=ALU.add))
                ch.link(nc.vector.tensor_scalar(r_, r_, turn * 6.283185307179586, None, ALU.add))
                ins = nc.vector.tensor_scalar(r_, r_, PI_IN, -PI_IN, ALU.min, ALU.max)
                if turn == 0.0:
                    ch.link(ins)
            ins.then_inc(sin_arg, 1)

            for m in range(5):
                wait_tile(dve, tile_no[("oi", m)])
                pump(unit_no[("oi", m)])
            def latents():
                order = ((3, V_KVN, 1), (4, V_KVN + 1, 1), (0, V_QN, 0), (1, V_QN + 1, 0), (2, V_QN + 2, 0))
                for j in range(6):
                    if 2 <= j < 5:
                        dve.wait_ge(h_ready, 3 * KD + j - 1)
                    if j < 5:
                        k, g, slot = order[j]
                        dve.wait_ge(r_ready[8], 1 if slot == 1 else 2)
                        nc.vector.scalar_tensor_tensor(out=tmp[:, j % 2, :], in0=y[:, k, :], scalar=vec[:, g:g + 1],
                                                       in1=rinv[:, slot, :], op0=ALU.mult, op1=ALU.mult).then_inc(h_f32, 1)
                    if j >= 1:
                        k = order[j - 1][0]
                        dve.wait_ge(h_high, 3 * KD + j)
                        nc.vector.tensor_tensor(h_lo[:, k, :], tmp[:, (j - 1) % 2, :], h_hi[:, k, :].bitcast(F32),
                                                ALU.subtract).then_inc(h_ready, 1)

            def rotate(n_plain, n_swapped, scale, dst, ready, done):
                wait_tile(dve, n_plain)
                nc.vector.scalar_tensor_tensor(out=dst, in0=bank[n_plain % 2][:, :], scalar=scale, in1=cosd[:, :],
                                               op0=ALU.mult, op1=ALU.mult).then_inc(rot_read, 1)
                wait_tile(dve, n_swapped)
                if done:
                    dve.wait_ge(ready, done)
                nc.vector.scalar_tensor_tensor(out=ang[:, :], in0=bank[n_swapped % 2][:, :], scalar=scale, in1=sind[:, :],
                                               op0=ALU.mult, op1=ALU.mult).then_inc(rot_read, 1)
                wait_read(dve, n_swapped)
                nc.vector.tensor_tensor(dst, dst, ang[:, :], ALU.add).then_inc(ready, 1)

            for m in (5, 6):
                n = tile_no[("oi", m)]
                wait_tile(dve, n)
                nc.vector.tensor_copy(qn[:, 1, m - 5, :], bank[n % 2][:, :]).then_inc(kr_read, 1)
                pump(unit_no[("oi", m)])
            latents()
            dve.wait_ge(sin_ready, 2)
            ch.link(nc.vector.tensor_scalar(sind[:, :], sind[:, :], ropec[:, 1:2], None, ALU.mult))
            ch.link(nc.vector.tensor_tensor(kr[:, :], qn[:, 1, 0, :], cosd[:, :], ALU.mult))
            ch.link(nc.vector.tensor_tensor(ang[:, :], qn[:, 1, 1, :], sind[:, :], ALU.mult))
            nc.vector.tensor_tensor(kr[:, :], kr[:, :], ang[:, :], ALU.add).then_inc(rope_ready, 1)
            for what in ("mv", "mk"):
                for g in range(2):
                    wait_tile(dve, tile_no[(what, g, 3)])
                    pump(unit_no[(what, g)])

            def q_evacuate(a):
                wait_tile(dve, tile_no[("qn", a, 1)])
                pump(unit_no[("qn", a)])
                rotate(tile_no[("qr", a, 0)], tile_no[("qr", a, 1)], SCALE, qr[:, a % 2, :], qr_ready, a)
                pump(unit_no[("qr", a)])

            def att_out(h):
                dve.wait_ge(att_high, h + 1)
                nc.vector.tensor_tensor(a_lo[:, h, :], po[:, :], a_hi[:, h, :].bitcast(F32),
                                        ALU.subtract).then_inc(att_ready, 1)

            dve.wait_ge(rope_ready, 1)
            q_evacuate(0)
            for j in range(4 * MLA_HEADS + 2):
                if j % 8 == 0 and j // 8 + 1 < MLA_HEADS // 2:
                    q_evacuate(j // 8 + 1)
                if j < 4 * MLA_HEADS:
                    width = (j % 4 + 1) * P
                    dve.wait_ge(s_done, j + 1)
                    nc.vector.tensor_reduce(stat[:, 0, j:j + 1], s_bank[j % 3][:, 0:width], AX_X, ALU.max,
                                            negate=True).then_inc(nmax_ready, 1)
                if 1 <= j <= 4 * MLA_HEADS:
                    i = j - 1
                    width = (i % 4 + 1) * P
                    dve.wait_ge(prob_exp, i + 1)
                    ch.link(nc.vector.reciprocal(stat[:, 2, i:i + 1], stat[:, 1, i:i + 1]))
                    nc.vector.tensor_scalar(prob[:, i % 3, 0:width], prob[:, i % 3, 0:width], stat[:, 2, i:i + 1], None,
                                            ALU.mult).then_inc(prob_ready, 1)
                if j >= 2:
                    i = j - 2
                    qb = i % 4
                    dve.wait_ge(pt_done, i + 1)
                    nc.vector.tensor_copy(p_t[:, 0:qb + 1, qb * P:(qb + 1) * P],
                                          t_bank[i % 2][:, 0:qb + 1, :]).then_inc(pt_ready, 1)
                if j >= 6 and j % 4 == 2:
                    att_out(j // 4 - 1)
            att_out(MLA_HEADS - 1)
            linear_out("oo", 5)
            post_norm(5, 1, 1)
            pre_norm(6, 1, 2, 3 * KD + 5)
            mlp(1, 7)
            post_norm(7, 1, 3)
            for m in range(2 * NT):
                n = tile_no[("out", m)]
                wait_tile(dve, n)
                nc.vector.tensor_copy(y[:, m, :], bank[n % 2][:, :]).then_inc(out_ready, 1)

        @block.tensor
        def _(pe):
            def mm3(dst, wh, wl, xh, xl_, first, last):
                nc.tensor.matmul(dst, wh, xl_, start=first, stop=False)
                nc.tensor.matmul(dst, wl, xh, start=False, stop=False)
                return nc.tensor.matmul(dst, wh, xh, start=False, stop=last)

            def slot(u, cols):
                n = unit_size(u)
                return (w_hi[:, u % SPLIT, 0:n].rearrange("p (k c) -> p k c", c=cols),
                        w_lo[:, u % SPLIT, 0:n].rearrange("p (k c) -> p k c", c=cols))

            def feature_tile(u, n, src_hi, src_lo, ready=None, base=0, i=None, kt=KD, k0=0, cols=P, c0=0, width=P):
                wh, wl = slot(u, cols)
                pe.wait_ge(lo_ready, u + 1 + (0 if i is None else 16 * (i - 1)))
                wait_bank(pe, n, i)
                for k in range(kt):
                    if ready is not None:
                        pe.wait_ge(ready, base + k + 1)
                    c = slice(c0, c0 + width)
                    ins = mm3(bank[n % 2][0:width, :], wh[:, k, c], wl[:, k, c], src_hi[:, k0 + k, :],
                              src_lo[:, k0 + k, :], k == 0, k == kt - 1)
                ins.then_inc(tile_done, 1)

            def sum_squares(j, k, total=KD, dst=misc, first=None, last=None):
                pe.wait_ge(sq_ready[j], k + 1)
                nc.tensor.matmul(dst[:, :], ones[:, :], sq[:, k % 2, :], start=(k == 0 if first is None else first),
                                 stop=(k == total - 1 if last is None else last)).then_inc(sq_used[j], 1)

            def norm_sums(j):
                for k in range(KD):
                    sum_squares(j, k)

            pe.wait_ge(consts_ready, 4)
            pe.wait_ge(vec_in, 16 * 9)
            nc.tensor.transpose(misc[:, 0:V_ROWS], vrows[:, :], ident[0:V_ROWS, 0:V_ROWS]).then_inc(vec_done, 1)
            for k in range(KD):
                n = tile_no[("x", k)]
                pe.wait_ge(x_in[k // 2], 16)
                wait_bank(pe, n)
                for t in range(NT):
                    ins = nc.tensor.transpose(bank[n % 2][:, t * P:(t + 1) * P], x_tok[:, t, k * P:(k + 1) * P], ident[:, :])
                ins.then_inc(tile_done, 1)
            pe.wait_ge(vec_ready, 1)
            norm_sums(0)

            n, u = tile_no[("ga", 0)], unit_no[("ga", 0)]
            feature_tile(u, n, h_hi, h_lo, h_ready, 0, cols=GATE_RANK, width=GATE_RANK)

            def project(p):
                for what, a, col in pack_tiles(p):
                    n = tile_no[(p, what, a)]
                    if what == "z":
                        pe.wait_ge(ga_ready, 1)
                        wait_bank(pe, n)
                        nc.tensor.matmul(bank[n % 2][:, :], w_gate[:, a * P:(a + 1) * P], ga_t[:, :], start=True,
                                         stop=True).then_inc(tile_done, 1)
                        continue
                    u = unit_no[(p, what, a)]
                    if what != "v":
                        feature_tile(u, n, h_hi, h_lo)
                        continue
                    wh, wl = slot(u, P)
                    pe.wait_ge(lo_ready, u + 1)
                    wait_bank(pe, n)
                    for t in range(NT):
                        s = slice(t * P, (t + 1) * P)
                        for k in range(KD):
                            ins = mm3(bank[n % 2][:, s], h_hi[:, k, s], h_lo[:, k, s], wh[:, k, :], wl[:, k, :],
                                      k == 0, k == KD - 1)
                    ins.then_inc(tile_done, 1)

            def attend(p):
                kind, a = PACKS[p]
                heads = [a] if kind == "hg" else [4 + 2 * a, 5 + 2 * a]
                q, k = q_sb[:, p % 2, :], k_sb[:, p % 2, :]
                n_kv = len(heads)
                width = P // n_kv
                vslot = [a] if kind == "hg" else [(2 * a) % 4, (2 * a + 1) % 4]
                for what, b, col in pack_tiles(p):
                    if what in ("q", "v", "k"):
                        wait_read(pe, tile_no[(p, what, b)])
                pe.wait_ge(xl_ready, (p + 1) * (LEVELS + 2))
                if heads[0] >= 1:
                    pe.wait_ge(o_rinv, heads[0])
                for c in range(NT - 1):
                    ins = nc.tensor.transpose(misc[:, c * P:(c + 1) * P], ke[:, c * P:(c + 1) * P], ident[:, :])
                ins.then_inc(ket_done, 1)

                def pairs(hh, c):
                    head = heads[hh]
                    idx = head * NT + c
                    r = slice(hh * width, (hh + 1) * width)
                    s = slice(c * P, (c + 1) * P)
                    if idx >= 2:
                        pe.wait_ge(p_read, idx - 1)
                    for lv in range(LEVELS):
                        nc.tensor.matmul(pp[idx % 2][:, lv, :], xl[r, lv, s], xl[r, lv, s], start=True, stop=True)
                    nc.tensor.matmul(pp[idx % 2][:, LEVELS, :], k[r, s], q[r, s], start=True, stop=True).then_inc(p_done, 1)

                def outputs(hh, c):
                    head = heads[hh]
                    idx = head * NT + c
                    r = slice(hh * width, (hh + 1) * width)
                    s = slice(c * P, (c + 1) * P)
                    if c == 0 and head >= 1:
                        pe.wait_ge(o_read, head)
                    pe.wait_ge(a_ready, idx + 1)
                    ins = nc.tensor.matmul(po[:, s], vbuf[:, vslot[hh], s], a_sb[:, idx % 4, :], start=True, stop=(c == 0))
                    if c >= 1:
                        pe.wait_ge(state_ready, p + 1)
                        ins = nc.tensor.matmul(po[:, s], state[r, c - 1, :], qe[r, s], start=False, stop=True)
                    if c == NT - 1:
                        ins.then_inc(o_done, 1)

                for hh, head in enumerate(heads):
                    pairs(hh, 0)
                    pairs(hh, 1)
                    if hh == 0:
                        pe.wait_ge(ket_ready, p + 1)
                        for c in range(NT - 1):
                            s = slice(c * P, (c + 1) * P)
                            for g in range(n_kv):
                                ins = nc.tensor.matmul(misc[g * width:(g + 1) * width, s],
                                                       ke_t[:, c, g * width:(g + 1) * width], vbuf[:, vslot[g], s],
                                                       start=True, stop=True)
                        ins.then_inc(kv_done, 1)
                    outputs(hh, 0)
                    pairs(hh, 2)
                    outputs(hh, 1)
                    pairs(hh, 3)
                    outputs(hh, 2)
                    outputs(hh, 3)
                    pe.wait_ge(o_sq, head + 1)
                    if hh == 1:
                        pe.wait_ge(o_rinv, head)
                    nc.tensor.matmul(misc[:, :], ones[:, :], sq[:, 0, :], start=True, stop=True).then_inc(o_sum, 1)

            for p in range(len(PACKS) + 1):
                if p < len(PACKS):
                    project(p)
                if p >= 1:
                    attend(p - 1)

            def linear_out(name, j, ready):
                for m in range(KD):
                    feature_tile(unit_no[(name, m)], tile_no[(name, m)], a_hi, a_lo, ready if m == 0 else None)
                    if m >= 1:
                        sum_squares(j, m - 1)
                sum_squares(j, KD - 1)

            def mlp(layer, j, hs):
                n0, u0 = tile_no[("mlp", layer, 0, 0)], unit_no[("mlp", layer, 0, 0)]

                def group(g, i=None, last=False):
                    n, u = n0 + 2 * KD * g, u0 + 2 * KD * g
                    for m in range(KD):
                        feature_tile(u + m, n + m, h_hi, h_lo, h_ready if g == 0 and m == 0 else None, hs, i)
                    for m in range(KD, 2 * KD):
                        ready = hid_ready[layer] if m == KD else None
                        feature_tile(u + m, n + m, a_hi, a_lo, ready, KD * (g if i is None else i), i)
                        if last and m > KD:
                            sum_squares(j, m - KD - 1)

                group(0)
                with pe.Fori(1, GROUPS - 1) as i:
                    group(1, i)
                group(GROUPS - 1, last=True)
                sum_squares(j, KD - 1)

            linear_out("eo", 1, mix_ready)
            pe.wait_ge(r_ready[1], 1)
            norm_sums(2)
            mlp(0, 3, KD)
            pe.wait_ge(r_ready[3], 1)
            norm_sums(4)

            for m in range(7):
                feature_tile(unit_no[("oi", m)], tile_no[("oi", m)], h_hi, h_lo, h_ready if m == 0 else None, 2 * KD)
                if m == 1:
                    pe.wait_ge(r_ready[4], 1)
                if 1 <= m <= 3:
                    sum_squares(8, m - 1, first=m == 1, last=m == 3)
                elif 4 <= m <= 5:
                    sum_squares(8, m - 1, dst=po, first=m == 4, last=m == 5)
            for g in range(2):
                u = unit_no[("mv", g)]
                wh, wl = slot(u, T)
                pe.wait_ge(lo_ready, u + 1)
                for t in range(NT):
                    n = tile_no[("mv", g, t)]
                    s = slice(t * P, (t + 1) * P)
                    wait_bank(pe, n)
                    for k in range(KV_RANK_T):
                        pe.wait_ge(h_ready, 3 * KD + k + 1)
                        ins = mm3(bank[n % 2][:, :], h_hi[:, 3 + k, s], h_lo[:, 3 + k, s], wh[:, k, :], wl[:, k, :],
                                  k == 0, k == KV_RANK_T - 1)
                    ins.then_inc(tile_done, 1)
            for g in range(2):
                for j in range(4):
                    feature_tile(unit_no[("mk", g)], tile_no[("mk", g, j)], h_hi, h_lo, kt=KV_RANK_T, k0=3, cols=T, c0=j * P)

            def project_q(a):
                for what in ("qn", "qr"):
                    for hh in range(2):
                        feature_tile(unit_no[(what, a)], tile_no[(what, a, hh)], h_hi, h_lo,
                                     h_ready if a == 0 else None, 3 * KD + 2, kt=Q_RANK_T, cols=2 * P, c0=hh * P)

            def scores(j):
                h, qb = divmod(j, 4)
                a, hh = divmod(h, 2)
                s = slice(qb * P, (qb + 1) * P)
                r = slice(hh * ROPE, (hh + 1) * ROPE)
                width = (qb + 1) * P
                dst = s_bank[j % 3]
                if j >= 3:
                    pe.wait_ge(prob_exp, j - 2)
                if qb == 0 and hh == 0:
                    pe.wait_ge(qr_ready, a + 1)
                    wait_read(pe, tile_no[("qn", a, 1)])
                nc.tensor.matmul(dst[:, 0:width], qr[r, a % 2, s], kr[r, 0:width], start=True, stop=False)
                nc.tensor.matmul(dst[:, 0:width], qn[:, a % 2, hh, s], y[:, h, 0:width], start=False, stop=False)
                nc.tensor.matmul(dst[:, width - P:width], mask_q[:, :], mask_k[:, :], start=False,
                                 stop=True).then_inc(s_done, 1)

            def transposes(j):
                pe.wait_ge(prob_ready, j + 1)
                if j >= 2:
                    pe.wait_ge(pt_ready, j - 1)
                for kb in range(j % 4 + 1):
                    ins = nc.tensor.transpose(t_bank[j % 2][:, kb, :], prob[:, j % 3, kb * P:(kb + 1) * P], ident[:, :])
                ins.then_inc(pt_done, 1)

            def values(h):
                pe.wait_ge(pt_ready, 4 * h + 4)
                if h >= 1:
                    pe.wait_ge(att_ready, h)
                for kb in range(NT):
                    ins = nc.tensor.matmul(po[:, kb * P:T], v_tok[:, kb, h * P:(h + 1) * P], p_t[:, kb, kb * P:T],
                                           start=(kb == 0), stop=(kb == NT - 1))
                ins.then_inc(pv_done, 1)

            project_q(0)
            pe.wait_ge(consts_ready, 6)
            pe.wait_ge(rope_ready, 1)
            pe.wait_ge(r_ready[8], 2)
            for j in range(4 * MLA_HEADS + 2):
                if j % 8 == 0 and j // 8 + 1 < MLA_HEADS // 2:
                    project_q(j // 8 + 1)
                if j < 4 * MLA_HEADS:
                    scores(j)
                if j >= 6 and j % 4 == 2:
                    values(j // 4 - 1)
                if 2 <= j:
                    transposes(j - 2)
            values(MLA_HEADS - 1)
            linear_out("oo", 5, att_ready)
            pe.wait_ge(r_ready[5], 1)
            norm_sums(6)
            mlp(1, 7, 3 * KD + 5)

            for m in range(2 * NT):
                t, half = divmod(m, 2)
                n = tile_no[("out", m)]
                pe.wait_ge(x_ready, 5 * KD)
                wait_bank(pe, n)
                for k in range(4):
                    ins = nc.tensor.transpose(bank[n % 2][:, k * P:(k + 1) * P],
                                              xT[:, 4 * half + k, t * P:(t + 1) * P], ident[:, :])
                ins.then_inc(tile_done, 1)


_INS = ["x", "positions", "norm_gains", "ev_w_in", "hg_lb_table", "gla_w_gate", "gla_b_gate", "hg_out_norm",
        "gla_out_norm", "ev_w_out", "od_w_in", "mla_q_norm", "mla_w_uq", "mla_kv_norm", "mla_w_ukv", "od_w_out",
        "mlp_w1", "mlp_w2"]


def kernel(**inputs):
    import numpy as np
    import concourse.bacc as _bacc
    from concourse.bass_utils import run_bass_kernel_spmd as _run

    inv_freq = np.float32(10000.0) ** (-np.arange(0, ROPE, 2, dtype=np.float32) / np.float32(ROPE))
    sign = np.repeat(np.array([-1.0, 1.0], np.float32), ROPE // 2)
    rope_const = np.stack([np.tile(inv_freq, 4), np.tile(sign, 2)], axis=1).astype(np.float32)

    nc = _bacc.Bacc("TRN2", target_bir_lowering=False, num_devices=1)
    arrays = {f"in_{n}": np.ascontiguousarray(inputs[n]) for n in _INS}
    arrays["rope_const"] = rope_const
    args = [nc.dram_tensor(n, a.shape, mybir.dt.from_np(a.dtype), kind="ExternalInput").ap() for n, a in arrays.items()]
    out = nc.dram_tensor("out_0", (1, T, D), F32, kind="ExternalOutput").ap()
    trunk(nc, *args, out)
    r = _run(nc, [arrays], core_ids=[0])
    return r.results[0]["out_0"]
```

```python
from contextlib import ExitStack

import concourse.bass as bass
from concourse import mybir

ALU = mybir.AluOpType
ACT = mybir.ActivationFunctionType
F32 = mybir.dt.float32
F32R = mybir.dt.float32r
I32 = mybir.dt.int32
AX_X = mybir.AxisListType.X

P = 128
T = 512
D = 1024
KD = D // P
NT = T // P
F = 4 * D
GROUPS = F // D
EPS = 1e-6
EXP_MAX = -87.0
HEADS = 4
GLA_DK = 64
GATE_RANK = 16
GATE_TEMP = 16.0
LEVELS = 7
PAIRS = 7
Q_RANK_T, KV_RANK_T = 3, 2
MLA_HEADS = 8
NOPE, ROPE, VDIM = 128, 64, 128
SCALE = float(NOPE + ROPE) ** -0.5
MASKED = -1e30

HQ, HF, HI, HG, GQ, GK, GV, GR, GA = 0, 512, 1024, 1536, 2048, 2304, 2560, 3072, 3584
V_LB, V_BG, V_HGN, V_GLN, V_QN, V_KVN, V_ROWS = 64, 72, 74, 75, 76, 79, 81

STAGE, SPLIT = 2, 4
UNIT = KD * P

TWO_PI_A, TWO_PI_B, TWO_PI_C = 6.28125, 0.0019350051879882812, 3.0199159819567e-07
MAGIC = 12582912.0
PI_IN = 3.1415925


def trunk(nc, x, positions, norm_gains, ev_w_in, hg_lb_table, gla_w_gate, gla_b_gate, hg_out_norm,
          gla_out_norm, ev_w_out, od_w_in, mla_q_norm, mla_w_uq, mla_kv_norm, mla_w_ukv, od_w_out,
          mlp_w1, mlp_w2, rope_const, out):

    PACKS = [("gla", 0), ("gla", 1), ("hg", 0), ("hg", 1), ("hg", 2), ("hg", 3)]
    HEAD = [4, 5, 6, 7, 0, 1, 2, 3]
    PACK_OF = [0, 0, 1, 1, 2, 3, 4, 5]
    FIRST = [0, 2, 4, 5, 6, 7]

    def gate_col(o):
        return GR + (HEAD[o] - 4) * P if HEAD[o] >= 4 else HG + HEAD[o] * P

    def key_tiles(p):
        kind, a = PACKS[p]
        if kind == "gla":
            return [(("k", p), GK + a * P), (("q", p), GQ + a * P), (("z", p), None)]
        return [(("f", p), HF + a * P), (("q", p), HQ + a * P)]

    def value_tiles(p):
        kind, a = PACKS[p]
        return [(("v", o), (GV + (HEAD[o] - 4) * P) if kind == "gla" else HI + a * P)
                for o in range(8) if PACK_OF[o] == p]

    GATES = [(), (), (0, 1), (2, 3), (), (4,), (5,), (6, 7)]
    SLOTS = []
    for st in range(8):
        values = value_tiles(st - 1) if 1 <= st < 7 else []
        turned = [(("w", o), None) for (_, o), _ in values]
        keys = key_tiles(st) if st < 6 else []
        gates = [(("g", o), gate_col(o)) for o in GATES[st]]
        first = (keys or gates)[:1]
        todo = values + first + turned + [t for t in gates + keys if t not in first]
        items = [(st - 1, lv) for lv in range(LEVELS + 2)] if 1 <= st < 7 else []
        groups = [(o, c) for o in range(8) if PACK_OF[o] == st - 2 for c in range(NT)] if st >= 2 else []
        if st == 7:
            todo += [(None, None)] * 2
        long_ = [i for i, (tile, col) in enumerate(todo) if col is not None or tile is None]
        n = len(long_)
        for i, (tile, col) in enumerate(todo):
            a, b = (long_.index(i), long_.index(i) + 1) if i in long_ else (0, 0)
            SLOTS.append((tile, col, items[a * len(items) // n:b * len(items) // n],
                          groups[a * len(groups) // n:b * len(groups) // n],
                          st if i == len(todo) - 1 and st < 6 else None))
    SLOTS += [(None, None, [], [], None)] * 5
    OUTPUTS, SQUARES, SUMS, MIXES = [[[] for _ in SLOTS] for _ in range(4)]
    pending = [[], []]
    for i, (tile, col, _, groups, _) in enumerate(SLOTS):
        if col is not None or tile is None:
            OUTPUTS[i] = pending[0]
            pending = [pending[1], groups]
            for o, c in OUTPUTS[i]:
                if c == NT - 1:
                    SQUARES[i].append(o)
    square_slot = [i for i in range(len(SLOTS)) for _ in SQUARES[i]] + [len(SLOTS) - 2]
    for o in range(8):
        gap = min(square_slot[o + 1] - square_slot[o], 3)
        MIXES[square_slot[o] + gap].append(o)
        SUMS[square_slot[o] + gap - 1].append(o)

    def rows(w, c0, c1):
        return w[:, c0:c1].rearrange("(k p) c -> p k c", p=P)

    units = []
    tile_of_unit = []
    tile_no = {}
    unit_no = {}

    def add_tile(name, unit=None):
        tile_no[name] = len(tile_no)
        if unit is not None:
            tile_of_unit[unit] = tile_no[name]

    def add_unit(name, loads):
        unit_no[name] = len(units)
        units.append(loads)
        tile_of_unit.append(None)
        return unit_no[name]

    for k in range(KD):
        add_tile(("x", k))
    w = ev_w_in[0]
    add_tile(("ga", 0), add_unit(("ga", 0), [((KD, GATE_RANK), 0, GATE_RANK, rows(w, GA, GA + GATE_RANK))]))
    for tile, col, *_ in SLOTS:
        if tile is not None:
            add_tile(tile, None if col is None else add_unit(tile, [((KD, P), 0, P, rows(w, col, col + P))]))
    for m in range(KD):
        add_tile(("eo", m), add_unit(("eo", m), [((KD, P), 0, P, rows(ev_w_out[0], m * P, (m + 1) * P))]))
        add_tile(("x2", m))

    def add_mlp(layer):
        for g in range(GROUPS):
            for m in range(2 * KD):
                add_tile(("mlp", layer, g, m), add_unit(("mlp", layer, g, m), None))

    add_mlp(0)
    w = od_w_in[0]
    for m in range(5):
        add_tile(("oi", m), add_unit(("oi", m), [((KD, P), 0, P, rows(w, m * P, (m + 1) * P))]))
    R0, RH = 5 * P, ROPE // 2
    add_tile(("oi", 5), add_unit(("oi", 5), [((KD, P), c, c + ROPE, rows(w, R0, R0 + ROPE)) for c in (0, ROPE)]))
    add_tile(("oi", 6), add_unit(("oi", 6), [((KD, P), c + d, c + d + RH, rows(w, R0 + RH - d, R0 + 2 * RH - d))
                                             for c in (0, ROPE) for d in (0, RH)]))
    w = mla_w_ukv[0].rearrange("(k p) (h c) -> k p h c", p=P, c=NOPE + VDIM)
    for what, c0 in (("mv", NOPE), ("mk", 0)):
        for g in range(2):
            u = add_unit((what, g), [((KV_RANK_T, 4 * P), None, k, w[k, :, 4 * g:4 * g + 4, c0:c0 + P])
                                     for k in range(KV_RANK_T)])
            for j in range(4):
                add_tile((what, g, j), u)
    w = mla_w_uq[0]
    for a in range(MLA_HEADS // 2):
        c = 2 * a * (NOPE + ROPE)
        u = add_unit(("qn", a), [((Q_RANK_T, 2 * P), hh * P, (hh + 1) * P, rows(w, c + hh * 192, c + hh * 192 + NOPE))
                                 for hh in range(2)])
        add_tile(("qn", a, 0), u)
        add_tile(("qn", a, 1), u)
        loads = [((Q_RANK_T, 2 * P), hh * ROPE, (hh + 1) * ROPE, rows(w, c + hh * 192 + NOPE, c + (hh + 1) * 192))
                 for hh in range(2)]
        for hh in range(2):
            r0 = c + hh * 192 + NOPE
            loads += [((Q_RANK_T, 2 * P), P + hh * ROPE + d, P + hh * ROPE + d + RH,
                       rows(w, r0 + RH - d, r0 + 2 * RH - d)) for d in (0, RH)]
        u = add_unit(("qr", a), loads)
        add_tile(("qr", a, 0), u)
        add_tile(("qr", a, 1), u)
    for m in range(KD):
        add_tile(("oo", m), add_unit(("oo", m), [((KD, P), 0, P, rows(od_w_out[0], m * P, (m + 1) * P))]))
    add_mlp(1)
    for m in range(2 * NT):
        add_tile(("out", m))
    n_units = len(units)
    loaded = []
    for u, loads in enumerate(units):
        loaded.append((loaded[u - STAGE] if u >= STAGE else 0) + 16 * (1 if loads is None else len(loads)))

    def unit_size(u):
        return UNIT if units[u] is None else units[u][0][0][0] * units[u][0][0][1]

    with ExitStack() as ctx:
        def sb(name, shape, dt=F32, scope=ctx):
            return scope.enter_context(nc.sbuf_tensor(name, shape, dt))

        def sem(name):
            return ctx.enter_context(nc.semaphore(name))

        xT = sb("xT", [P, KD, T])
        h_hi = sb("h_hi", [P, KD, T], F32R)
        h_lo = sb("h_lo", [P, KD, T], F32R)
        a_hi = sb("a_hi", [P, KD, T], F32R)
        a_lo = sb("a_lo", [P, KD, T], F32R)
        y = sb("y", [P, KD, T])
        stage = sb("stage", [P, STAGE, UNIT])
        w_hi = sb("w_hi", [P, SPLIT, UNIT], F32R)
        w_lo = sb("w_lo", [P, SPLIT, UNIT], F32R)
        ident = sb("ident", [P, P])
        ones = sb("ones", [P, P])
        eps = sb("eps", [P, 1])
        masks = sb("masks", [P, PAIRS, P])
        vec = sb("vec", [P, V_ROWS])
        lbt = sb("lbt", [P, 6, HEADS])
        w_gate = sb("w_gate", [GATE_RANK, HEADS * GLA_DK])
        ropec = sb("ropec", [P, 2])
        sq = sb("sq", [P, 2, T])
        tmp = sb("tmp", [P, 2, T])
        rinv = sb("rinv", [P, 2, T])

        with ExitStack() as s1:
            x_tok = sb("x_tok", [P, NT, D], F32, s1)
            vrows = sb("vrows", [V_ROWS, P], F32, s1)
        with ExitStack() as s2:
            vbuf = sb("vbuf", [P, 4, T], F32, s2)
            xl = sb("xl", [P, LEVELS, T], F32, s2)
            dec = sb("dec", [P, 3, T], F32, s2)
            q_sb = sb("q_sb", [P, 2, T], F32, s2)
            k_sb = sb("k_sb", [P, 2, T], F32, s2)
            b_sb = sb("b_sb", [P, T], F32, s2)
            qe0 = sb("qe", [P, T], F32, s2)
            ke = sb("ke", [P, T], F32, s2)
            e_last = sb("e_last", [P, 2, NT], F32, s2)
            a_sb = sb("a_sb", [P, 4, P], F32, s2)
            ke_t = sb("ke_t", [P, NT - 1, P], F32, s2)
            state = sb("state", [P, NT - 1, P], F32, s2)
            t_f = sb("t_f", [P, T], F32, s2)
            t_g = sb("t_g", [P, T], F32, s2)
            ga_t = sb("ga_t", [GATE_RANK, T], F32, s2)
        xls = [xl[:, :, :], xT[:, 0:LEVELS, :]]
        qes = [qe0[:, :], xT[:, LEVELS, :]]
        qs = [q_sb[:, 0, :], q_sb[:, 1, :], y[:, 6, :]]
        ks = [k_sb[:, 0, :], k_sb[:, 1, :], y[:, 7, :]]
        GATE_SLOTS = 6
        with ExitStack() as s3:
            v_tok = sb("v_tok", [P, NT, D], F32, s3)
            kr = sb("kr", [P, T], F32, s3)
            cosd = sb("cosd", [P, T], F32, s3)
            sind = sb("sind", [P, T], F32, s3)
            ang = sb("ang", [P, T], F32, s3)
            qn = sb("qn", [P, 2, 2, T], F32, s3)
            qr = sb("qr", [P, 2, T], F32, s3)
            prob = sb("prob", [P, 3, T], F32, s3)
            p_t = sb("p_t", [P, NT, T], F32, s3)
            pos_i = p_t[:, 0, :].bitcast(I32)
            mask_q = sb("mask_q", [P, P], F32, s3)
            mask_k = sb("mask_k", [P, P], F32, s3)
            stat = sb("stat", [P, 3, 4 * MLA_HEADS], F32, s3)

        bank = [ctx.enter_context(nc.psum_tensor(f"bank{b}", [P, T], F32)) for b in range(2)]
        pp = [ctx.enter_context(nc.psum_tensor(f"pp{b}", [P, 8, P], F32)) for b in range(2)]
        po = ctx.enter_context(nc.psum_tensor("po", [P, T], F32))
        misc = ctx.enter_context(nc.psum_tensor("misc", [P, T], F32))
        s_bank = [pp[0][:, 0:4, :], pp[0][:, 4:8, :], pp[1][:, 0:4, :]]
        s_bank = [v.rearrange("p a b -> p (a b)") for v in s_bank]
        t_bank = [pp[1][:, 4:8, :], misc[:, :].rearrange("p (a b) -> p a b", a=4)]

        x_in = [sem(f"x_in{i}") for i in range(4)]
        vec_in, consts_ready, vec_done = sem("vec_in"), sem("consts_ready"), sem("vec_done")
        vec_ready, pos_in, out_stored = sem("vec_ready"), sem("pos_in"), sem("out_stored")
        stage_in = [sem(f"stage_in{s}") for s in range(STAGE)]
        hi_ready, lo_ready = sem("hi_ready"), sem("lo_ready")
        tile_done = sem("tile_done")
        act_chain, dve_chain, pool_chain = sem("act_chain"), sem("dve_chain"), sem("pool_chain")
        x_ready = sem("x_ready")
        y_ready = {j: sem(f"y_ready{j}") for j in (1, 3, 5, 7)}
        sq_ready = [sem(f"sq_ready{j}") for j in range(9)]
        sq_used = [sem(f"sq_used{j}") for j in range(9)]
        r_ready = [sem(f"r_ready{j}") for j in range(9)]
        h_f32, h_high, h_ready = sem("h_f32"), sem("h_high"), sem("h_ready")
        f_sig, f_gate, f_log, b_ready = sem("f_sig"), sem("f_gate"), sem("f_log"), sem("b_ready")
        g_sig, gate_ready, q_ready, k_ready = sem("g_sig"), sem("gate_ready"), sem("q_ready"), sem("k_ready")
        v_ready, ga_ready, d_ready, e_ready = sem("v_ready"), sem("ga_ready"), sem("d_ready"), sem("e_ready")
        xl_ready, ket_done, ket_ready = sem("xl_ready"), sem("ket_done"), sem("ket_ready")
        kv_done, state_ready, p_done, p_read = sem("kv_done"), sem("state_ready"), sem("p_done"), sem("p_read")
        a_ready, o_done, o_sq, o_sum = sem("a_ready"), sem("o_done"), sem("o_sq"), sem("o_sum")
        o_rinv, o_read, mix_f32, mix_high, mix_ready = (sem("o_rinv"), sem("o_read"), sem("mix_f32"),
                                                        sem("mix_high"), sem("mix_ready"))
        c_ready, rope_ready, vt_ready, kt_ready = sem("c_ready"), sem("rope_ready"), sem("vt_ready"), sem("kt_ready")
        sin_arg, sin_ready, qn_ready, qr_ready = sem("sin_arg"), sem("sin_ready"), sem("qn_ready"), sem("qr_ready")
        s_done, nmax_ready, prob_exp, prob_ready = sem("s_done"), sem("nmax_ready"), sem("prob_exp"), sem("prob_ready")
        pt_done, pt_ready, pv_done, att_high, att_ready = (sem("pt_done"), sem("pt_ready"), sem("pv_done"),
                                                           sem("att_high"), sem("att_ready"))
        relu_ready = [sem(f"relu_ready{l}") for l in range(2)]
        hid_f32 = [sem(f"hid_f32_{l}") for l in range(2)]
        hid_high = [sem(f"hid_high{l}") for l in range(2)]
        hid_ready = [sem(f"hid_ready{l}") for l in range(2)]
        y_zero = [sem(f"y_zero{l}") for l in range(2)]
        x_again, x2_ready = sem("x_again"), sem("x2_ready")
        v_raw, p_zero, f_clamped, g_clamped = sem("v_raw"), sem("p_zero"), sem("f_clamped"), sem("g_clamped")
        z_read, kr_read, rot_read = sem("z_read"), sem("kr_read"), sem("rot_read")
        out_ready = sem("out_ready")

        read = {}

        def says(name, s, value):
            read[tile_no[name]] = (s, value)

        for k in range(KD):
            says(("x", k), x_ready, k + 1)
            says(("eo", k), y_ready[1], k + 1)
            says(("oo", k), y_ready[5], k + 1)
            says(("out", k), out_ready, k + 1)
            for layer, j in ((0, 3), (1, 7)):
                for g in range(GROUPS):
                    says(("mlp", layer, g, k), hid_f32[layer], g * KD + k + 1)
                    says(("mlp", layer, g, KD + k), y_ready[j], g * KD + k + 1)
            if k < 7:
                says(("oi", k), c_ready if k < 5 else kr_read, k + 1 if k < 5 else k - 4)
            says(("mv", k // 4, k % 4), vt_ready, k + 1)
            says(("mk", k // 4, k % 4), kt_ready, k + 1)
            says(("qn", k // 2, k % 2), qn_ready, k + 1)
            says(("qr", k // 2, k % 2), rot_read, k + 1)
        says(("ga", 0), ga_ready, 1)
        for (what, i) in [t for t, *_ in SLOTS if t is not None]:
            says((what, i), *{"f": (f_clamped, i - 1), "g": (gate_ready, i + 1), "q": (q_ready, i + 1),
                              "k": (k_ready, i + 1), "z": (z_read, i + 1), "v": (v_raw, i + 1), "w": (v_ready, i + 1)}[what])
        for k in range(KD):
            says(("x2", k), x2_ready, k + 1)

        def wait_read(eng, n):
            eng.wait_ge(*read[n])

        def wait_bank(eng, n, i=None):
            if i is None:
                if n >= 2:
                    wait_read(eng, n - 2)
            else:
                s, value = read[n - 2]
                eng.wait_ge(s, value + KD * (i - 1))

        def wait_tile(eng, n, i=0):
            eng.wait_ge(tile_done, n + 1 + 16 * i)

        def split_high(act, u, i=0):
            if u >= n_units:
                return
            act.wait_ge(stage_in[u % STAGE], loaded[u] + 16 * (16 // STAGE) * i)
            if u >= SPLIT:
                act.wait_ge(tile_done, tile_of_unit[u - SPLIT] + 1 + 16 * i)
            n = unit_size(u)
            nc.scalar.copy(w_hi[:, u % SPLIT, 0:n], stage[:, u % STAGE, 0:n]).then_inc(hi_ready, 1)

        def split_low(dve, u, i=0):
            if u >= n_units:
                return
            dve.wait_ge(hi_ready, u + 1 + 16 * i)
            n = unit_size(u)
            nc.vector.tensor_tensor(w_lo[:, u % SPLIT, 0:n], stage[:, u % STAGE, 0:n],
                                    w_hi[:, u % SPLIT, 0:n].bitcast(F32), ALU.subtract).then_inc(lo_ready, 1)

        AHEAD_HI, AHEAD_LO = SPLIT, SPLIT - 1

        class Chain:
            def __init__(self, eng, s):
                self.eng, self.sem, self.n = eng, s, 0

            def link(self, ins, i=0, per=0):
                self.n += 1
                ins.then_inc(self.sem, 1)
                self.eng.wait_ge(self.sem, self.n + per * i)

        def halves(ap, L):
            return ap.rearrange("p (b h j) -> p b h j", h=2, j=L)

        def gain(layer, n, k):
            c = (layer * 4 + n) * KD + k
            return vec[:, c:c + 1]

        block = ctx.enter_context(nc.Block())

        @block.sync
        def _(sp):
            for i in range(4):
                c = slice(i * 2 * P, (i + 1) * 2 * P)
                sp.dma_start(x_tok[:, :, c], x[0].rearrange("(t p) d -> p t d", p=P)[:, :, c]).then_inc(x_in[i], 16)

            def stage_free(u, i=0):
                if u >= STAGE:
                    sp.wait_ge(hi_ready, u - STAGE + 1 + 16 * i)
                    sp.wait_ge(lo_ready, u - STAGE + 1 + 16 * i)

            def load(u):
                stage_free(u)
                for shape, c0, c1, src in units[u]:
                    size = shape[0] * shape[1]
                    slot = stage[:, u % STAGE, 0:size].rearrange("p (k c) -> p k c", k=shape[0])
                    if c0 is None:
                        dst = slot[:, c1, :].rearrange("p (h c) -> p h c", c=P)
                    else:
                        dst = slot[:, :, c0:c1]
                    sp.dma_start(dst, src).then_inc(stage_in[u % STAGE], 16)

            def load_mlp(layer):
                u0 = unit_no[("mlp", layer, 0, 0)]
                w1 = mlp_w1[layer].rearrange("(k p) n -> p k n", p=P)
                w2 = mlp_w2[layer].rearrange("(g k p) n -> p (g k) n", p=P, k=KD)
                with sp.Fori(0, GROUPS) as i:
                    for m in range(2 * KD):
                        u = u0 + m
                        stage_free(u, i)
                        dst = stage[:, u % STAGE, :].rearrange("p (k c) -> p k c", k=KD)
                        if m < KD:
                            src = w1[:, :, bass.ds(i * D + m * P, P)]
                        else:
                            src = w2[:, bass.ds(i * KD, KD), (m - KD) * P:(m - KD + 1) * P]
                        sp.dma_start(dst, src).then_inc(stage_in[u % STAGE], 16)

            for u in range(unit_no[("mlp", 0, 0, 0)]):
                load(u)
            load_mlp(0)
            sp.dma_start(pos_i, positions.partition_broadcast(P)).then_inc(pos_in, 16)
            for u in range(unit_no[("oi", 0)], unit_no[("mlp", 1, 0, 0)]):
                load(u)
            load_mlp(1)
            for m in range(2 * NT):
                t, half = divmod(m, 2)
                sp.wait_ge(out_ready, m + 1)
                sp.dma_start(out[0, t * P:(t + 1) * P, half * T:(half + 1) * T], y[:, m, :]).then_inc(out_stored, 16)
            sp.wait_ge(out_stored, 16 * 2 * NT)

        @block.gpsimd
        def _(pool):
            nc.gpsimd.memset(ones[:, :], 1.0).then_inc(consts_ready, 1)
            nc.gpsimd.memset(eps[:, :], EPS).then_inc(consts_ready, 1)
            ch = Chain(pool, pool_chain)
            ch.link(nc.gpsimd.memset(ident[:, :], 0.0))
            nc.gpsimd.affine_select(out=ident[:, :], in_=ident[:, :], compare_op=ALU.not_equal, fill=1.0, base=0,
                                    pattern=[[-1, P]], channel_multiplier=1).then_inc(consts_ready, 1)
            ch.link(nc.gpsimd.memset(masks[:, :, :], 0.0))
            ch.link(nc.gpsimd.memset(masks[:, 0, :], 1.0))
            for lv in range(2, LEVELS):
                L = 64 >> lv
                right = masks[:, lv - 1, :].rearrange("p (b h j) -> p b h j", h=2, j=L)[:, :, 1, :]
                ch.link(nc.gpsimd.memset(right, 1.0))
                ch.link(nc.gpsimd.affine_select(out=right, in_=right, compare_op=ALU.is_ge, fill=0.0, base=0,
                                                pattern=[[-2 * L, P // (2 * L)], [0, L]], channel_multiplier=1))
                ch.link(nc.gpsimd.affine_select(out=right, in_=right, compare_op=ALU.is_ge, fill=0.0, base=L - 1,
                                                pattern=[[2 * L, P // (2 * L)], [0, L]], channel_multiplier=-1))
            nc.gpsimd.affine_select(out=masks[:, PAIRS - 1, :], in_=masks[:, PAIRS - 1, :], compare_op=ALU.not_equal,
                                    fill=1.0, base=0, pattern=[[-1, P]], channel_multiplier=1).then_inc(consts_ready, 1)

            for p in range(len(PACKS)):
                pool.wait_ge(b_ready, p + 1)
                for lv in range(LEVELS + 1):
                    item = p * (LEVELS + 2) + lv
                    if item >= 3:
                        pool.wait_ge(xl_ready, item - 2)
                    L = 64 >> lv
                    if lv < LEVELS:
                        ref = halves(b_sb[:, :], L)[:, :, 0, L - 1:L]
                    else:
                        L = P // 2
                        ref = halves(b_sb[:, :], L)[:, :, 1, L - 1:L]
                    shape = [P, T // (2 * L), 2 * L]
                    nc.gpsimd.tensor_tensor(dec[:, item % 3, :].rearrange("p (b j) -> p b j", j=2 * L),
                                            b_sb[:, :].rearrange("p (b j) -> p b j", j=2 * L),
                                            ref.to_broadcast(shape), ALU.subtract).then_inc(d_ready, 1)
            pool.wait_ge(mix_ready, 8)
            pool.dma_start(x_tok[:, :, :], x[0].rearrange("(t p) d -> p t d", p=P)).then_inc(x_again, 16)
            pool.wait_ge(y_zero[0], 1)
            ch.link(nc.gpsimd.memset(mask_q[:, :], 0.0))
            ch.link(nc.gpsimd.memset(mask_k[:, :], 0.0))
            nc.gpsimd.memset(mask_q[0:1, 0:P // 2], MASKED).then_inc(consts_ready, 1)
            nc.gpsimd.memset(mask_k[0:1, P // 2:P], 1.0).then_inc(consts_ready, 1)

        @block.scalar
        def _(act):
            ch = Chain(act, act_chain)
            small = [(0, norm_gains.rearrange("l n (k p) -> (l n k) p", p=P)),
                     (V_LB, hg_lb_table.rearrange("r (h p) -> (r h) p", p=P)),
                     (V_BG, gla_b_gate.rearrange("e (k p) -> (e k) p", p=P)),
                     (V_HGN, hg_out_norm), (V_GLN, gla_out_norm),
                     (V_QN, mla_q_norm.rearrange("e (k p) -> (e k) p", p=P)),
                     (V_KVN, mla_kv_norm.rearrange("e (k p) -> (e k) p", p=P))]
            for r, src in small:
                act.dma_start(vrows[r:r + src.shape[0], :], src).then_inc(vec_in, 16)
            act.dma_start(w_gate[:, :], gla_w_gate[0]).then_inc(vec_in, 16)
            act.dma_start(ropec[:, :], rope_const).then_inc(vec_in, 16)

            def inv_rms(src, width, slot, ready):
                ch.link(nc.scalar.activation(rinv[:, slot, :], src, ACT.Ln, bias=eps[:, 0:1], scale=1.0 / width))
                nc.scalar.activation(rinv[:, slot, :], rinv[:, slot, :], ACT.Exp, scale=-0.5).then_inc(ready, 1)

            def pre_norm(j, xs, hs, split_first=False):
                for k in range(KD):
                    act.wait_ge(x_ready, xs + k + 1)
                    if k >= 2:
                        act.wait_ge(sq_used[j], k - 1)
                    nc.scalar.activation(sq[:, k % 2, :], xT[:, k, :], ACT.Square).then_inc(sq_ready[j], 1)
                    if split_first and k == KD // 2:
                        split_high(act, 0)
                act.wait_ge(sq_used[j], KD)
                inv_rms(misc[:, :], D, 0, r_ready[j])
                if split_first:
                    split_high(act, 1)
                    split_high(act, 2)
                for k in range(KD):
                    act.wait_ge(h_f32, hs + k + 1)
                    nc.scalar.copy(h_hi[:, k, :], tmp[:, k % 2, :]).then_inc(h_high, 1)
                if split_first:
                    split_high(act, 3)

            def y_square(j, ys, m):
                act.wait_ge(y_ready[j], ys + m + 1)
                if m >= 2:
                    act.wait_ge(sq_used[j], m - 1)
                nc.scalar.activation(sq[:, m % 2, :], y[:, m, :], ACT.Square).then_inc(sq_ready[j], 1)

            def post_norm(j):
                act.wait_ge(sq_used[j], KD)
                inv_rms(misc[:, :], D, 1, r_ready[j])

            def pump(u, i=0):
                split_high(act, u + AHEAD_HI, i)

            nc.scalar.preload_act_table_set("natural_log_exp_and_others")
            act.wait_ge(consts_ready, 4)
            act.wait_ge(vec_ready, 2)
            nc.scalar.activation(lbt[:, 1:3, :], lbt[:, 1:3, :], ACT.Exp).then_inc(vec_ready, 1)
            pre_norm(0, 0, 0, split_first=True)

            n = tile_no[("ga", 0)]
            wait_tile(act, n)
            nc.scalar.copy(ga_t[:, :], bank[n % 2][0:GATE_RANK, :]).then_inc(ga_ready, 1)
            pump(unit_no[("ga", 0)])

            def decay(p, lv):
                s = 1.0 if PACKS[p][0] == "hg" else 1.0 / GATE_TEMP
                item = p * (LEVELS + 2) + lv
                d = dec[:, item % 3, :]
                if lv <= LEVELS:
                    act.wait_ge(d_ready, p * (LEVELS + 1) + lv + 1)
                if lv < LEVELS:
                    v = halves(d, 64 >> lv)
                    nc.scalar.activation(v[:, :, 0, :], v[:, :, 0, :], ACT.Exp, scale=-s).then_inc(e_ready, 1)
                    nc.scalar.activation(v[:, :, 1, :], v[:, :, 1, :], ACT.Exp, scale=s).then_inc(e_ready, 1)
                elif lv == LEVELS:
                    nc.scalar.activation(d, d, ACT.Exp, scale=-s).then_inc(e_ready, 1)
                    if p >= 2:
                        act.wait_ge(state_ready, p - 1)
                    last = b_sb[:, :].rearrange("p (c j) -> p c j", j=P)[:, :, P - 1]
                    nc.scalar.activation(e_last[:, p % 2, :], last, ACT.Exp, scale=s).then_inc(e_ready, 1)
                else:
                    act.wait_ge(xl_ready, item - 2)
                    nc.scalar.activation(d, b_sb[:, :], ACT.Exp, scale=s).then_inc(e_ready, 1)

            def sigmoid(t, clamped, ready):
                act.wait_ge(*clamped)
                ch.link(nc.scalar.activation(t, t, ACT.Exp, scale=-1.0))
                ch.link(nc.scalar.activation(t, t, ACT.Ln, bias=1.0))
                nc.scalar.activation(t, t, ACT.Exp, scale=-1.0).then_inc(ready, 1)

            def evacuate(what, i):
                n = tile_no[(what, i)]
                ps = bank[n % 2][:, :]
                wait_tile(act, n)
                if what in ("q", "k") and i >= 3:
                    act.wait_ge(p_done, NT * FIRST[i - 2])
                if what == "f":
                    sigmoid(t_f[:, :], (f_clamped, i - 1), f_sig)
                elif what == "g":
                    sigmoid(t_g[:, :], (g_clamped, i + 1), g_sig)
                elif what == "q":
                    scale = 1.0 if PACKS[i][0] == "hg" else GLA_DK ** -0.5
                    nc.scalar.activation(qs[i % 3], ps, ACT.Copy, scale=scale).then_inc(q_ready, 1)
                    if PACKS[i][0] == "hg":
                        act.wait_ge(f_gate, i + 1)
                        nc.scalar.activation(t_f[:, :], t_f[:, :], ACT.Ln).then_inc(f_log, 1)
                elif what == "k":
                    nc.scalar.activation(ks[i % 3], ps, ACT.Copy).then_inc(k_ready, 1)
                elif what == "v":
                    if i >= 4:
                        act.wait_ge(o_done, i - 3)
                    nc.scalar.activation(vbuf[:, i % 4, :], ps, ACT.Copy).then_inc(v_raw, 1)
                elif what == "w":
                    nc.scalar.activation(vbuf[:, i % 4, :], ps, ACT.Copy).then_inc(v_ready, 1)
                elif what == "z":
                    if i >= 1:
                        act.wait_ge(b_ready, i)
                    bg = vec[:, V_BG + i:V_BG + i + 1]
                    nc.scalar.activation(t_f[:, :], ps, ACT.Identity, bias=bg).then_inc(z_read, 1)
                    act.wait_ge(z_read, i + 1)
                    ch.link(nc.scalar.activation(t_g[:, :], t_f[:, :], ACT.Abs))
                    ch.link(nc.scalar.activation(t_g[:, :], t_g[:, :], ACT.Exp, scale=-1.0))
                    nc.scalar.activation(t_g[:, :], t_g[:, :], ACT.Ln, bias=1.0).then_inc(f_log, 1)

            def head_square(o):
                act.wait_ge(o_done, o + 1)
                if o >= 1:
                    act.wait_ge(o_sum, o)
                    act.wait_ge(mix_ready, o)
                nc.scalar.activation(sq[:, 0, :], po[:, :], ACT.Square).then_inc(o_sq, 1)
                nc.scalar.activation(sq[:, 1, :], po[:, :], ACT.Copy).then_inc(o_read, 1)

            def head_norm(o):
                act.wait_ge(o_sum, o + 1)
                if o >= 1:
                    act.wait_ge(mix_f32, o)
                inv_rms(misc[:, :], P, 0, o_rinv)

            def head_high(o):
                act.wait_ge(mix_f32, o + 1)
                nc.scalar.copy(a_hi[:, HEAD[o], :], sq[:, 1, :]).then_inc(mix_high, 1)

            for i, (tile, col, items, groups, end) in enumerate(SLOTS):
                if tile is not None:
                    evacuate(*tile)
                    if col is not None:
                        pump(unit_no[tile])
                for p, lv in items:
                    decay(p, lv)
                for o in SUMS[i]:
                    head_norm(o)
                for o in MIXES[i]:
                    head_high(o)
                for o in SQUARES[i]:
                    head_square(o)
                for o, c in groups:
                    p = PACK_OF[o]
                    if c == 0 and FIRST[p] == o:
                        act.wait_ge(ket_done, p + 1)
                        nc.scalar.activation(ke_t[:, :, :].rearrange("p c d -> p (c d)"), misc[:, 0:(NT - 1) * P],
                                             ACT.Copy).then_inc(ket_ready, 1)

            def linear_out(name, j):
                for m in range(KD):
                    if m >= 1:
                        y_square(j, 0, m - 1)
                    wait_tile(act, tile_no[(name, m)])
                    pump(unit_no[(name, m)])
                y_square(j, 0, KD - 1)
                post_norm(j)

            linear_out("eo", 1)
            pre_norm(2, KD, KD)

            def mlp(layer, j):
                n0, u0 = tile_no[("mlp", layer, 0, 0)], unit_no[("mlp", layer, 0, 0)]

                def group(i, last):
                    for m in range(2 * KD):
                        n = n0 + m
                        wait_tile(act, n, i)
                        if m < KD:
                            if m >= 2:
                                act.wait_ge(hid_f32[layer], m - 1 + KD * i)
                            nc.scalar.activation(sq[:, m % 2, :], bank[n % 2][:, :], ACT.Relu).then_inc(relu_ready[layer], 1)
                        if not last or m < 2 * KD - AHEAD_HI or layer == 0:
                            pump(u0 + m, i)
                        if m < KD:
                            act.wait_ge(hid_f32[layer], m + 1 + KD * i)
                            nc.scalar.copy(a_hi[:, m, :], tmp[:, m % 2, :]).then_inc(hid_high[layer], 1)
                        elif last and m > KD:
                            y_square(j, (GROUPS - 1) * KD, m - KD - 1)

                with act.Fori(0, GROUPS - 1) as i:
                    group(i, False)
                group(GROUPS - 1, True)
                y_square(j, (GROUPS - 1) * KD, KD - 1)
                post_norm(j)

            mlp(0, 3)

            pre_norm(4, 2 * KD, 2 * KD)
            for m in range(5):
                n = tile_no[("oi", m)]
                wait_tile(act, n)
                nc.scalar.activation(y[:, m, :], bank[n % 2][:, :], ACT.Copy).then_inc(c_ready, 1)
                act.wait_ge(c_ready, m + 1)
                if m >= 2:
                    act.wait_ge(sq_used[8], m - 1)
                nc.scalar.activation(sq[:, m % 2, :], y[:, m, :], ACT.Square).then_inc(sq_ready[8], 1)
                pump(unit_no[("oi", m)])
            for m in (5, 6):
                wait_tile(act, tile_no[("oi", m)])
                pump(unit_no[("oi", m)])
            act.wait_ge(sq_used[8], 5)
            inv_rms(po[:, :], KV_RANK_T * P, 1, r_ready[8])
            inv_rms(misc[:, :], Q_RANK_T * P, 0, r_ready[8])
            for j, k in enumerate((3, 4, 0, 1, 2)):
                act.wait_ge(h_f32, 3 * KD + j + 1)
                nc.scalar.copy(h_hi[:, k, :], tmp[:, j % 2, :]).then_inc(h_high, 1)
            act.wait_ge(sin_arg, 1)
            nc.scalar.activation(sind[:, :], sind[:, :], ACT.Sin).then_inc(sin_ready, 1)
            nc.scalar.activation(cosd[:, :], cosd[:, :], ACT.Sin).then_inc(sin_ready, 1)
            nc.scalar.preload_act_table_set("natural_log_exp_and_others")
            for what in ("mv", "mk"):
                for g in range(2):
                    for j in range(4):
                        n = tile_no[(what, g, j)]
                        wait_tile(act, n)
                        dst = v_tok[:, j, g * T:(g + 1) * T] if what == "mv" else y[:, 4 * g + j, :]
                        nc.scalar.activation(dst, bank[n % 2][:, :], ACT.Copy).then_inc(
                            vt_ready if what == "mv" else kt_ready, 1)
                    pump(unit_no[(what, g)])

            def q_evacuate(a):
                if a == 1:
                    act.wait_ge(rope_ready, 1)
                for hh in range(2):
                    n = tile_no[("qn", a, hh)]
                    wait_tile(act, n)
                    nc.scalar.activation(qn[:, a % 2, hh, :], bank[n % 2][:, :], ACT.Copy,
                                         scale=SCALE).then_inc(qn_ready, 1)
                pump(unit_no[("qn", a)])
                wait_tile(act, tile_no[("qr", a, 1)])
                pump(unit_no[("qr", a)])

            def att_out(h):
                act.wait_ge(pv_done, h + 1)
                nc.scalar.copy(a_hi[:, h, :], po[:, :]).then_inc(att_high, 1)

            q_evacuate(0)
            for j in range(4 * MLA_HEADS + 2):
                if j % 8 == 0 and j // 8 + 1 < MLA_HEADS // 2:
                    q_evacuate(j // 8 + 1)
                if j < 4 * MLA_HEADS:
                    width = (j % 4 + 1) * P
                    act.wait_ge(nmax_ready, j + 1)
                    nc.scalar.activation(prob[:, j % 3, 0:width], s_bank[j % 3][:, 0:width], ACT.Exp,
                                         bias=stat[:, 0, j:j + 1], accum_out=stat[:, 1, j:j + 1]).then_inc(prob_exp, 1)
                if j >= 6 and j % 4 == 2:
                    att_out(j // 4 - 1)
            att_out(MLA_HEADS - 1)
            linear_out("oo", 5)
            pre_norm(6, 3 * KD, 3 * KD + 5)
            mlp(1, 7)

        @block.vector
        def _(dve):
            ch = Chain(dve, dve_chain)

            def pump(u, i=0):
                split_low(dve, u + AHEAD_LO, i)

            def pre_norm(j, layer, which, hs):
                dve.wait_ge(r_ready[j], 1)
                for k in range(KD + 1):
                    if 2 <= k < KD:
                        dve.wait_ge(h_ready, hs + k - 1)
                    if k < KD:
                        nc.vector.scalar_tensor_tensor(out=tmp[:, k % 2, :], in0=xT[:, k, :], scalar=gain(layer, which, k),
                                                       in1=rinv[:, 0, :], op0=ALU.mult, op1=ALU.mult).then_inc(h_f32, 1)
                    if k >= 1:
                        dve.wait_ge(h_high, hs + k)
                        nc.vector.tensor_tensor(h_lo[:, k - 1, :], tmp[:, (k - 1) % 2, :],
                                                h_hi[:, k - 1, :].bitcast(F32), ALU.subtract).then_inc(h_ready, 1)
                dve.wait_ge(h_ready, hs + KD)

            def post_norm(j, layer, which):
                dve.wait_ge(r_ready[j], 1)
                for k in range(KD):
                    ch.link(nc.vector.scalar_tensor_tensor(out=y[:, k, :], in0=y[:, k, :], scalar=gain(layer, which, k),
                                                           in1=rinv[:, 1, :], op0=ALU.mult, op1=ALU.mult))
                    nc.vector.tensor_tensor(xT[:, k, :], xT[:, k, :], y[:, k, :], ALU.add).then_inc(x_ready, 1)

            dve.wait_ge(vec_done, 1)
            nc.vector.tensor_copy(vec[:, :], misc[:, 0:V_ROWS]).then_inc(vec_ready, 1)
            dve.wait_ge(vec_ready, 1)
            t0, t1 = vec[:, V_LB:V_LB + HEADS], vec[:, V_LB + HEADS:V_LB + 2 * HEADS]
            ch.link(nc.vector.tensor_tensor(lbt[:, 0, :], t0, t1, ALU.max))
            ch.link(nc.vector.tensor_tensor(lbt[:, 1, :], t0, lbt[:, 0, :], ALU.subtract))
            nc.vector.tensor_tensor(lbt[:, 2, :], t1, lbt[:, 0, :], ALU.subtract).then_inc(vec_ready, 1)
            dve.wait_ge(vec_ready, 3)
            ch.link(nc.vector.tensor_tensor(lbt[:, 0, :], lbt[:, 1, :], lbt[:, 2, :], ALU.add))
            ch.link(nc.vector.reciprocal(lbt[:, 3, :], lbt[:, 0, :]))
            ch.link(nc.vector.tensor_tensor(lbt[:, 4, :], lbt[:, 1, :], lbt[:, 3, :], ALU.mult))
            ch.link(nc.vector.tensor_scalar(lbt[:, 5, :], lbt[:, 4, :], -1.0, 1.0, ALU.mult, ALU.add))

            for b in range(2):
                nc.vector.memset(pp[b][:, 0, :], 0.0).then_inc(p_zero, 1)
            for k in range(KD):
                n = tile_no[("x", k)]
                wait_tile(dve, n)
                nc.vector.tensor_copy(xT[:, k, :], bank[n % 2][:, :]).then_inc(x_ready, 1)
            split_low(dve, 0)
            split_low(dve, 1)
            pre_norm(0, 0, 0, 0)
            split_low(dve, 2)
            wait_tile(dve, tile_no[("ga", 0)])
            pump(unit_no[("ga", 0)])

            def decayed(p, lv):
                item = p * (LEVELS + 2) + lv
                q, k, e, x_ = qs[p % 3], ks[p % 3], dec[:, item % 3, :], xls[p % 2]
                done = p * (2 * LEVELS + 3) + 2 * lv
                dve.wait_ge(e_ready, done + 2 if lv <= LEVELS else done + 1)
                if lv < LEVELS:
                    L = 64 >> lv
                    nc.vector.tensor_tensor(halves(x_[:, lv, :], L)[:, :, 0, :], halves(k, L)[:, :, 0, :],
                                            halves(e, L)[:, :, 0, :], ALU.mult)
                    nc.vector.tensor_tensor(halves(x_[:, lv, :], L)[:, :, 1, :], halves(q, L)[:, :, 1, :],
                                            halves(e, L)[:, :, 1, :], ALU.mult).then_inc(xl_ready, 1)
                elif lv == LEVELS:
                    if p >= 1:
                        dve.wait_ge(ket_done, p)
                    nc.vector.tensor_tensor(ke[:, :], k, e, ALU.mult).then_inc(xl_ready, 1)
                else:
                    if p >= 2:
                        dve.wait_ge(o_done, FIRST[p - 1])
                    nc.vector.tensor_tensor(qes[p % 2], q, e, ALU.mult).then_inc(xl_ready, 1)

            def clamp(what, i):
                n = tile_no[(what, i)]
                wait_tile(dve, n)
                if what == "f":
                    dve.wait_ge(b_ready, i)
                    nc.vector.tensor_scalar(t_f[:, :], bank[n % 2][:, :], EXP_MAX, None, ALU.max).then_inc(f_clamped, 1)
                else:
                    dve.wait_ge(f_gate, 2)
                    if i >= 1:
                        dve.wait_ge(gate_ready, i)
                    nc.vector.tensor_scalar(t_g[:, :], bank[n % 2][:, :], EXP_MAX, None, ALU.max).then_inc(g_clamped, 1)

            def evacuate(what, i):
                n = tile_no[(what, i)]
                if what == "f":
                    a = PACKS[i][1]
                    dve.wait_ge(f_sig, i - 1)
                    ch.link(nc.vector.tensor_scalar(t_f[:, :], t_f[:, :], lbt[:, 5, a:a + 1], lbt[:, 4, a:a + 1],
                                                    ALU.mult, ALU.add))
                    nc.vector.tensor_scalar(ks[i % 3], t_f[:, :], -1.0, 1.0, ALU.mult, ALU.add).then_inc(f_gate, 1)
                elif what == "g":
                    dve.wait_ge(g_sig, i + 1)
                    if i >= GATE_SLOTS:
                        dve.wait_ge(mix_f32, i - GATE_SLOTS + 1)
                    nc.vector.tensor_tensor(y[:, i % GATE_SLOTS, :], bank[n % 2][:, :], t_g[:, :],
                                            ALU.mult).then_inc(gate_ready, 1)
                elif what == "z":
                    dve.wait_ge(f_log, i + 1)
                    nc.vector.scalar_tensor_tensor(out=t_f[:, :], in0=t_f[:, :], scalar=0.0, in1=t_g[:, :],
                                                   op0=ALU.min, op1=ALU.subtract).then_inc(f_gate, 1)
                else:
                    wait_tile(dve, n)

            def cumulate(p):
                dve.wait_ge(f_log, p + 1)
                dve.wait_ge(f_gate, p + 1)
                for c in range(NT):
                    s = slice(c * P, (c + 1) * P)
                    ins = nc.vector.tensor_tensor_scan(b_sb[:, s], ones[:, :], t_f[:, s], 0.0, ALU.mult, ALU.add)
                ins.then_inc(b_ready, 1)

            def head_gate(o):
                dve.wait_ge(o_rinv, o + 1)
                g = V_HGN if HEAD[o] < 4 else V_GLN
                ch.link(nc.vector.scalar_tensor_tensor(out=sq[:, 1, :], in0=sq[:, 1, :], scalar=vec[:, g:g + 1],
                                                       in1=rinv[:, 0, :], op0=ALU.mult, op1=ALU.mult))
                dve.wait_ge(gate_ready, o + 1)
                nc.vector.tensor_tensor(sq[:, 1, :], sq[:, 1, :], y[:, o % GATE_SLOTS, :], ALU.mult).then_inc(mix_f32, 1)

            def head_low(o):
                dve.wait_ge(mix_high, o + 1)
                nc.vector.tensor_tensor(a_lo[:, HEAD[o], :], sq[:, 1, :], a_hi[:, HEAD[o], :].bitcast(F32),
                                        ALU.subtract).then_inc(mix_ready, 1)

            def update_state(p):
                dve.wait_ge(kv_done, p + 1)
                kv = misc[:, 0:(NT - 1) * P].rearrange("p (c d) -> p c d", c=NT - 1)
                ch.link(nc.vector.tensor_copy(state[:, 0, :], kv[:, 0, :]))
                for cc in range(1, NT - 1):
                    ins = nc.vector.scalar_tensor_tensor(
                        out=state[:, cc, :], in0=state[:, cc - 1, :], scalar=e_last[:, p % 2, cc:cc + 1],
                        in1=kv[:, cc, :], op0=ALU.mult, op1=ALU.add)
                    if cc < NT - 2:
                        ch.link(ins)
                ins.then_inc(state_ready, 1)

            def group(o, c):
                idx = o * NT + c
                pm = tmp[:, :, :].rearrange("p a t -> p (a t)")[:, 0:PAIRS * P]
                dve.wait_ge(p_done, idx + 1)
                if idx >= 1:
                    dve.wait_ge(a_ready, idx)
                nc.vector.tensor_tensor(pm, pp[idx % 2][:, 0:PAIRS, :].rearrange("p l t -> p (l t)"),
                                        masks[:, :, :].rearrange("p l t -> p (l t)"), ALU.mult).then_inc(p_read, 1)
                dve.wait_ge(p_read, idx + 1)
                nc.vector.tensor_reduce(a_sb[:, idx % 4, :], pm.rearrange("p (l t) -> p t l", l=PAIRS),
                                        AX_X, ALU.add).then_inc(a_ready, 1)
                if c == 2 and FIRST[PACK_OF[o]] == o:
                    update_state(PACK_OF[o])

            for i, (tile, col, items, groups, end) in enumerate(SLOTS):
                if tile is not None:
                    if tile[0] in "fg":
                        clamp(*tile)
                    if col is not None:
                        wait_tile(dve, tile_no[tile])
                        pump(unit_no[tile])
                    evacuate(*tile)
                for o in MIXES[i]:
                    head_gate(o)
                for p, lv in items:
                    decayed(p, lv)
                if end is not None:
                    cumulate(end)
                for o in MIXES[i]:
                    head_low(o)
                for o, c in groups:
                    group(o, c)

            def linear_out(name, j):
                for m in range(KD):
                    n = tile_no[(name, m)]
                    wait_tile(dve, n)
                    nc.vector.tensor_copy(y[:, m, :], bank[n % 2][:, :]).then_inc(y_ready[j], 1)
                    pump(unit_no[(name, m)])
                    if name == "eo":
                        n = tile_no[("x2", m)]
                        wait_tile(dve, n)
                        nc.vector.tensor_copy(xT[:, m, :], bank[n % 2][:, :]).then_inc(x2_ready, 1)

            def mlp(layer, j):
                n0, u0 = tile_no[("mlp", layer, 0, 0)], unit_no[("mlp", layer, 0, 0)]
                nc.vector.memset(y[:, :, :], 0.0).then_inc(y_zero[layer], 1)
                dve.wait_ge(y_zero[layer], 1)

                def group(i, last):
                    for m in range(2 * KD):
                        n = n0 + m
                        if m < KD:
                            dve.wait_ge(relu_ready[layer], m + 1 + KD * i)
                            if m >= 2:
                                dve.wait_ge(hid_ready[layer], m - 1 + KD * i)
                            nc.vector.tensor_tensor(tmp[:, m % 2, :], sq[:, m % 2, :], bank[n % 2][:, :],
                                                    ALU.mult).then_inc(hid_f32[layer], 1)
                        else:
                            wait_tile(dve, n, i)
                            nc.vector.tensor_tensor(y[:, m - KD, :], y[:, m - KD, :], bank[n % 2][:, :],
                                                    ALU.add).then_inc(y_ready[j], 1)
                        if not last or m < 2 * KD - AHEAD_LO or layer == 0:
                            pump(u0 + m, i)
                        if m < KD:
                            dve.wait_ge(hid_high[layer], m + 1 + KD * i)
                            nc.vector.tensor_tensor(a_lo[:, m, :], tmp[:, m % 2, :], a_hi[:, m, :].bitcast(F32),
                                                    ALU.subtract).then_inc(hid_ready[layer], 1)

                with dve.Fori(0, GROUPS - 1) as i:
                    group(i, False)
                group(GROUPS - 1, True)

            linear_out("eo", 1)
            dve.wait_ge(x2_ready, KD)
            post_norm(1, 0, 1)
            pre_norm(2, 0, 2, KD)
            mlp(0, 3)
            post_norm(3, 0, 3)
            pre_norm(4, 1, 0, 2 * KD)

            dve.wait_ge(pos_in, 16)
            ch.link(nc.vector.tensor_copy(ang[:, :], pos_i))
            ch.link(nc.vector.tensor_scalar(ang[:, :], ang[:, :], ropec[:, 0:1], None, ALU.mult))
            for dst, turn in ((sind, 0.0), (cosd, 0.25)):
                n_, r_ = tmp[:, 0, :], dst[:, :]
                ch.link(nc.vector.tensor_scalar(n_, ang[:, :], 0.15915494309189535, turn, ALU.mult, ALU.add))
                ch.link(nc.vector.tensor_scalar(n_, n_, MAGIC, None, ALU.add))
                ch.link(nc.vector.tensor_scalar(n_, n_, MAGIC, None, ALU.subtract))
                ch.link(nc.vector.scalar_tensor_tensor(out=r_, in0=n_, scalar=-TWO_PI_A, in1=ang[:, :],
                                                       op0=ALU.mult, op1=ALU.add))
                ch.link(nc.vector.scalar_tensor_tensor(out=r_, in0=n_, scalar=-TWO_PI_B, in1=r_,
                                                       op0=ALU.mult, op1=ALU.add))
                ch.link(nc.vector.scalar_tensor_tensor(out=r_, in0=n_, scalar=-TWO_PI_C, in1=r_,
                                                       op0=ALU.mult, op1=ALU.add))
                ch.link(nc.vector.tensor_scalar(r_, r_, turn * 6.283185307179586, None, ALU.add))
                ins = nc.vector.tensor_scalar(r_, r_, PI_IN, -PI_IN, ALU.min, ALU.max)
                if turn == 0.0:
                    ch.link(ins)
            ins.then_inc(sin_arg, 1)

            for m in range(5):
                wait_tile(dve, tile_no[("oi", m)])
                pump(unit_no[("oi", m)])
            def latents():
                order = ((3, V_KVN, 1), (4, V_KVN + 1, 1), (0, V_QN, 0), (1, V_QN + 1, 0), (2, V_QN + 2, 0))
                for j in range(6):
                    if 2 <= j < 5:
                        dve.wait_ge(h_ready, 3 * KD + j - 1)
                    if j < 5:
                        k, g, slot = order[j]
                        dve.wait_ge(r_ready[8], 1 if slot == 1 else 2)
                        nc.vector.scalar_tensor_tensor(out=tmp[:, j % 2, :], in0=y[:, k, :], scalar=vec[:, g:g + 1],
                                                       in1=rinv[:, slot, :], op0=ALU.mult, op1=ALU.mult).then_inc(h_f32, 1)
                    if j >= 1:
                        k = order[j - 1][0]
                        dve.wait_ge(h_high, 3 * KD + j)
                        nc.vector.tensor_tensor(h_lo[:, k, :], tmp[:, (j - 1) % 2, :], h_hi[:, k, :].bitcast(F32),
                                                ALU.subtract).then_inc(h_ready, 1)

            def rotate(n_plain, n_swapped, scale, dst, ready, done):
                wait_tile(dve, n_plain)
                nc.vector.scalar_tensor_tensor(out=dst, in0=bank[n_plain % 2][:, :], scalar=scale, in1=cosd[:, :],
                                               op0=ALU.mult, op1=ALU.mult).then_inc(rot_read, 1)
                wait_tile(dve, n_swapped)
                if done:
                    dve.wait_ge(ready, done)
                nc.vector.scalar_tensor_tensor(out=ang[:, :], in0=bank[n_swapped % 2][:, :], scalar=scale, in1=sind[:, :],
                                               op0=ALU.mult, op1=ALU.mult).then_inc(rot_read, 1)
                wait_read(dve, n_swapped)
                nc.vector.tensor_tensor(dst, dst, ang[:, :], ALU.add).then_inc(ready, 1)

            for m in (5, 6):
                n = tile_no[("oi", m)]
                wait_tile(dve, n)
                nc.vector.tensor_copy(qn[:, 1, m - 5, :], bank[n % 2][:, :]).then_inc(kr_read, 1)
                pump(unit_no[("oi", m)])
            latents()
            dve.wait_ge(sin_ready, 2)
            ch.link(nc.vector.tensor_scalar(sind[:, :], sind[:, :], ropec[:, 1:2], None, ALU.mult))
            ch.link(nc.vector.tensor_tensor(kr[:, :], qn[:, 1, 0, :], cosd[:, :], ALU.mult))
            ch.link(nc.vector.tensor_tensor(ang[:, :], qn[:, 1, 1, :], sind[:, :], ALU.mult))
            nc.vector.tensor_tensor(kr[:, :], kr[:, :], ang[:, :], ALU.add).then_inc(rope_ready, 1)
            for what in ("mv", "mk"):
                for g in range(2):
                    wait_tile(dve, tile_no[(what, g, 3)])
                    pump(unit_no[(what, g)])

            def q_evacuate(a):
                wait_tile(dve, tile_no[("qn", a, 1)])
                pump(unit_no[("qn", a)])
                rotate(tile_no[("qr", a, 0)], tile_no[("qr", a, 1)], SCALE, qr[:, a % 2, :], qr_ready, a)
                pump(unit_no[("qr", a)])

            def att_out(h):
                dve.wait_ge(att_high, h + 1)
                nc.vector.tensor_tensor(a_lo[:, h, :], po[:, :], a_hi[:, h, :].bitcast(F32),
                                        ALU.subtract).then_inc(att_ready, 1)

            dve.wait_ge(rope_ready, 1)
            q_evacuate(0)
            for j in range(4 * MLA_HEADS + 2):
                if j % 8 == 0 and j // 8 + 1 < MLA_HEADS // 2:
                    q_evacuate(j // 8 + 1)
                if j < 4 * MLA_HEADS:
                    width = (j % 4 + 1) * P
                    dve.wait_ge(s_done, j + 1)
                    nc.vector.tensor_reduce(stat[:, 0, j:j + 1], s_bank[j % 3][:, 0:width], AX_X, ALU.max,
                                            negate=True).then_inc(nmax_ready, 1)
                if 1 <= j <= 4 * MLA_HEADS:
                    i = j - 1
                    width = (i % 4 + 1) * P
                    dve.wait_ge(prob_exp, i + 1)
                    ch.link(nc.vector.reciprocal(stat[:, 2, i:i + 1], stat[:, 1, i:i + 1]))
                    nc.vector.tensor_scalar(prob[:, i % 3, 0:width], prob[:, i % 3, 0:width], stat[:, 2, i:i + 1], None,
                                            ALU.mult).then_inc(prob_ready, 1)
                if j >= 2:
                    i = j - 2
                    qb = i % 4
                    dve.wait_ge(pt_done, i + 1)
                    nc.vector.tensor_copy(p_t[:, 0:qb + 1, qb * P:(qb + 1) * P],
                                          t_bank[i % 2][:, 0:qb + 1, :]).then_inc(pt_ready, 1)
                if j >= 6 and j % 4 == 2:
                    att_out(j // 4 - 1)
            att_out(MLA_HEADS - 1)
            linear_out("oo", 5)
            post_norm(5, 1, 1)
            pre_norm(6, 1, 2, 3 * KD + 5)
            mlp(1, 7)
            post_norm(7, 1, 3)
            for m in range(2 * NT):
                n = tile_no[("out", m)]
                wait_tile(dve, n)
                nc.vector.tensor_copy(y[:, m, :], bank[n % 2][:, :]).then_inc(out_ready, 1)

        @block.tensor
        def _(pe):
            def mm3(dst, wh, wl, xh, xl_, first, last):
                nc.tensor.matmul(dst, wh, xl_, start=first, stop=False)
                nc.tensor.matmul(dst, wl, xh, start=False, stop=False)
                return nc.tensor.matmul(dst, wh, xh, start=False, stop=last)

            def slot(u, cols):
                n = unit_size(u)
                return (w_hi[:, u % SPLIT, 0:n].rearrange("p (k c) -> p k c", c=cols),
                        w_lo[:, u % SPLIT, 0:n].rearrange("p (k c) -> p k c", c=cols))

            def feature_tile(u, n, src_hi, src_lo, ready=None, base=0, i=None, kt=KD, k0=0, cols=P, c0=0, width=P, order=None):
                wh, wl = slot(u, cols)
                pe.wait_ge(lo_ready, u + 1 + (0 if i is None else 16 * (i - 1)))
                wait_bank(pe, n, i)
                for j, k in enumerate(order or range(kt)):
                    if ready is not None:
                        pe.wait_ge(ready, base + j + 1)
                    c = slice(c0, c0 + width)
                    ins = mm3(bank[n % 2][0:width, :], wh[:, k, c], wl[:, k, c], src_hi[:, k0 + k, :],
                              src_lo[:, k0 + k, :], j == 0, j == kt - 1)
                ins.then_inc(tile_done, 1)

            def sum_squares(j, k, total=KD, dst=misc, first=None, last=None):
                pe.wait_ge(sq_ready[j], k + 1)
                nc.tensor.matmul(dst[:, :], ones[:, :], sq[:, k % 2, :], start=(k == 0 if first is None else first),
                                 stop=(k == total - 1 if last is None else last)).then_inc(sq_used[j], 1)

            def norm_sums(j):
                for k in range(KD):
                    sum_squares(j, k)

            pe.wait_ge(consts_ready, 4)
            pe.wait_ge(vec_in, 16 * 9)
            nc.tensor.transpose(misc[:, 0:V_ROWS], vrows[:, :], ident[0:V_ROWS, 0:V_ROWS]).then_inc(vec_done, 1)
            for k in range(KD):
                n = tile_no[("x", k)]
                pe.wait_ge(x_in[k // 2], 16)
                wait_bank(pe, n)
                for t in range(NT):
                    ins = nc.tensor.transpose(bank[n % 2][:, t * P:(t + 1) * P], x_tok[:, t, k * P:(k + 1) * P], ident[:, :])
                ins.then_inc(tile_done, 1)
            pe.wait_ge(vec_ready, 1)
            norm_sums(0)

            n, u = tile_no[("ga", 0)], unit_no[("ga", 0)]
            feature_tile(u, n, h_hi, h_lo, h_ready, 0, cols=GATE_RANK, width=GATE_RANK)

            def project(tile, col):
                n = tile_no[tile]
                what, i = tile
                if what == "z":
                    pe.wait_ge(ga_ready, 1)
                    wait_bank(pe, n)
                    nc.tensor.matmul(bank[n % 2][:, :], w_gate[:, i * P:(i + 1) * P], ga_t[:, :], start=True,
                                     stop=True).then_inc(tile_done, 1)
                    return
                if what == "w":
                    pe.wait_ge(v_raw, i + 1)
                    wait_bank(pe, n)
                    for t in range(NT):
                        ins = nc.tensor.transpose(bank[n % 2][:, t * P:(t + 1) * P],
                                                  vbuf[:, i % 4, t * P:(t + 1) * P], ident[:, :])
                    ins.then_inc(tile_done, 1)
                    return
                feature_tile(unit_no[tile], n, h_hi, h_lo)

            def head_rows(o):
                w_ = P if HEAD[o] < 4 else GLA_DK
                first = (o - FIRST[PACK_OF[o]]) * w_
                return slice(first, first + w_)

            def pairs(o, c):
                p, idx, r, s = PACK_OF[o], o * NT + c, head_rows(o), slice(c * P, (c + 1) * P)
                pe.wait_ge(xl_ready, (p + 1) * (LEVELS + 2))
                if idx >= 2:
                    pe.wait_ge(p_read, idx - 1)
                else:
                    pe.wait_ge(p_zero, idx + 1)
                for lv in range(2):
                    L = 64 >> lv
                    for b in range(0, P, 2 * L):
                        nc.tensor.matmul(pp[idx % 2][b:b + L, 0, b + L:b + 2 * L], xls[p % 2][r, lv, c * P + b:c * P + b + L],
                                         xls[p % 2][r, lv, c * P + b + L:c * P + b + 2 * L], start=True, stop=True)
                for lv in range(2, LEVELS):
                    nc.tensor.matmul(pp[idx % 2][:, lv - 1, :], xls[p % 2][r, lv, s], xls[p % 2][r, lv, s],
                                     start=True, stop=True)
                nc.tensor.matmul(pp[idx % 2][:, PAIRS - 1, :], ks[p % 3][r, s], qs[p % 3][r, s], start=True,
                                 stop=True).then_inc(p_done, 1)

            def outputs(o, c):
                p, idx, r, s = PACK_OF[o], o * NT + c, head_rows(o), slice(c * P, (c + 1) * P)
                if c == 0:
                    pe.wait_ge(v_ready, o + 1)
                    if o >= 1:
                        pe.wait_ge(o_read, o)
                pe.wait_ge(a_ready, idx + 1)
                ins = nc.tensor.matmul(po[:, s], vbuf[:, o % 4, s], a_sb[:, idx % 4, :], start=True, stop=(c == 0))
                if c >= 1:
                    pe.wait_ge(state_ready, p + 1)
                    ins = nc.tensor.matmul(po[:, s], state[r, c - 1, :], qes[p % 2][r, s], start=False, stop=True)
                if c == NT - 1:
                    ins.then_inc(o_done, 1)

            misc_read = []

            def head_sum(o):
                pe.wait_ge(o_sq, o + 1)
                pe.wait_ge(*misc_read[-1])
                misc_read.append((o_rinv, o + 1))
                nc.tensor.matmul(misc[:, :], ones[:, :], sq[:, 0, :], start=True, stop=True).then_inc(o_sum, 1)

            def transpose_keys(p):
                pe.wait_ge(xl_ready, (p + 1) * (LEVELS + 2))
                if misc_read:
                    pe.wait_ge(*misc_read[-1])
                misc_read.append((ket_ready, p + 1))
                for c in range(NT - 1):
                    ins = nc.tensor.transpose(misc[:, c * P:(c + 1) * P], ke[:, c * P:(c + 1) * P], ident[:, :])
                ins.then_inc(ket_done, 1)

            def chunk_states(p):
                heads = [o for o in range(8) if PACK_OF[o] == p]
                pe.wait_ge(ket_ready, p + 1)
                pe.wait_ge(v_ready, heads[-1] + 1)
                pe.wait_ge(*misc_read[-1])
                misc_read.append((state_ready, p + 1))
                for c in range(NT - 1):
                    s = slice(c * P, (c + 1) * P)
                    for o in heads:
                        r = head_rows(o)
                        ins = nc.tensor.matmul(misc[r, s], ke_t[:, c, r], vbuf[:, o % 4, s], start=True, stop=True)
                ins.then_inc(kv_done, 1)

            for i, (tile, col, items, groups, end) in enumerate(SLOTS):
                if tile is not None:
                    project(tile, col)
                for o, c in OUTPUTS[i]:
                    outputs(o, c)
                for o in SUMS[i]:
                    head_sum(o)
                for o, c in groups:
                    first = FIRST[PACK_OF[o]] == o
                    if c == 0 and first:
                        transpose_keys(PACK_OF[o])
                    pairs(o, c)
                    if c == 2 and first:
                        chunk_states(PACK_OF[o])

            def linear_out(name, j, ready):
                for m in range(KD):
                    feature_tile(unit_no[(name, m)], tile_no[(name, m)], a_hi, a_lo, ready if m == 0 else None,
                                 order=HEAD if name == "eo" else None)
                    if m >= 1:
                        sum_squares(j, m - 1)
                    if name == "eo":
                        n = tile_no[("x2", m)]
                        pe.wait_ge(x_again, 16)
                        wait_bank(pe, n)
                        for t in range(NT):
                            ins = nc.tensor.transpose(bank[n % 2][:, t * P:(t + 1) * P],
                                                      x_tok[:, t, m * P:(m + 1) * P], ident[:, :])
                        ins.then_inc(tile_done, 1)
                sum_squares(j, KD - 1)

            def mlp(layer, j, hs):
                n0, u0 = tile_no[("mlp", layer, 0, 0)], unit_no[("mlp", layer, 0, 0)]

                def group(g, i=None, last=False):
                    n, u = n0 + 2 * KD * g, u0 + 2 * KD * g
                    for m in range(KD):
                        feature_tile(u + m, n + m, h_hi, h_lo, h_ready if g == 0 and m == 0 else None, hs, i)
                    for m in range(KD, 2 * KD):
                        ready = hid_ready[layer] if m == KD else None
                        feature_tile(u + m, n + m, a_hi, a_lo, ready, KD * (g if i is None else i), i)
                        if last and m > KD:
                            sum_squares(j, m - KD - 1)

                group(0)
                with pe.Fori(1, GROUPS - 1) as i:
                    group(1, i)
                group(GROUPS - 1, last=True)
                sum_squares(j, KD - 1)

            linear_out("eo", 1, mix_ready)
            pe.wait_ge(r_ready[1], 1)
            norm_sums(2)
            mlp(0, 3, KD)
            pe.wait_ge(r_ready[3], 1)
            norm_sums(4)

            for m in range(7):
                feature_tile(unit_no[("oi", m)], tile_no[("oi", m)], h_hi, h_lo, h_ready if m == 0 else None, 2 * KD)
                if m == 1:
                    pe.wait_ge(r_ready[4], 1)
                if 1 <= m <= 3:
                    sum_squares(8, m - 1, first=m == 1, last=m == 3)
                elif 4 <= m <= 5:
                    sum_squares(8, m - 1, dst=po, first=m == 4, last=m == 5)
            for g in range(2):
                u = unit_no[("mv", g)]
                wh, wl = slot(u, T)
                pe.wait_ge(lo_ready, u + 1)
                for t in range(NT):
                    n = tile_no[("mv", g, t)]
                    s = slice(t * P, (t + 1) * P)
                    wait_bank(pe, n)
                    for k in range(KV_RANK_T):
                        pe.wait_ge(h_ready, 3 * KD + k + 1)
                        ins = mm3(bank[n % 2][:, :], h_hi[:, 3 + k, s], h_lo[:, 3 + k, s], wh[:, k, :], wl[:, k, :],
                                  k == 0, k == KV_RANK_T - 1)
                    ins.then_inc(tile_done, 1)
            for g in range(2):
                for j in range(4):
                    feature_tile(unit_no[("mk", g)], tile_no[("mk", g, j)], h_hi, h_lo, kt=KV_RANK_T, k0=3, cols=T, c0=j * P)

            def project_q(a):
                for what in ("qn", "qr"):
                    for hh in range(2):
                        feature_tile(unit_no[(what, a)], tile_no[(what, a, hh)], h_hi, h_lo,
                                     h_ready if a == 0 else None, 3 * KD + 2, kt=Q_RANK_T, cols=2 * P, c0=hh * P)

            def scores(j):
                h, qb = divmod(j, 4)
                a, hh = divmod(h, 2)
                s = slice(qb * P, (qb + 1) * P)
                r = slice(hh * ROPE, (hh + 1) * ROPE)
                width = (qb + 1) * P
                dst = s_bank[j % 3]
                if j >= 3:
                    pe.wait_ge(prob_exp, j - 2)
                if qb == 0 and hh == 0:
                    pe.wait_ge(qr_ready, a + 1)
                    wait_read(pe, tile_no[("qn", a, 1)])
                nc.tensor.matmul(dst[:, 0:width], qr[r, a % 2, s], kr[r, 0:width], start=True, stop=False)
                nc.tensor.matmul(dst[:, 0:width], qn[:, a % 2, hh, s], y[:, h, 0:width], start=False, stop=False)
                nc.tensor.matmul(dst[:, width - P:width], mask_q[:, :], mask_k[:, :], start=False,
                                 stop=True).then_inc(s_done, 1)

            def transposes(j):
                pe.wait_ge(prob_ready, j + 1)
                if j >= 2:
                    pe.wait_ge(pt_ready, j - 1)
                for kb in range(j % 4 + 1):
                    ins = nc.tensor.transpose(t_bank[j % 2][:, kb, :], prob[:, j % 3, kb * P:(kb + 1) * P], ident[:, :])
                ins.then_inc(pt_done, 1)

            def values(h):
                pe.wait_ge(pt_ready, 4 * h + 4)
                if h >= 1:
                    pe.wait_ge(att_ready, h)
                for kb in range(NT):
                    ins = nc.tensor.matmul(po[:, kb * P:T], v_tok[:, kb, h * P:(h + 1) * P], p_t[:, kb, kb * P:T],
                                           start=(kb == 0), stop=(kb == NT - 1))
                ins.then_inc(pv_done, 1)

            project_q(0)
            pe.wait_ge(consts_ready, 6)
            pe.wait_ge(rope_ready, 1)
            pe.wait_ge(r_ready[8], 2)
            for j in range(4 * MLA_HEADS + 2):
                if j % 8 == 0 and j // 8 + 1 < MLA_HEADS // 2:
                    project_q(j // 8 + 1)
                if j < 4 * MLA_HEADS:
                    scores(j)
                if j >= 6 and j % 4 == 2:
                    values(j // 4 - 1)
                if 2 <= j:
                    transposes(j - 2)
            values(MLA_HEADS - 1)
            linear_out("oo", 5, att_ready)
            pe.wait_ge(r_ready[5], 1)
            norm_sums(6)
            mlp(1, 7, 3 * KD + 5)

            for m in range(2 * NT):
                t, half = divmod(m, 2)
                n = tile_no[("out", m)]
                pe.wait_ge(x_ready, 5 * KD)
                wait_bank(pe, n)
                for k in range(4):
                    ins = nc.tensor.transpose(bank[n % 2][:, k * P:(k + 1) * P],
                                              xT[:, 4 * half + k, t * P:(t + 1) * P], ident[:, :])
                ins.then_inc(tile_done, 1)


_INS = ["x", "positions", "norm_gains", "ev_w_in", "hg_lb_table", "gla_w_gate", "gla_b_gate", "hg_out_norm",
        "gla_out_norm", "ev_w_out", "od_w_in", "mla_q_norm", "mla_w_uq", "mla_kv_norm", "mla_w_ukv", "od_w_out",
        "mlp_w1", "mlp_w2"]


def kernel(**inputs):
    import numpy as np
    import concourse.bacc as _bacc
    from concourse.bass_utils import run_bass_kernel_spmd as _run

    inv_freq = np.float32(10000.0) ** (-np.arange(0, ROPE, 2, dtype=np.float32) / np.float32(ROPE))
    sign = np.repeat(np.array([-1.0, 1.0], np.float32), ROPE // 2)
    rope_const = np.stack([np.tile(inv_freq, 4), np.tile(sign, 2)], axis=1).astype(np.float32)

    nc = _bacc.Bacc("TRN2", target_bir_lowering=False, num_devices=1)
    arrays = {f"in_{n}": np.ascontiguousarray(inputs[n]) for n in _INS}
    arrays["rope_const"] = rope_const
    args = [nc.dram_tensor(n, a.shape, mybir.dt.from_np(a.dtype), kind="ExternalInput").ap() for n, a in arrays.items()]
    out = nc.dram_tensor("out_0", (1, T, D), F32, kind="ExternalOutput").ap()
    trunk(nc, *args, out)
    r = _run(nc, [arrays], core_ids=[0])
    return r.results[0]["out_0"]
```

```python
from contextlib import ExitStack

import concourse.bass as bass
from concourse import mybir

ALU = mybir.AluOpType
ACT = mybir.ActivationFunctionType
F32 = mybir.dt.float32
F32R = mybir.dt.float32r
I32 = mybir.dt.int32
AX_X = mybir.AxisListType.X

P = 128
T = 512
D = 1024
KD = D // P
NT = T // P
F = 4 * D
GROUPS = F // D
EPS = 1e-6
EXP_MAX = -87.0
HEADS = 4
GLA_DK = 64
GATE_RANK = 16
GATE_TEMP = 16.0
LEVELS = 7
PAIRS = 7
Q_RANK_T, KV_RANK_T = 3, 2
MLA_HEADS = 8
NOPE, ROPE, VDIM = 128, 64, 128
SCALE = float(NOPE + ROPE) ** -0.5
MASKED = -1e30

HQ, HF, HI, HG, GQ, GK, GV, GR, GA = 0, 512, 1024, 1536, 2048, 2304, 2560, 3072, 3584
V_LB, V_BG, V_HGN, V_GLN, V_QN, V_KVN, V_ROWS = 64, 72, 74, 75, 76, 79, 81

STAGE, SPLIT = 2, 4
UNIT = KD * P

TWO_PI_A, TWO_PI_B, TWO_PI_C = 6.28125, 0.0019350051879882812, 3.0199159819567e-07
MAGIC = 12582912.0
PI_IN = 3.1415925


def trunk(nc, x, positions, norm_gains, ev_w_in, hg_lb_table, gla_w_gate, gla_b_gate, hg_out_norm,
          gla_out_norm, ev_w_out, od_w_in, mla_q_norm, mla_w_uq, mla_kv_norm, mla_w_ukv, od_w_out,
          mlp_w1, mlp_w2, rope_const, out):

    PACKS = [("gla", 0), ("gla", 1), ("hg", 0), ("hg", 1), ("hg", 2), ("hg", 3)]
    HEAD = [4, 5, 6, 7, 0, 1, 2, 3]
    PACK_OF = [0, 0, 1, 1, 2, 3, 4, 5]
    FIRST = [0, 2, 4, 5, 6, 7]

    def gate_col(o):
        return GR + (HEAD[o] - 4) * P if HEAD[o] >= 4 else HG + HEAD[o] * P

    def key_tiles(p):
        kind, a = PACKS[p]
        if kind == "gla":
            return [(("k", p), GK + a * P), (("q", p), GQ + a * P), (("z", p), None)]
        return [(("f", p), HF + a * P), (("q", p), HQ + a * P)]

    def value_tiles(p):
        kind, a = PACKS[p]
        return [(("v", o), (GV + (HEAD[o] - 4) * P) if kind == "gla" else HI + a * P)
                for o in range(8) if PACK_OF[o] == p]

    GATES = [(), (), (0,), (1,), (2, 3), (4,), (5, 6), (7,)]
    SLOTS = []
    late = []
    for st in range(8):
        values = value_tiles(st - 1) if 1 <= st < 7 else []
        turned = [(("w", o), None) for (_, o), _ in values]
        keys = key_tiles(st) if st < 6 else []
        gates = [(("g", o), gate_col(o)) for o in GATES[st]]
        first = (keys or gates)[:1]
        todo = values + first + turned + [t for t in gates + keys if t not in first]
        items = [(st - 1, lv) for lv in range(LEVELS + 2)] if 1 <= st < 7 else []
        groups = [(o, c) for o in range(8) if PACK_OF[o] == st - 2 for c in range(NT)] if st >= 2 else []
        if st == 7:
            todo += [(None, None)] * 2
        long_ = [i for i, (tile, col) in enumerate(todo) if col is not None or tile is None]
        n = len(long_)
        shares = [late] + [groups[a * len(groups) // n:(a + 1) * len(groups) // n] for a in range(n)]
        late = shares.pop()
        for i, (tile, col) in enumerate(todo):
            a = long_.index(i) if i in long_ else None
            its = [] if not a else items[(a - 1) * len(items) // (n - 1):a * len(items) // (n - 1)]
            SLOTS.append((tile, col, its, [] if a is None else shares[a],
                          st if i == len(todo) - 1 and st < 6 else None))
    SLOTS += [(None, None, [], late, None)] + [(None, None, [], [], None)] * 5
    OUTPUTS, SQUARES, SUMS, MIXES = [[[] for _ in SLOTS] for _ in range(4)]
    pending = [[], []]
    for i, (tile, col, _, groups, _) in enumerate(SLOTS):
        if col is not None or tile is None:
            OUTPUTS[i] = pending[0]
            pending = [pending[1], groups]
            for o, c in OUTPUTS[i]:
                if c == NT - 1:
                    SQUARES[i].append(o)
    square_slot = [i for i in range(len(SLOTS)) for _ in SQUARES[i]] + [len(SLOTS) - 2]
    for o in range(8):
        gap = min(square_slot[o + 1] - square_slot[o], 3)
        MIXES[square_slot[o] + gap].append(o)
        SUMS[square_slot[o] + gap - 1].append(o)

    def rows(w, c0, c1):
        return w[:, c0:c1].rearrange("(k p) c -> p k c", p=P)

    units = []
    tile_of_unit = []
    tile_no = {}
    unit_no = {}

    def add_tile(name, unit=None):
        tile_no[name] = len(tile_no)
        if unit is not None:
            tile_of_unit[unit] = tile_no[name]

    def add_unit(name, loads):
        unit_no[name] = len(units)
        units.append(loads)
        tile_of_unit.append(None)
        return unit_no[name]

    for k in range(KD):
        add_tile(("x", k))
    w = ev_w_in[0]
    add_tile(("ga", 0), add_unit(("ga", 0), [((KD, GATE_RANK), 0, GATE_RANK, rows(w, GA, GA + GATE_RANK))]))
    for tile, col, *_ in SLOTS:
        if tile is not None:
            add_tile(tile, None if col is None else add_unit(tile, [((KD, P), 0, P, rows(w, col, col + P))]))
    for m in range(KD):
        add_tile(("eo", m), add_unit(("eo", m), [((KD, P), 0, P, rows(ev_w_out[0], m * P, (m + 1) * P))]))
        if m >= 1:
            add_tile(("x2", m - 1))
    add_tile(("x2", KD - 1))

    def add_mlp(layer):
        for g in range(GROUPS):
            for m in range(2 * KD):
                add_tile(("mlp", layer, g, m), add_unit(("mlp", layer, g, m), None))

    add_mlp(0)
    w = od_w_in[0]
    LATENTS = [3, 4, 0, 1, 2]
    for m in LATENTS:
        add_tile(("oi", m), add_unit(("oi", m), [((KD, P), 0, P, rows(w, m * P, (m + 1) * P))]))
    R0, RH = 5 * P, ROPE // 2
    add_tile(("oi", 5), add_unit(("oi", 5), [((KD, P), c, c + ROPE, rows(w, R0, R0 + ROPE)) for c in (0, ROPE)]))
    add_tile(("oi", 6), add_unit(("oi", 6), [((KD, P), c + d, c + d + RH, rows(w, R0 + RH - d, R0 + 2 * RH - d))
                                             for c in (0, ROPE) for d in (0, RH)]))
    w = mla_w_ukv[0].rearrange("(k p) (h c) -> k p h c", p=P, c=NOPE + VDIM)
    for what, c0 in (("mv", NOPE), ("mk", 0)):
        for g in range(2):
            u = add_unit((what, g), [((KV_RANK_T, 4 * P), None, k, w[k, :, 4 * g:4 * g + 4, c0:c0 + P])
                                     for k in range(KV_RANK_T)])
            for j in range(4):
                add_tile((what, g, j), u)
    w = mla_w_uq[0]
    for a in range(MLA_HEADS // 2):
        c = 2 * a * (NOPE + ROPE)
        u = add_unit(("qn", a), [((Q_RANK_T, 2 * P), hh * P, (hh + 1) * P, rows(w, c + hh * 192, c + hh * 192 + NOPE))
                                 for hh in range(2)])
        add_tile(("qn", a, 0), u)
        add_tile(("qn", a, 1), u)
        loads = [((Q_RANK_T, 2 * P), hh * ROPE, (hh + 1) * ROPE, rows(w, c + hh * 192 + NOPE, c + (hh + 1) * 192))
                 for hh in range(2)]
        for hh in range(2):
            r0 = c + hh * 192 + NOPE
            loads += [((Q_RANK_T, 2 * P), P + hh * ROPE + d, P + hh * ROPE + d + RH,
                       rows(w, r0 + RH - d, r0 + 2 * RH - d)) for d in (0, RH)]
        u = add_unit(("qr", a), loads)
        add_tile(("qr", a, 0), u)
        add_tile(("qr", a, 1), u)
    for m in range(KD):
        add_tile(("oo", m), add_unit(("oo", m), [((KD, P), 0, P, rows(od_w_out[0], m * P, (m + 1) * P))]))
    add_mlp(1)
    for m in range(2 * NT):
        add_tile(("out", m))
    n_units = len(units)
    loaded = []
    for u, loads in enumerate(units):
        loaded.append((loaded[u - STAGE] if u >= STAGE else 0) + 16 * (1 if loads is None else len(loads)))

    def unit_size(u):
        return UNIT if units[u] is None else units[u][0][0][0] * units[u][0][0][1]

    with ExitStack() as ctx:
        def sb(name, shape, dt=F32, scope=ctx):
            return scope.enter_context(nc.sbuf_tensor(name, shape, dt))

        def sem(name):
            return ctx.enter_context(nc.semaphore(name))

        xT = sb("xT", [P, KD, T])
        h_hi = sb("h_hi", [P, KD, T], F32R)
        h_lo = sb("h_lo", [P, KD, T], F32R)
        a_hi = sb("a_hi", [P, KD, T], F32R)
        a_lo = sb("a_lo", [P, KD, T], F32R)
        y = sb("y", [P, KD, T])
        stage = sb("stage", [P, STAGE, UNIT])
        w_hi = sb("w_hi", [P, SPLIT, UNIT], F32R)
        w_lo = sb("w_lo", [P, SPLIT, UNIT], F32R)
        ident = sb("ident", [P, P])
        ones = sb("ones", [P, P])
        eps = sb("eps", [P, 1])
        masks = sb("masks", [P, PAIRS, P])
        vec = sb("vec", [P, V_ROWS])
        lbt = sb("lbt", [P, 6, HEADS])
        w_gate = sb("w_gate", [GATE_RANK, HEADS * GLA_DK])
        ropec = sb("ropec", [P, 2])
        sq = sb("sq", [P, 2, T])
        tmp = sb("tmp", [P, 2, T])
        rinv = sb("rinv", [P, 2, T])

        with ExitStack() as s1:
            x_tok = sb("x_tok", [P, NT, D], F32, s1)
            vrows = sb("vrows", [V_ROWS, P], F32, s1)
        with ExitStack() as s2:
            vbuf = sb("vbuf", [P, 4, T], F32, s2)
            xl = sb("xl", [P, LEVELS, T], F32, s2)
            dec = sb("dec", [P, 3, T], F32, s2)
            q_sb = sb("q_sb", [P, 2, T], F32, s2)
            k_sb = sb("k_sb", [P, 2, T], F32, s2)
            b_sb = sb("b_sb", [P, T], F32, s2)
            qe0 = sb("qe", [P, T], F32, s2)
            ke = sb("ke", [P, T], F32, s2)
            e_last = sb("e_last", [P, 2, NT], F32, s2)
            a_sb = sb("a_sb", [P, 4, P], F32, s2)
            ke_t = sb("ke_t", [P, NT - 1, P], F32, s2)
            state = sb("state", [P, NT - 1, P], F32, s2)
            t_f = sb("t_f", [P, T], F32, s2)
            t_g = sb("t_g", [P, T], F32, s2)
            ga_t = sb("ga_t", [GATE_RANK, T], F32, s2)
        with ExitStack() as s3:
            v_tok = sb("v_tok", [P, NT, D], F32, s3)
            kr = sb("kr", [P, T], F32, s3)
            cosd = sb("cosd", [P, T], F32, s3)
            sind = sb("sind", [P, T], F32, s3)
            ang = sb("ang", [P, T], F32, s3)
            qn = sb("qn", [P, 2, 2, T], F32, s3)
            qr = sb("qr", [P, 2, T], F32, s3)
            prob = sb("prob", [P, 3, T], F32, s3)
            p_t = sb("p_t", [P, NT, T], F32, s3)
            pos_i = p_t[:, 0, :].bitcast(I32)
            mask_q = sb("mask_q", [P, P], F32, s3)
            mask_k = sb("mask_k", [P, P], F32, s3)
            stat = sb("stat", [P, 3, 4 * MLA_HEADS], F32, s3)

        xls = [xl[:, :, :], xT[:, 0:LEVELS, :]]
        qes = [qe0[:, :], xT[:, LEVELS, :]]
        qs = [q_sb[:, 0, :], q_sb[:, 1, :], y[:, 6, :]]
        ks = [k_sb[:, 0, :], k_sb[:, 1, :], y[:, 7, :]]
        GATE_SLOTS = 6
        acc, squares = qn[:, 0, 0, :], [qn[:, 1, 0, :], qn[:, 0, 1, :]]
        ms_in, eps_in, r_in = prob[:, 2, :], prob[:, 0, :], prob[:, 1, :]

        bank = [ctx.enter_context(nc.psum_tensor(f"bank{b}", [P, T], F32)) for b in range(2)]
        pp = [ctx.enter_context(nc.psum_tensor(f"pp{b}", [P, 8, P], F32)) for b in range(2)]
        po = ctx.enter_context(nc.psum_tensor("po", [P, T], F32))
        misc = ctx.enter_context(nc.psum_tensor("misc", [P, T], F32))
        s_bank = [pp[0][:, 0:4, :], pp[0][:, 4:8, :], pp[1][:, 0:4, :]]
        s_bank = [v.rearrange("p a b -> p (a b)") for v in s_bank]
        t_bank = [pp[1][:, 4:8, :], misc[:, :].rearrange("p (a b) -> p a b", a=4)]

        x_in = [sem(f"x_in{i}") for i in range(4)]
        vec_in, consts_ready, vec_done = sem("vec_in"), sem("consts_ready"), sem("vec_done")
        vec_ready, pos_in, out_stored = sem("vec_ready"), sem("pos_in"), sem("out_stored")
        stage_in = [sem(f"stage_in{s}") for s in range(STAGE)]
        hi_ready, lo_ready = sem("hi_ready"), sem("lo_ready")
        tile_done = sem("tile_done")
        act_chain, dve_chain, pool_chain = sem("act_chain"), sem("dve_chain"), sem("pool_chain")
        x_ready = sem("x_ready")
        y_ready = {j: sem(f"y_ready{j}") for j in (1, 3, 5, 7)}
        sum_done = [sem(f"sum_done{j}") for j in range(8)]
        x_odd = sem("x_odd")
        ms_ready, y_scaled, x_new, sq_x = sem("ms_ready"), sem("y_scaled"), sem("x_new"), sem("sq_x")
        sq_ready = [sem(f"sq_ready{j}") for j in range(9)]
        sq_used = [sem(f"sq_used{j}") for j in range(9)]
        r_ready = [sem(f"r_ready{j}") for j in range(9)]
        h_f32, h_high, h_ready = sem("h_f32"), sem("h_high"), sem("h_ready")
        f_sig, f_gate, f_log, b_ready = sem("f_sig"), sem("f_gate"), sem("f_log"), sem("b_ready")
        g_sig, gate_ready, q_ready, k_ready = sem("g_sig"), sem("gate_ready"), sem("q_ready"), sem("k_ready")
        v_ready, ga_ready, d_ready, e_ready = sem("v_ready"), sem("ga_ready"), sem("d_ready"), sem("e_ready")
        xl_ready, ket_done, ket_ready = sem("xl_ready"), sem("ket_done"), sem("ket_ready")
        kv_done, state_ready, p_done, p_read = sem("kv_done"), sem("state_ready"), sem("p_done"), sem("p_read")
        a_ready, o_done, o_sq, o_sum = sem("a_ready"), sem("o_done"), sem("o_sq"), sem("o_sum")
        o_rinv, o_read, mix_f32, mix_high, mix_ready = (sem("o_rinv"), sem("o_read"), sem("mix_f32"),
                                                        sem("mix_high"), sem("mix_ready"))
        c_ready, rope_ready, vt_ready, kt_ready = sem("c_ready"), sem("rope_ready"), sem("vt_ready"), sem("kt_ready")
        sin_arg, sin_ready, qn_ready, qr_ready = sem("sin_arg"), sem("sin_ready"), sem("qn_ready"), sem("qr_ready")
        s_done, nmax_ready, prob_exp, prob_ready = sem("s_done"), sem("nmax_ready"), sem("prob_exp"), sem("prob_ready")
        pt_done, pt_ready, pv_done, att_high, att_ready = (sem("pt_done"), sem("pt_ready"), sem("pv_done"),
                                                           sem("att_high"), sem("att_ready"))
        relu_ready = [sem(f"relu_ready{l}") for l in range(2)]
        hid_f32 = [sem(f"hid_f32_{l}") for l in range(2)]
        hid_high = [sem(f"hid_high{l}") for l in range(2)]
        hid_ready = [sem(f"hid_ready{l}") for l in range(2)]
        y_zero = [sem(f"y_zero{l}") for l in range(2)]
        x_again, x2_ready = sem("x_again"), sem("x2_ready")
        v_raw, p_zero, f_clamped, g_clamped = sem("v_raw"), sem("p_zero"), sem("f_clamped"), sem("g_clamped")
        z_read, kr_read, rot_read = sem("z_read"), sem("kr_read"), sem("rot_read")
        out_ready = sem("out_ready")

        read = {}

        def says(name, s, value):
            read[tile_no[name]] = (s, value)

        for k in range(KD):
            says(("x", k), x_ready, k + 1)
            says(("eo", k), y_ready[1], k + 1)
            says(("oo", k), y_ready[5], k + 1)
            says(("out", k), out_ready, k + 1)
            for layer, j in ((0, 3), (1, 7)):
                for g in range(GROUPS):
                    says(("mlp", layer, g, k), hid_f32[layer], g * KD + k + 1)
                    says(("mlp", layer, g, KD + k), y_ready[j], g * KD + k + 1)
            if k < 7:
                says(("oi", k), c_ready if k < 5 else kr_read, LATENTS.index(k) + 1 if k < 5 else k - 4)
            says(("mv", k // 4, k % 4), vt_ready, k + 1)
            says(("mk", k // 4, k % 4), kt_ready, k + 1)
            says(("qn", k // 2, k % 2), qn_ready, k + 1)
            says(("qr", k // 2, k % 2), rot_read, k + 1)
        says(("ga", 0), ga_ready, 1)
        for (what, i) in [t for t, *_ in SLOTS if t is not None]:
            says((what, i), *{"f": (f_clamped, i - 1), "g": (gate_ready, i + 1), "q": (q_ready, i + 1),
                              "k": (k_ready, i + 1), "z": (z_read, i + 1), "v": (v_raw, i + 1), "w": (v_ready, i + 1)}[what])
        for k in range(KD):
            says(("x2", k), x2_ready, k + 1)

        def wait_read(eng, n):
            eng.wait_ge(*read[n])

        def wait_bank(eng, n, i=None):
            if i is None:
                if n >= 2:
                    wait_read(eng, n - 2)
            else:
                s, value = read[n - 2]
                eng.wait_ge(s, value + KD * (i - 1))

        def wait_tile(eng, n, i=0):
            eng.wait_ge(tile_done, n + 1 + 16 * i)

        def split_high(act, u, i=0):
            if u >= n_units:
                return
            act.wait_ge(stage_in[u % STAGE], loaded[u] + 16 * (16 // STAGE) * i)
            if u >= SPLIT:
                act.wait_ge(tile_done, tile_of_unit[u - SPLIT] + 1 + 16 * i)
            n = unit_size(u)
            nc.scalar.copy(w_hi[:, u % SPLIT, 0:n], stage[:, u % STAGE, 0:n]).then_inc(hi_ready, 1)

        def split_low(dve, u, i=0):
            if u >= n_units:
                return
            dve.wait_ge(hi_ready, u + 1 + 16 * i)
            n = unit_size(u)
            nc.vector.tensor_tensor(w_lo[:, u % SPLIT, 0:n], stage[:, u % STAGE, 0:n],
                                    w_hi[:, u % SPLIT, 0:n].bitcast(F32), ALU.subtract).then_inc(lo_ready, 1)

        AHEAD_HI, AHEAD_LO = SPLIT, SPLIT - 1

        class Chain:
            def __init__(self, eng, s):
                self.eng, self.sem, self.n = eng, s, 0

            def link(self, ins, i=0, per=0):
                self.n += 1
                ins.then_inc(self.sem, 1)
                self.eng.wait_ge(self.sem, self.n + per * i)

        def halves(ap, L):
            return ap.rearrange("p (b h j) -> p b h j", h=2, j=L)

        def gain(layer, n, k):
            c = (layer * 4 + n) * KD + k
            return vec[:, c:c + 1]

        block = ctx.enter_context(nc.Block())

        @block.sync
        def _(sp):
            for i in range(4):
                c = slice(i * 2 * P, (i + 1) * 2 * P)
                sp.dma_start(x_tok[:, :, c], x[0].rearrange("(t p) d -> p t d", p=P)[:, :, c]).then_inc(x_in[i], 16)

            def stage_free(u, i=0):
                if u >= STAGE:
                    sp.wait_ge(hi_ready, u - STAGE + 1 + 16 * i)
                    sp.wait_ge(lo_ready, u - STAGE + 1 + 16 * i)

            def load(u):
                stage_free(u)
                for shape, c0, c1, src in units[u]:
                    size = shape[0] * shape[1]
                    slot = stage[:, u % STAGE, 0:size].rearrange("p (k c) -> p k c", k=shape[0])
                    if c0 is None:
                        dst = slot[:, c1, :].rearrange("p (h c) -> p h c", c=P)
                    else:
                        dst = slot[:, :, c0:c1]
                    sp.dma_start(dst, src).then_inc(stage_in[u % STAGE], 16)

            def load_mlp(layer):
                u0 = unit_no[("mlp", layer, 0, 0)]
                w1 = mlp_w1[layer].rearrange("(k p) n -> p k n", p=P)
                w2 = mlp_w2[layer].rearrange("(g k p) n -> p (g k) n", p=P, k=KD)
                with sp.Fori(0, GROUPS) as i:
                    for m in range(2 * KD):
                        u = u0 + m
                        stage_free(u, i)
                        dst = stage[:, u % STAGE, :].rearrange("p (k c) -> p k c", k=KD)
                        if m < KD:
                            src = w1[:, :, bass.ds(i * D + m * P, P)]
                        else:
                            src = w2[:, bass.ds(i * KD, KD), (m - KD) * P:(m - KD + 1) * P]
                        sp.dma_start(dst, src).then_inc(stage_in[u % STAGE], 16)

            for u in range(unit_no[("mlp", 0, 0, 0)]):
                load(u)
            load_mlp(0)
            for u in range(unit_no[("oi", LATENTS[0])], unit_no[("mlp", 1, 0, 0)]):
                load(u)
            load_mlp(1)
            for m in range(2 * NT):
                half, t = divmod(m, NT)
                sp.wait_ge(out_ready, m + 1)
                sp.dma_start(out[0, t * P:(t + 1) * P, half * T:(half + 1) * T], y[:, m, :]).then_inc(out_stored, 16)
            sp.wait_ge(out_stored, 16 * 2 * NT)

        @block.gpsimd
        def _(pool):
            nc.gpsimd.memset(ones[:, :], 1.0).then_inc(consts_ready, 1)
            nc.gpsimd.memset(eps[:, :], EPS).then_inc(consts_ready, 1)
            ch = Chain(pool, pool_chain)
            ch.link(nc.gpsimd.memset(ident[:, :], 0.0))
            nc.gpsimd.affine_select(out=ident[:, :], in_=ident[:, :], compare_op=ALU.not_equal, fill=1.0, base=0,
                                    pattern=[[-1, P]], channel_multiplier=1).then_inc(consts_ready, 1)
            ch.link(nc.gpsimd.memset(masks[:, :, :], 0.0))
            ch.link(nc.gpsimd.memset(masks[:, 0, :], 1.0))
            for lv in range(2, LEVELS):
                L = 64 >> lv
                right = masks[:, lv - 1, :].rearrange("p (b h j) -> p b h j", h=2, j=L)[:, :, 1, :]
                ch.link(nc.gpsimd.memset(right, 1.0))
                ch.link(nc.gpsimd.affine_select(out=right, in_=right, compare_op=ALU.is_ge, fill=0.0, base=0,
                                                pattern=[[-2 * L, P // (2 * L)], [0, L]], channel_multiplier=1))
                ch.link(nc.gpsimd.affine_select(out=right, in_=right, compare_op=ALU.is_ge, fill=0.0, base=L - 1,
                                                pattern=[[2 * L, P // (2 * L)], [0, L]], channel_multiplier=-1))
            nc.gpsimd.affine_select(out=masks[:, PAIRS - 1, :], in_=masks[:, PAIRS - 1, :], compare_op=ALU.not_equal,
                                    fill=1.0, base=0, pattern=[[-1, P]], channel_multiplier=1).then_inc(consts_ready, 1)

            for p in range(len(PACKS)):
                pool.wait_ge(b_ready, p + 1)
                for lv in range(LEVELS + 1):
                    item = p * (LEVELS + 2) + lv
                    if item >= 3:
                        pool.wait_ge(xl_ready, item - 2)
                    L = 64 >> lv
                    if lv < LEVELS:
                        ref = halves(b_sb[:, :], L)[:, :, 0, L - 1:L]
                    else:
                        L = P // 2
                        ref = halves(b_sb[:, :], L)[:, :, 1, L - 1:L]
                    shape = [P, T // (2 * L), 2 * L]
                    nc.gpsimd.tensor_tensor(dec[:, item % 3, :].rearrange("p (b j) -> p b j", j=2 * L),
                                            b_sb[:, :].rearrange("p (b j) -> p b j", j=2 * L),
                                            ref.to_broadcast(shape), ALU.subtract).then_inc(d_ready, 1)
            pool.wait_ge(mix_ready, 8)
            pool.dma_start(x_tok[:, :, :], x[0].rearrange("(t p) d -> p t d", p=P)).then_inc(x_again, 16)

            def add_squares(j):
                for m in range(1, KD - 2):
                    pool.wait_ge(sq_ready[j], m + 1)
                    if m >= 2:
                        pool.wait_ge(sq_used[j], m - 1)
                    nc.gpsimd.tensor_tensor(acc, acc, squares[m % 2], ALU.add).then_inc(sq_used[j], 1)

            def residual(step, every=1):
                if step == 0:
                    pool.wait_ge(x2_ready, KD)
                for k in range(0, KD, every):
                    pool.wait_ge(y_scaled, step * KD + k + 1)
                    nc.gpsimd.tensor_tensor(xT[:, k, :], xT[:, k, :], y[:, k, :], ALU.add).then_inc(x_new, 1)

            def square_residual(step):
                pool.wait_ge(x_new, (step + 1) * KD)
                for k in range(KD):
                    ch.link(nc.gpsimd.tensor_tensor(squares[1] if k else acc, xT[:, k, :], xT[:, k, :], ALU.mult))
                    if k:
                        ins = nc.gpsimd.tensor_tensor(acc, acc, squares[1], ALU.add)
                        if k < KD - 1:
                            ch.link(ins)
                ins.then_inc(sq_x, 1)

            add_squares(1)
            residual(0)
            pool.wait_ge(x_new, KD)
            nc.gpsimd.memset(y[:, :, :], 0.0).then_inc(y_zero[0], 1)
            square_residual(0)
            turns, part = p_t[:, 1, :], p_t[:, 2, :]
            pool.wait_ge(y_zero[0], 1)
            pool.dma_start(pos_i, positions.partition_broadcast(P)).then_inc(pos_in, 16)
            pool.wait_ge(pos_in, 16)
            ch.link(nc.gpsimd.tensor_copy(ang[:, :], pos_i))
            ch.link(nc.gpsimd.tensor_scalar(ang[:, :], ang[:, :], ropec[:, 0:1], None, ALU.mult))
            for dst, turn in ((sind, 0.0), (cosd, 0.25)):
                ch.link(nc.gpsimd.tensor_scalar(turns, ang[:, :], 0.15915494309189535, turn, ALU.mult, ALU.add))
                ch.link(nc.gpsimd.tensor_scalar(turns, turns, MAGIC, None, ALU.add))
                ch.link(nc.gpsimd.tensor_scalar(turns, turns, MAGIC, None, ALU.subtract))
                for i, two_pi in enumerate((TWO_PI_A, TWO_PI_B, TWO_PI_C)):
                    ch.link(nc.gpsimd.tensor_scalar(part, turns, two_pi, None, ALU.mult))
                    ch.link(nc.gpsimd.tensor_tensor(dst[:, :], dst[:, :] if i else ang[:, :], part, ALU.subtract))
                ch.link(nc.gpsimd.tensor_scalar(dst[:, :], dst[:, :], turn * 6.283185307179586, None, ALU.add))
                ins = nc.gpsimd.tensor_scalar(dst[:, :], dst[:, :], PI_IN, -PI_IN, ALU.min, ALU.max)
                if turn == 0.0:
                    ch.link(ins)
            ins.then_inc(sin_arg, 1)
            add_squares(3)
            residual(1)
            square_residual(1)
            pool.wait_ge(y_zero[0], 1)
            ch.link(nc.gpsimd.memset(mask_q[:, :], 0.0))
            ch.link(nc.gpsimd.memset(mask_k[:, :], 0.0))
            nc.gpsimd.memset(mask_q[0:1, 0:P // 2], MASKED).then_inc(consts_ready, 1)
            nc.gpsimd.memset(mask_k[0:1, P // 2:P], 1.0).then_inc(consts_ready, 1)
            add_squares(5)
            residual(2)
            pool.wait_ge(x_new, 3 * KD)
            nc.gpsimd.memset(y[:, :, :], 0.0).then_inc(y_zero[1], 1)
            square_residual(2)
            add_squares(7)
            residual(3, 2)

        @block.scalar
        def _(act):
            ch = Chain(act, act_chain)
            small = [(0, norm_gains.rearrange("l n (k p) -> (l n k) p", p=P)),
                     (V_LB, hg_lb_table.rearrange("r (h p) -> (r h) p", p=P)),
                     (V_BG, gla_b_gate.rearrange("e (k p) -> (e k) p", p=P)),
                     (V_HGN, hg_out_norm), (V_GLN, gla_out_norm),
                     (V_QN, mla_q_norm.rearrange("e (k p) -> (e k) p", p=P)),
                     (V_KVN, mla_kv_norm.rearrange("e (k p) -> (e k) p", p=P))]
            for r, src in small:
                act.dma_start(vrows[r:r + src.shape[0], :], src).then_inc(vec_in, 16)
            act.dma_start(w_gate[:, :], gla_w_gate[0]).then_inc(vec_in, 16)
            act.dma_start(ropec[:, :], rope_const).then_inc(vec_in, 16)

            def inv_rms(src, width, slot, ready):
                ch.link(nc.scalar.activation(rinv[:, slot, :], src, ACT.Ln, bias=eps[:, 0:1], scale=1.0 / width))
                nc.scalar.activation(rinv[:, slot, :], rinv[:, slot, :], ACT.Exp, scale=-0.5).then_inc(ready, 1)

            def pre_norm(j, xs, hs, split_first=False):
                for k in range(KD):
                    act.wait_ge(x_ready, xs + k + 1)
                    if k >= 2:
                        act.wait_ge(sq_used[j], k - 1)
                    nc.scalar.activation(sq[:, k % 2, :], xT[:, k, :], ACT.Square).then_inc(sq_ready[j], 1)
                    if split_first and k == KD // 2:
                        split_high(act, 0)
                act.wait_ge(sq_used[j], KD)
                inv_rms(misc[:, :], D, 0, r_ready[j])
                if split_first:
                    split_high(act, 1)
                    split_high(act, 2)
                for k in range(KD):
                    act.wait_ge(h_f32, hs + k + 1)
                    nc.scalar.copy(h_hi[:, k, :], tmp[:, k % 2, :]).then_inc(h_high, 1)
                if split_first:
                    split_high(act, 3)

            def y_square(j, ys, m):
                act.wait_ge(y_ready[j], ys + m + 1)
                if m == 0 and j >= 3:
                    act.wait_ge(sum_done[j - 1], 1)
                if m >= 3:
                    act.wait_ge(sq_used[j], m - 2)
                nc.scalar.activation(acc if m == 0 else squares[m % 2], y[:, m, :], ACT.Square).then_inc(sq_ready[j], 1)

            def post_norm(j):
                if j in (1, 5):
                    act.wait_ge(sum_done[j], 1)
                    inv_rms(misc[:, :], D, 1, r_ready[j])
                else:
                    act.wait_ge(ms_ready, {3: 2, 7: 6}[j])
                    ch.link(nc.scalar.activation(rinv[:, 1, :], rinv[:, 1, :], ACT.Ln))
                    nc.scalar.activation(rinv[:, 1, :], rinv[:, 1, :], ACT.Exp, scale=-0.5).then_inc(r_ready[j], 1)

            def scaled_high(step, layer, which, hs):
                for k in range(KD):
                    act.wait_ge(x_new, step * KD + k + 1)
                    nc.scalar.activation(h_hi[:, k, :], xT[:, k, :], ACT.Copy, scale=gain(layer, which, k)).then_inc(h_high, 1)

            def pump(u, i=0):
                split_high(act, u + AHEAD_HI, i)

            nc.scalar.preload_act_table_set("natural_log_exp_and_others")
            act.wait_ge(consts_ready, 4)
            act.wait_ge(vec_ready, 2)
            nc.scalar.activation(lbt[:, 1:3, :], lbt[:, 1:3, :], ACT.Exp).then_inc(vec_ready, 1)
            pre_norm(0, 0, 0, split_first=True)

            n = tile_no[("ga", 0)]
            wait_tile(act, n)
            nc.scalar.copy(ga_t[:, :], bank[n % 2][0:GATE_RANK, :]).then_inc(ga_ready, 1)
            pump(unit_no[("ga", 0)])

            def decay(p, lv):
                s = 1.0 if PACKS[p][0] == "hg" else 1.0 / GATE_TEMP
                item = p * (LEVELS + 2) + lv
                d = dec[:, item % 3, :]
                if lv <= LEVELS:
                    act.wait_ge(d_ready, p * (LEVELS + 1) + lv + 1)
                if lv < LEVELS:
                    v = halves(d, 64 >> lv)
                    nc.scalar.activation(v[:, :, 0, :], v[:, :, 0, :], ACT.Exp, scale=-s).then_inc(e_ready, 1)
                    nc.scalar.activation(v[:, :, 1, :], v[:, :, 1, :], ACT.Exp, scale=s).then_inc(e_ready, 1)
                elif lv == LEVELS:
                    nc.scalar.activation(d, d, ACT.Exp, scale=-s).then_inc(e_ready, 1)
                    if p >= 2:
                        act.wait_ge(state_ready, p - 1)
                    last = b_sb[:, :].rearrange("p (c j) -> p c j", j=P)[:, :, P - 1]
                    nc.scalar.activation(e_last[:, p % 2, :], last, ACT.Exp, scale=s).then_inc(e_ready, 1)
                else:
                    act.wait_ge(xl_ready, item - 2)
                    nc.scalar.activation(d, b_sb[:, :], ACT.Exp, scale=s).then_inc(e_ready, 1)

            def sigmoid(t, clamped, ready):
                act.wait_ge(*clamped)
                ch.link(nc.scalar.activation(t, t, ACT.Exp, scale=-1.0))
                ch.link(nc.scalar.activation(t, t, ACT.Ln, bias=1.0))
                nc.scalar.activation(t, t, ACT.Exp, scale=-1.0).then_inc(ready, 1)

            def evacuate(what, i):
                n = tile_no[(what, i)]
                ps = bank[n % 2][:, :]
                wait_tile(act, n)
                if what in ("q", "k") and i >= 3:
                    act.wait_ge(p_done, NT * FIRST[i - 2])
                if what == "f":
                    sigmoid(t_f[:, :], (f_clamped, i - 1), f_sig)
                elif what == "g":
                    sigmoid(t_g[:, :], (g_clamped, i + 1), g_sig)
                elif what == "q":
                    scale = 1.0 if PACKS[i][0] == "hg" else GLA_DK ** -0.5
                    nc.scalar.activation(qs[i % 3], ps, ACT.Copy, scale=scale).then_inc(q_ready, 1)
                    if PACKS[i][0] == "hg":
                        act.wait_ge(f_gate, i + 1)
                        nc.scalar.activation(t_f[:, :], t_f[:, :], ACT.Ln).then_inc(f_log, 1)
                elif what == "k":
                    nc.scalar.activation(ks[i % 3], ps, ACT.Copy).then_inc(k_ready, 1)
                elif what == "v":
                    if i >= 4:
                        act.wait_ge(o_done, i - 3)
                    nc.scalar.activation(vbuf[:, i % 4, :], ps, ACT.Copy).then_inc(v_raw, 1)
                elif what == "w":
                    nc.scalar.activation(vbuf[:, i % 4, :], ps, ACT.Copy).then_inc(v_ready, 1)
                elif what == "z":
                    if i >= 1:
                        act.wait_ge(b_ready, i)
                    bg = vec[:, V_BG + i:V_BG + i + 1]
                    nc.scalar.activation(t_f[:, :], ps, ACT.Identity, bias=bg).then_inc(z_read, 1)
                    act.wait_ge(z_read, i + 1)
                    ch.link(nc.scalar.activation(t_g[:, :], t_f[:, :], ACT.Abs))
                    ch.link(nc.scalar.activation(t_g[:, :], t_g[:, :], ACT.Exp, scale=-1.0))
                    nc.scalar.activation(t_g[:, :], t_g[:, :], ACT.Ln, bias=1.0).then_inc(f_log, 1)

            def head_square(o):
                act.wait_ge(o_done, o + 1)
                if o >= 1:
                    act.wait_ge(o_sum, o)
                    act.wait_ge(mix_ready, o)
                nc.scalar.activation(sq[:, 0, :], po[:, :], ACT.Square).then_inc(o_sq, 1)
                nc.scalar.activation(sq[:, 1, :], po[:, :], ACT.Copy).then_inc(o_read, 1)

            def head_norm(o):
                act.wait_ge(o_sum, o + 1)
                if o >= 1:
                    act.wait_ge(mix_f32, o)
                inv_rms(misc[:, :], P, 0, o_rinv)

            def head_high(o):
                act.wait_ge(mix_f32, o + 1)
                nc.scalar.copy(a_hi[:, HEAD[o], :], sq[:, 1, :]).then_inc(mix_high, 1)

            for i, (tile, col, items, groups, end) in enumerate(SLOTS):
                if tile is not None:
                    evacuate(*tile)
                    if col is not None:
                        pump(unit_no[tile])
                for p, lv in items:
                    decay(p, lv)
                for o in SUMS[i]:
                    head_norm(o)
                for o in MIXES[i]:
                    head_high(o)
                for o in SQUARES[i]:
                    head_square(o)
                for o, c in groups:
                    p = PACK_OF[o]
                    if c == 0 and FIRST[p] == o:
                        act.wait_ge(ket_done, p + 1)
                        nc.scalar.activation(ke_t[:, :, :].rearrange("p c d -> p (c d)"), misc[:, 0:(NT - 1) * P],
                                             ACT.Copy).then_inc(ket_ready, 1)

            def linear_out(name, j):
                for m in range(KD):
                    if m >= 1:
                        y_square(j, 0, m - 1)
                    wait_tile(act, tile_no[(name, m)])
                    pump(unit_no[(name, m)])
                y_square(j, 0, KD - 1)
                post_norm(j)

            linear_out("eo", 1)
            scaled_high(0, 0, 2, KD)

            def mlp(layer, j):
                n0, u0 = tile_no[("mlp", layer, 0, 0)], unit_no[("mlp", layer, 0, 0)]

                def group(i, last):
                    for m in range(2 * KD):
                        n = n0 + m
                        wait_tile(act, n, i)
                        if m < KD:
                            if m >= 2:
                                act.wait_ge(hid_f32[layer], m - 1 + KD * i)
                            nc.scalar.activation(sq[:, m % 2, :], bank[n % 2][:, :], ACT.Relu).then_inc(relu_ready[layer], 1)
                        if not last or m < 2 * KD - AHEAD_HI or layer == 0:
                            pump(u0 + m, i)
                        if m < KD:
                            act.wait_ge(hid_f32[layer], m + 1 + KD * i)
                            nc.scalar.copy(a_hi[:, m, :], tmp[:, m % 2, :]).then_inc(hid_high[layer], 1)
                        elif last and m > KD:
                            y_square(j, (GROUPS - 1) * KD, m - KD - 1)

                with act.Fori(0, GROUPS - 1) as i:
                    group(i, False)
                if layer == 0:
                    act.wait_ge(sin_arg, 1)
                    nc.scalar.activation(sind[:, :], sind[:, :], ACT.Sin).then_inc(sin_ready, 1)
                    nc.scalar.activation(cosd[:, :], cosd[:, :], ACT.Sin).then_inc(sin_ready, 1)
                    nc.scalar.preload_act_table_set("natural_log_exp_and_others")
                group(GROUPS - 1, True)
                y_square(j, (GROUPS - 1) * KD, KD - 1)
                post_norm(j)

            mlp(0, 3)

            scaled_high(1, 1, 0, 2 * KD)
            for i, m in enumerate(LATENTS):
                n = tile_no[("oi", m)]
                wait_tile(act, n)
                nc.scalar.activation(y[:, m, :], bank[n % 2][:, :], ACT.Copy).then_inc(c_ready, 1)
                act.wait_ge(c_ready, i + 1)
                if i >= 2:
                    act.wait_ge(sq_used[8], i - 1)
                nc.scalar.activation(sq[:, i % 2, :], y[:, m, :], ACT.Square).then_inc(sq_ready[8], 1)
                pump(unit_no[("oi", m)])

            def inv_root(v, ready):
                ch.link(nc.scalar.activation(v, v, ACT.Ln))
                nc.scalar.activation(v, v, ACT.Exp, scale=-0.5).then_inc(ready, 1)

            def latent_high(i):
                act.wait_ge(h_f32, KD + i + 1)
                nc.scalar.copy((a_hi if i < KV_RANK_T else h_hi)[:, LATENTS[i], :], tmp[:, i % 2, :]).then_inc(h_high, 1)

            act.wait_ge(ms_ready, 3)
            inv_root(rinv[:, 1, :], r_ready[8])
            latent_high(0)
            latent_high(1)
            for m in (5, 6):
                wait_tile(act, tile_no[("oi", m)])
                pump(unit_no[("oi", m)])
            for what in ("mv", "mk"):
                for g in range(2):
                    for j in range(4):
                        n = tile_no[(what, g, j)]
                        wait_tile(act, n)
                        dst = v_tok[:, j, g * T:(g + 1) * T] if what == "mv" else y[:, 4 * g + j, :]
                        nc.scalar.activation(dst, bank[n % 2][:, :], ACT.Copy).then_inc(
                            vt_ready if what == "mv" else kt_ready, 1)
                        if (what, g, j) == ("mv", 0, 1):
                            act.wait_ge(ms_ready, 4)
                            inv_root(rinv[:, 0, :], r_ready[8])
                        elif what == "mv" and g == 1 and j < 3:
                            latent_high(2 + j)
                        elif (what, g, j) == ("mk", 0, 0):
                            inv_root(ms_in, r_ready[4])
                    pump(unit_no[(what, g)])

            def q_evacuate(a):
                if a == 1:
                    act.wait_ge(rope_ready, 1)
                for hh in range(2):
                    n = tile_no[("qn", a, hh)]
                    wait_tile(act, n)
                    nc.scalar.activation(qn[:, a % 2, hh, :], bank[n % 2][:, :], ACT.Copy,
                                         scale=SCALE).then_inc(qn_ready, 1)
                pump(unit_no[("qn", a)])
                wait_tile(act, tile_no[("qr", a, 1)])
                pump(unit_no[("qr", a)])

            def att_out(h):
                act.wait_ge(pv_done, h + 1)
                nc.scalar.copy(a_hi[:, h, :], po[:, :]).then_inc(att_high, 1)

            q_evacuate(0)
            for j in range(4 * MLA_HEADS + 2):
                if j % 8 == 0 and j // 8 + 1 < MLA_HEADS // 2:
                    q_evacuate(j // 8 + 1)
                if j < 4 * MLA_HEADS:
                    width = (j % 4 + 1) * P
                    act.wait_ge(nmax_ready, j + 1)
                    nc.scalar.activation(prob[:, j % 3, 0:width], s_bank[j % 3][:, 0:width], ACT.Exp,
                                         bias=stat[:, 0, j:j + 1], accum_out=stat[:, 1, j:j + 1]).then_inc(prob_exp, 1)
                if j >= 6 and j % 4 == 2:
                    att_out(j // 4 - 1)
            att_out(MLA_HEADS - 1)
            linear_out("oo", 5)
            scaled_high(2, 1, 2, 3 * KD + 5)
            mlp(1, 7)
            for m in range(2 * NT):
                n = tile_no[("out", m)]
                wait_tile(act, n)
                nc.scalar.activation(y[:, m, :], bank[n % 2][:, :], ACT.Copy).then_inc(out_ready, 1)

        @block.vector
        def _(dve):
            ch = Chain(dve, dve_chain)

            def pump(u, i=0):
                split_low(dve, u + AHEAD_LO, i)

            def pre_norm(j, layer, which, hs):
                dve.wait_ge(r_ready[j], 1)
                for k in range(KD + 1):
                    if 2 <= k < KD:
                        dve.wait_ge(h_ready, hs + k - 1)
                    if k < KD:
                        nc.vector.scalar_tensor_tensor(out=tmp[:, k % 2, :], in0=xT[:, k, :], scalar=gain(layer, which, k),
                                                       in1=rinv[:, 0, :], op0=ALU.mult, op1=ALU.mult).then_inc(h_f32, 1)
                    if k >= 1:
                        dve.wait_ge(h_high, hs + k)
                        nc.vector.tensor_tensor(h_lo[:, k - 1, :], tmp[:, (k - 1) % 2, :],
                                                h_hi[:, k - 1, :].bitcast(F32), ALU.subtract).then_inc(h_ready, 1)
                dve.wait_ge(h_ready, hs + KD)

            def scale_output(j, layer, which, after, hs):
                dve.wait_ge(r_ready[j], 1)
                for k in range(KD + 2):
                    if k < KD:
                        nc.vector.scalar_tensor_tensor(out=y[:, k, :], in0=y[:, k, :], scalar=gain(layer, which, k),
                                                       in1=rinv[:, 1, :], op0=ALU.mult, op1=ALU.mult).then_inc(y_scaled, 1)
                    if k < KD and k % 2 == 1 and after is None:
                        dve.wait_ge(y_scaled, 3 * KD + k + 1)
                        nc.vector.tensor_tensor(xT[:, k, :], xT[:, k, :], y[:, k, :], ALU.add).then_inc(x_odd, 1)
                    if k >= 2 and after is not None:
                        dve.wait_ge(h_high, hs + k - 1)
                        nc.vector.scalar_tensor_tensor(out=h_lo[:, k - 2, :], in0=xT[:, k - 2, :],
                                                       scalar=gain(*after, k - 2), in1=h_hi[:, k - 2, :].bitcast(F32),
                                                       op0=ALU.mult, op1=ALU.subtract).then_inc(h_ready, 1)

            dve.wait_ge(vec_done, 1)
            nc.vector.tensor_copy(vec[:, :], misc[:, 0:V_ROWS]).then_inc(vec_ready, 1)
            dve.wait_ge(vec_ready, 1)
            t0, t1 = vec[:, V_LB:V_LB + HEADS], vec[:, V_LB + HEADS:V_LB + 2 * HEADS]
            ch.link(nc.vector.tensor_tensor(lbt[:, 0, :], t0, t1, ALU.max))
            ch.link(nc.vector.tensor_tensor(lbt[:, 1, :], t0, lbt[:, 0, :], ALU.subtract))
            nc.vector.tensor_tensor(lbt[:, 2, :], t1, lbt[:, 0, :], ALU.subtract).then_inc(vec_ready, 1)
            dve.wait_ge(vec_ready, 3)
            ch.link(nc.vector.tensor_tensor(lbt[:, 0, :], lbt[:, 1, :], lbt[:, 2, :], ALU.add))
            ch.link(nc.vector.reciprocal(lbt[:, 3, :], lbt[:, 0, :]))
            ch.link(nc.vector.tensor_tensor(lbt[:, 4, :], lbt[:, 1, :], lbt[:, 3, :], ALU.mult))
            ch.link(nc.vector.tensor_scalar(lbt[:, 5, :], lbt[:, 4, :], -1.0, 1.0, ALU.mult, ALU.add))

            for b in range(2):
                nc.vector.memset(pp[b][:, 0, :], 0.0).then_inc(p_zero, 1)
            for k in range(KD):
                n = tile_no[("x", k)]
                wait_tile(dve, n)
                nc.vector.tensor_copy(xT[:, k, :], bank[n % 2][:, :]).then_inc(x_ready, 1)
            split_low(dve, 0)
            split_low(dve, 1)
            pre_norm(0, 0, 0, 0)
            split_low(dve, 2)
            wait_tile(dve, tile_no[("ga", 0)])
            pump(unit_no[("ga", 0)])

            def decayed(p, lv):
                item = p * (LEVELS + 2) + lv
                q, k, e, x_ = qs[p % 3], ks[p % 3], dec[:, item % 3, :], xls[p % 2]
                done = p * (2 * LEVELS + 3) + 2 * lv
                if lv == 0 and p >= 2:
                    dve.wait_ge(p_done, NT * FIRST[p - 1])
                dve.wait_ge(e_ready, done + 2 if lv <= LEVELS else done + 1)
                if lv < LEVELS:
                    L = 64 >> lv
                    nc.vector.tensor_tensor(halves(x_[:, lv, :], L)[:, :, 0, :], halves(k, L)[:, :, 0, :],
                                            halves(e, L)[:, :, 0, :], ALU.mult)
                    nc.vector.tensor_tensor(halves(x_[:, lv, :], L)[:, :, 1, :], halves(q, L)[:, :, 1, :],
                                            halves(e, L)[:, :, 1, :], ALU.mult).then_inc(xl_ready, 1)
                elif lv == LEVELS:
                    if p >= 1:
                        dve.wait_ge(ket_done, p)
                    nc.vector.tensor_tensor(ke[:, :], k, e, ALU.mult).then_inc(xl_ready, 1)
                else:
                    if p >= 2:
                        dve.wait_ge(o_done, FIRST[p - 1])
                    nc.vector.tensor_tensor(qes[p % 2], q, e, ALU.mult).then_inc(xl_ready, 1)

            def clamp(what, i):
                n = tile_no[(what, i)]
                wait_tile(dve, n)
                if what == "f":
                    dve.wait_ge(b_ready, i)
                    nc.vector.tensor_scalar(t_f[:, :], bank[n % 2][:, :], EXP_MAX, None, ALU.max).then_inc(f_clamped, 1)
                else:
                    dve.wait_ge(f_gate, 2)
                    if i >= 1:
                        dve.wait_ge(gate_ready, i)
                    nc.vector.tensor_scalar(t_g[:, :], bank[n % 2][:, :], EXP_MAX, None, ALU.max).then_inc(g_clamped, 1)

            def evacuate(what, i):
                n = tile_no[(what, i)]
                if what == "f":
                    a = PACKS[i][1]
                    dve.wait_ge(f_sig, i - 1)
                    ch.link(nc.vector.tensor_scalar(t_f[:, :], t_f[:, :], lbt[:, 5, a:a + 1], lbt[:, 4, a:a + 1],
                                                    ALU.mult, ALU.add))
                    nc.vector.tensor_scalar(ks[i % 3], t_f[:, :], -1.0, 1.0, ALU.mult, ALU.add).then_inc(f_gate, 1)
                elif what == "g":
                    dve.wait_ge(g_sig, i + 1)
                    if i >= GATE_SLOTS:
                        dve.wait_ge(mix_f32, i - GATE_SLOTS + 1)
                    nc.vector.tensor_tensor(y[:, i % GATE_SLOTS, :], bank[n % 2][:, :], t_g[:, :],
                                            ALU.mult).then_inc(gate_ready, 1)
                elif what == "z":
                    dve.wait_ge(f_log, i + 1)
                    nc.vector.scalar_tensor_tensor(out=t_f[:, :], in0=t_f[:, :], scalar=0.0, in1=t_g[:, :],
                                                   op0=ALU.min, op1=ALU.subtract).then_inc(f_gate, 1)
                else:
                    wait_tile(dve, n)

            def cumulate(p):
                dve.wait_ge(f_log, p + 1)
                dve.wait_ge(f_gate, p + 1)
                for c in range(NT):
                    s = slice(c * P, (c + 1) * P)
                    ins = nc.vector.tensor_tensor_scan(b_sb[:, s], ones[:, :], t_f[:, s], 0.0, ALU.mult, ALU.add)
                ins.then_inc(b_ready, 1)

            def head_gate(o):
                dve.wait_ge(o_rinv, o + 1)
                g = V_HGN if HEAD[o] < 4 else V_GLN
                ch.link(nc.vector.scalar_tensor_tensor(out=sq[:, 1, :], in0=sq[:, 1, :], scalar=vec[:, g:g + 1],
                                                       in1=rinv[:, 0, :], op0=ALU.mult, op1=ALU.mult))
                dve.wait_ge(gate_ready, o + 1)
                nc.vector.tensor_tensor(sq[:, 1, :], sq[:, 1, :], y[:, o % GATE_SLOTS, :], ALU.mult).then_inc(mix_f32, 1)

            def head_low(o):
                dve.wait_ge(mix_high, o + 1)
                nc.vector.tensor_tensor(a_lo[:, HEAD[o], :], sq[:, 1, :], a_hi[:, HEAD[o], :].bitcast(F32),
                                        ALU.subtract).then_inc(mix_ready, 1)

            def update_state(p):
                dve.wait_ge(kv_done, p + 1)
                kv = misc[:, 0:(NT - 1) * P].rearrange("p (c d) -> p c d", c=NT - 1)
                ch.link(nc.vector.tensor_copy(state[:, 0, :], kv[:, 0, :]))
                for cc in range(1, NT - 1):
                    ins = nc.vector.scalar_tensor_tensor(
                        out=state[:, cc, :], in0=state[:, cc - 1, :], scalar=e_last[:, p % 2, cc:cc + 1],
                        in1=kv[:, cc, :], op0=ALU.mult, op1=ALU.add)
                    if cc < NT - 2:
                        ch.link(ins)
                ins.then_inc(state_ready, 1)

            def group(o, c):
                idx = o * NT + c
                pm = tmp[:, :, :].rearrange("p a t -> p (a t)")[:, 0:PAIRS * P]
                dve.wait_ge(p_done, idx + 1)
                if idx >= 1:
                    dve.wait_ge(a_ready, idx)
                nc.vector.tensor_tensor(pm, pp[idx % 2][:, 0:PAIRS, :].rearrange("p l t -> p (l t)"),
                                        masks[:, :, :].rearrange("p l t -> p (l t)"), ALU.mult).then_inc(p_read, 1)
                dve.wait_ge(p_read, idx + 1)
                nc.vector.tensor_reduce(a_sb[:, idx % 4, :], pm.rearrange("p (l t) -> p t l", l=PAIRS),
                                        AX_X, ALU.add).then_inc(a_ready, 1)
                if c == 2 and FIRST[PACK_OF[o]] == o:
                    update_state(PACK_OF[o])

            for i, (tile, col, items, groups, end) in enumerate(SLOTS):
                if tile is not None:
                    if tile[0] in "fg":
                        clamp(*tile)
                    if col is not None:
                        wait_tile(dve, tile_no[tile])
                        pump(unit_no[tile])
                    evacuate(*tile)
                for o in MIXES[i]:
                    head_gate(o)
                for p, lv in items:
                    decayed(p, lv)
                if end is not None:
                    cumulate(end)
                for o in MIXES[i]:
                    head_low(o)
                for o, c in groups:
                    group(o, c)

            def linear_out(name, j):
                for m in range(KD):
                    n = tile_no[(name, m)]
                    wait_tile(dve, n)
                    nc.vector.tensor_copy(y[:, m, :], bank[n % 2][:, :]).then_inc(y_ready[j], 1)
                    pump(unit_no[(name, m)])
                    for k in ([m - 1] if m >= 1 else []) + ([m] if m == KD - 1 else []):
                        if name == "eo":
                            n = tile_no[("x2", k)]
                            wait_tile(dve, n)
                            nc.vector.tensor_copy(xT[:, k, :], bank[n % 2][:, :]).then_inc(x2_ready, 1)

            def mlp(layer, j):
                n0, u0 = tile_no[("mlp", layer, 0, 0)], unit_no[("mlp", layer, 0, 0)]
                dve.wait_ge(y_zero[layer], 1)

                def group(i, last):
                    for m in range(2 * KD):
                        n = n0 + m
                        if m < KD:
                            dve.wait_ge(relu_ready[layer], m + 1 + KD * i)
                            if m >= 2:
                                dve.wait_ge(hid_ready[layer], m - 1 + KD * i)
                            nc.vector.tensor_tensor(tmp[:, m % 2, :], sq[:, m % 2, :], bank[n % 2][:, :],
                                                    ALU.mult).then_inc(hid_f32[layer], 1)
                        else:
                            wait_tile(dve, n, i)
                            nc.vector.tensor_tensor(y[:, m - KD, :], y[:, m - KD, :], bank[n % 2][:, :],
                                                    ALU.add).then_inc(y_ready[j], 1)
                        if not last or m < 2 * KD - AHEAD_LO or layer == 0:
                            pump(u0 + m, i)
                        if m < KD:
                            dve.wait_ge(hid_high[layer], m + 1 + KD * i)
                            nc.vector.tensor_tensor(a_lo[:, m, :], tmp[:, m % 2, :], a_hi[:, m, :].bitcast(F32),
                                                    ALU.subtract).then_inc(hid_ready[layer], 1)

                with dve.Fori(0, GROUPS - 1) as i:
                    group(i, False)
                j_in, count = j - 1, 0 if layer == 0 else 4
                dve.wait_ge(sum_done[j_in], 1)
                nc.vector.tensor_scalar(rinv[:, 0, :], s_bank[0], 1.0 / D, EPS, ALU.mult, ALU.add).then_inc(ms_ready, 1)
                dve.wait_ge(ms_ready, count + 1)
                ch.link(nc.vector.scalar_tensor_tensor(out=rinv[:, 0, :], in0=rinv[:, 0, :], scalar=EPS,
                                                       in1=rinv[:, 0, :], op0=ALU.mult, op1=ALU.mult))
                group(GROUPS - 1, True)
                dve.wait_ge(sum_done[j], 1)
                nc.vector.scalar_tensor_tensor(out=rinv[:, 1, :], in0=misc[:, :], scalar=1.0 / D, in1=rinv[:, 0, :],
                                               op0=ALU.mult, op1=ALU.add).then_inc(ms_ready, 1)

            linear_out("eo", 1)
            scale_output(1, 0, 1, (0, 2), KD)
            mlp(0, 3)
            scale_output(3, 0, 3, (1, 0), 2 * KD)

            for m in LATENTS:
                wait_tile(dve, tile_no[("oi", m)])
                pump(unit_no[("oi", m)])
            def latents(first, last):
                for j in range(first, last + 1):
                    if j < last:
                        if j >= 2:
                            dve.wait_ge(h_ready, 3 * KD + j - 1)
                        k = LATENTS[j]
                        g, slot = (V_KVN + j, 1) if j < 2 else (V_QN + j - 2, 0)
                        nc.vector.scalar_tensor_tensor(out=tmp[:, j % 2, :], in0=y[:, k, :], scalar=vec[:, g:g + 1],
                                                       in1=rinv[:, slot, :], op0=ALU.mult, op1=ALU.mult).then_inc(h_f32, 1)
                    if j > first:
                        k = LATENTS[j - 1]
                        dve.wait_ge(h_high, 3 * KD + j)
                        hi, lo = (a_hi, a_lo) if j - 1 < KV_RANK_T else (h_hi, h_lo)
                        nc.vector.tensor_tensor(lo[:, k, :], tmp[:, (j - 1) % 2, :], hi[:, k, :].bitcast(F32),
                                                ALU.subtract).then_inc(h_ready, 1)

            def rotate(n_plain, n_swapped, scale, dst, ready, done):
                wait_tile(dve, n_plain)
                nc.vector.scalar_tensor_tensor(out=dst, in0=bank[n_plain % 2][:, :], scalar=scale, in1=cosd[:, :],
                                               op0=ALU.mult, op1=ALU.mult).then_inc(rot_read, 1)
                wait_tile(dve, n_swapped)
                if done:
                    dve.wait_ge(ready, done)
                nc.vector.scalar_tensor_tensor(out=ang[:, :], in0=bank[n_swapped % 2][:, :], scalar=scale, in1=sind[:, :],
                                               op0=ALU.mult, op1=ALU.mult).then_inc(rot_read, 1)
                wait_read(dve, n_swapped)
                nc.vector.tensor_tensor(dst, dst, ang[:, :], ALU.add).then_inc(ready, 1)

            dve.wait_ge(sum_done[4], 1)
            ch.link(nc.vector.tensor_scalar(ms_in, s_bank[0], 1.0 / D, EPS, ALU.mult, ALU.add))
            ch.link(nc.vector.tensor_scalar(eps_in, ms_in, EPS, None, ALU.mult))
            dve.wait_ge(sq_used[8], 2)
            nc.vector.scalar_tensor_tensor(out=rinv[:, 1, :], in0=po[:, :], scalar=1.0 / (KV_RANK_T * P),
                                           in1=eps_in, op0=ALU.mult, op1=ALU.add).then_inc(ms_ready, 1)
            dve.wait_ge(r_ready[8], 1)
            latents(0, 2)
            for m in (5, 6):
                n = tile_no[("oi", m)]
                wait_tile(dve, n)
                nc.vector.tensor_copy(qn[:, 1, m - 5, :], bank[n % 2][:, :]).then_inc(kr_read, 1)
                pump(unit_no[("oi", m)])
            dve.wait_ge(sq_used[8], 5)
            nc.vector.scalar_tensor_tensor(out=rinv[:, 0, :], in0=misc[:, :], scalar=1.0 / (Q_RANK_T * P), in1=eps_in,
                                           op0=ALU.mult, op1=ALU.add).then_inc(ms_ready, 1)
            for what in ("mv", "mk"):
                for g in range(2):
                    if (what, g) == ("mv", 1):
                        dve.wait_ge(r_ready[8], 2)
                        latents(2, 5)
                    wait_tile(dve, tile_no[(what, g, 3)])
                    pump(unit_no[(what, g)])
            dve.wait_ge(sin_ready, 2)
            ch.link(nc.vector.tensor_scalar(sind[:, :], sind[:, :], ropec[:, 1:2], None, ALU.mult))
            ch.link(nc.vector.tensor_tensor(kr[:, :], qn[:, 1, 0, :], cosd[:, :], ALU.mult))
            ch.link(nc.vector.tensor_tensor(ang[:, :], qn[:, 1, 1, :], sind[:, :], ALU.mult))
            ch.link(nc.vector.tensor_tensor(kr[:, :], kr[:, :], ang[:, :], ALU.add))
            dve.wait_ge(r_ready[4], 1)
            nc.vector.tensor_tensor(kr[:, :], kr[:, :], ms_in, ALU.mult).then_inc(rope_ready, 1)

            def q_evacuate(a):
                wait_tile(dve, tile_no[("qn", a, 1)])
                pump(unit_no[("qn", a)])
                rotate(tile_no[("qr", a, 0)], tile_no[("qr", a, 1)], SCALE, qr[:, a % 2, :], qr_ready, a)
                pump(unit_no[("qr", a)])

            def att_out(h):
                dve.wait_ge(att_high, h + 1)
                nc.vector.tensor_tensor(a_lo[:, h, :], po[:, :], a_hi[:, h, :].bitcast(F32),
                                        ALU.subtract).then_inc(att_ready, 1)

            dve.wait_ge(rope_ready, 1)
            q_evacuate(0)
            for j in range(4 * MLA_HEADS + 2):
                if j % 8 == 0 and j // 8 + 1 < MLA_HEADS // 2:
                    q_evacuate(j // 8 + 1)
                if j < 4 * MLA_HEADS:
                    width = (j % 4 + 1) * P
                    dve.wait_ge(s_done, j + 1)
                    nc.vector.tensor_reduce(stat[:, 0, j:j + 1], s_bank[j % 3][:, 0:width], AX_X, ALU.max,
                                            negate=True).then_inc(nmax_ready, 1)
                if 1 <= j <= 4 * MLA_HEADS:
                    i = j - 1
                    width = (i % 4 + 1) * P
                    dve.wait_ge(prob_exp, i + 1)
                    ch.link(nc.vector.reciprocal(stat[:, 2, i:i + 1], stat[:, 1, i:i + 1]))
                    nc.vector.tensor_scalar(prob[:, i % 3, 0:width], prob[:, i % 3, 0:width], stat[:, 2, i:i + 1], None,
                                            ALU.mult).then_inc(prob_ready, 1)
                if j >= 2:
                    i = j - 2
                    qb = i % 4
                    dve.wait_ge(pt_done, i + 1)
                    nc.vector.tensor_copy(p_t[:, 0:qb + 1, qb * P:(qb + 1) * P],
                                          t_bank[i % 2][:, 0:qb + 1, :]).then_inc(pt_ready, 1)
                if j >= 6 and j % 4 == 2:
                    att_out(j // 4 - 1)
            att_out(MLA_HEADS - 1)
            linear_out("oo", 5)
            scale_output(5, 1, 1, (1, 2), 3 * KD + 5)
            mlp(1, 7)
            scale_output(7, 1, 3, None, None)

        @block.tensor
        def _(pe):
            def mm3(dst, wh, wl, xh, xl_, first, last):
                nc.tensor.matmul(dst, wh, xl_, start=first, stop=False)
                nc.tensor.matmul(dst, wl, xh, start=False, stop=False)
                return nc.tensor.matmul(dst, wh, xh, start=False, stop=last)

            def slot(u, cols):
                n = unit_size(u)
                return (w_hi[:, u % SPLIT, 0:n].rearrange("p (k c) -> p k c", c=cols),
                        w_lo[:, u % SPLIT, 0:n].rearrange("p (k c) -> p k c", c=cols))

            def feature_tile(u, n, src_hi, src_lo, ready=None, base=0, i=None, kt=KD, k0=0, cols=P, c0=0, width=P, order=None):
                wh, wl = slot(u, cols)
                pe.wait_ge(lo_ready, u + 1 + (0 if i is None else 16 * (i - 1)))
                wait_bank(pe, n, i)
                for j, k in enumerate(order or range(kt)):
                    if ready is not None:
                        pe.wait_ge(ready, base + j + 1)
                    c = slice(c0, c0 + width)
                    ins = mm3(bank[n % 2][0:width, :], wh[:, k, c], wl[:, k, c], src_hi[:, k0 + k, :],
                              src_lo[:, k0 + k, :], j == 0, j == kt - 1)
                ins.then_inc(tile_done, 1)

            def tile_pair(u, n, hs, cols=(P, P)):
                for d in range(2):
                    pe.wait_ge(lo_ready, u + d + 1)
                    wait_bank(pe, n + d)
                for k in range(KD):
                    pe.wait_ge(h_ready, hs + k + 1)
                    for d in range(2):
                        wh, wl = slot(u + d, cols[d])
                        ins = mm3(bank[(n + d) % 2][0:cols[d], :], wh[:, k, :], wl[:, k, :], h_hi[:, k, :], h_lo[:, k, :],
                                  k == 0, k == KD - 1)
                        if k == KD - 1:
                            ins.then_inc(tile_done, 1)

            def sum_squares(j, k, total=KD, dst=misc, first=None, last=None):
                pe.wait_ge(sq_ready[j], k + 1)
                nc.tensor.matmul(dst[:, :], ones[:, :], sq[:, k % 2, :], start=(k == 0 if first is None else first),
                                 stop=(k == total - 1 if last is None else last)).then_inc(sq_used[j], 1)

            def norm_sums(j):
                for k in range(KD):
                    sum_squares(j, k)

            def output_sum(j):
                pe.wait_ge(sq_used[j], KD - 3)
                nc.tensor.matmul(misc[:, :], ones[:, :], acc, start=True, stop=False)
                for m in (KD - 2, KD - 1):
                    pe.wait_ge(sq_ready[j], m + 1)
                    ins = nc.tensor.matmul(misc[:, :], ones[:, :], squares[m % 2], start=False, stop=m == KD - 1)
                ins.then_inc(sum_done[j], 1)

            def residual_sum(j):
                pe.wait_ge(sq_x, j // 2)
                nc.tensor.matmul(s_bank[0], ones[:, :], acc, start=True, stop=True).then_inc(sum_done[j], 1)

            pe.wait_ge(consts_ready, 4)
            pe.wait_ge(vec_in, 16 * 9)
            nc.tensor.transpose(misc[:, 0:V_ROWS], vrows[:, :], ident[0:V_ROWS, 0:V_ROWS]).then_inc(vec_done, 1)
            for k in range(KD):
                n = tile_no[("x", k)]
                pe.wait_ge(x_in[k // 2], 16)
                wait_bank(pe, n)
                for t in range(NT):
                    ins = nc.tensor.transpose(bank[n % 2][:, t * P:(t + 1) * P], x_tok[:, t, k * P:(k + 1) * P], ident[:, :])
                ins.then_inc(tile_done, 1)
            pe.wait_ge(vec_ready, 1)
            norm_sums(0)

            tile_pair(unit_no[("ga", 0)], tile_no[("ga", 0)], 0, (GATE_RANK, P))

            def project(tile, col):
                n = tile_no[tile]
                what, i = tile
                if what == "z":
                    pe.wait_ge(ga_ready, 1)
                    wait_bank(pe, n)
                    nc.tensor.matmul(bank[n % 2][:, :], w_gate[:, i * P:(i + 1) * P], ga_t[:, :], start=True,
                                     stop=True).then_inc(tile_done, 1)
                    return
                if what == "w":
                    pe.wait_ge(v_raw, i + 1)
                    wait_bank(pe, n)
                    for t in range(NT):
                        ins = nc.tensor.transpose(bank[n % 2][:, t * P:(t + 1) * P],
                                                  vbuf[:, i % 4, t * P:(t + 1) * P], ident[:, :])
                    ins.then_inc(tile_done, 1)
                    return
                feature_tile(unit_no[tile], n, h_hi, h_lo)

            def head_rows(o):
                w_ = P if HEAD[o] < 4 else GLA_DK
                first = (o - FIRST[PACK_OF[o]]) * w_
                return slice(first, first + w_)

            def pairs(o, c):
                p, idx, r, s = PACK_OF[o], o * NT + c, head_rows(o), slice(c * P, (c + 1) * P)
                pe.wait_ge(xl_ready, (p + 1) * (LEVELS + 2))
                if idx >= 2:
                    pe.wait_ge(p_read, idx - 1)
                else:
                    pe.wait_ge(p_zero, idx + 1)
                for lv in range(2):
                    L = 64 >> lv
                    for b in range(0, P, 2 * L):
                        nc.tensor.matmul(pp[idx % 2][b:b + L, 0, b + L:b + 2 * L], xls[p % 2][r, lv, c * P + b:c * P + b + L],
                                         xls[p % 2][r, lv, c * P + b + L:c * P + b + 2 * L], start=True, stop=True)
                for lv in range(2, LEVELS):
                    nc.tensor.matmul(pp[idx % 2][:, lv - 1, :], xls[p % 2][r, lv, s], xls[p % 2][r, lv, s],
                                     start=True, stop=True)
                nc.tensor.matmul(pp[idx % 2][:, PAIRS - 1, :], ks[p % 3][r, s], qs[p % 3][r, s], start=True,
                                 stop=True).then_inc(p_done, 1)

            def outputs(o, c):
                p, idx, r, s = PACK_OF[o], o * NT + c, head_rows(o), slice(c * P, (c + 1) * P)
                if c == 0:
                    pe.wait_ge(v_ready, o + 1)
                    if o >= 1:
                        pe.wait_ge(o_read, o)
                pe.wait_ge(a_ready, idx + 1)
                ins = nc.tensor.matmul(po[:, s], vbuf[:, o % 4, s], a_sb[:, idx % 4, :], start=True, stop=(c == 0))
                if c >= 1:
                    pe.wait_ge(state_ready, p + 1)
                    ins = nc.tensor.matmul(po[:, s], state[r, c - 1, :], qes[p % 2][r, s], start=False, stop=True)
                if c == NT - 1:
                    ins.then_inc(o_done, 1)

            misc_read = []

            def head_sum(o):
                pe.wait_ge(o_sq, o + 1)
                pe.wait_ge(*misc_read[-1])
                misc_read.append((o_rinv, o + 1))
                nc.tensor.matmul(misc[:, :], ones[:, :], sq[:, 0, :], start=True, stop=True).then_inc(o_sum, 1)

            def transpose_keys(p):
                pe.wait_ge(xl_ready, (p + 1) * (LEVELS + 2))
                if misc_read:
                    pe.wait_ge(*misc_read[-1])
                misc_read.append((ket_ready, p + 1))
                for c in range(NT - 1):
                    ins = nc.tensor.transpose(misc[:, c * P:(c + 1) * P], ke[:, c * P:(c + 1) * P], ident[:, :])
                ins.then_inc(ket_done, 1)

            def chunk_states(p):
                heads = [o for o in range(8) if PACK_OF[o] == p]
                pe.wait_ge(ket_ready, p + 1)
                pe.wait_ge(v_ready, heads[-1] + 1)
                pe.wait_ge(*misc_read[-1])
                misc_read.append((state_ready, p + 1))
                for c in range(NT - 1):
                    s = slice(c * P, (c + 1) * P)
                    for o in heads:
                        r = head_rows(o)
                        ins = nc.tensor.matmul(misc[r, s], ke_t[:, c, r], vbuf[:, o % 4, s], start=True, stop=True)
                ins.then_inc(kv_done, 1)

            for i, (tile, col, items, groups, end) in enumerate(SLOTS):
                if tile is not None and i > 0:
                    project(tile, col)
                for o, c in OUTPUTS[i]:
                    outputs(o, c)
                for o in SUMS[i]:
                    head_sum(o)
                for o, c in groups:
                    first = FIRST[PACK_OF[o]] == o
                    if c == 0 and first:
                        transpose_keys(PACK_OF[o])
                    pairs(o, c)
                    if c == 2 and first:
                        chunk_states(PACK_OF[o])

            def linear_out(name, j, ready):
                for m in range(KD):
                    feature_tile(unit_no[(name, m)], tile_no[(name, m)], a_hi, a_lo, ready if m == 0 else None,
                                 order=HEAD if name == "eo" else None)
                    for k in ([m - 1] if m >= 1 else []) + ([m] if m == KD - 1 else []):
                        if name == "eo":
                            n = tile_no[("x2", k)]
                            pe.wait_ge(x_again, 16)
                            wait_bank(pe, n)
                            for t in range(NT):
                                ins = nc.tensor.transpose(bank[n % 2][:, t * P:(t + 1) * P],
                                                          x_tok[:, t, k * P:(k + 1) * P], ident[:, :])
                            ins.then_inc(tile_done, 1)
                output_sum(j)

            def mlp(layer, j, hs):
                n0, u0 = tile_no[("mlp", layer, 0, 0)], unit_no[("mlp", layer, 0, 0)]

                def group(g, i=None):
                    n, u = n0 + 2 * KD * g, u0 + 2 * KD * g
                    if g == 0:
                        tile_pair(u, n, hs)
                    for m in range(2 if g == 0 else 0, KD):
                        feature_tile(u + m, n + m, h_hi, h_lo, i=i)
                    for m in range(KD, 2 * KD):
                        ready = hid_ready[layer] if m == KD else None
                        feature_tile(u + m, n + m, a_hi, a_lo, ready, KD * (g if i is None else i), i)

                group(0)
                with pe.Fori(1, GROUPS - 1) as i:
                    group(1, i)
                residual_sum(j - 1)
                group(GROUPS - 1)
                output_sum(j)

            linear_out("eo", 1, mix_ready)
            mlp(0, 3, KD)

            for i, m in enumerate(LATENTS + [5, 6]):
                if i == 0:
                    tile_pair(unit_no[("oi", m)], tile_no[("oi", m)], 2 * KD)
                elif i >= 2:
                    feature_tile(unit_no[("oi", m)], tile_no[("oi", m)], h_hi, h_lo)
                if 1 <= i <= 2:
                    if i == 1:
                        pe.wait_ge(r_ready[3], 1)
                    sum_squares(8, i - 1, dst=po, first=i == 1, last=i == 2)
                elif 3 <= i <= 5:
                    sum_squares(8, i - 1, first=i == 3, last=i == 5)
                if i == 4:
                    residual_sum(4)
            for g in range(2):
                u = unit_no[("mv", g)]
                wh, wl = slot(u, T)
                pe.wait_ge(lo_ready, u + 1)
                for t in range(NT):
                    n = tile_no[("mv", g, t)]
                    s = slice(t * P, (t + 1) * P)
                    wait_bank(pe, n)
                    for k in range(KV_RANK_T):
                        pe.wait_ge(h_ready, 3 * KD + k + 1)
                        ins = mm3(bank[n % 2][:, :], a_hi[:, 3 + k, s], a_lo[:, 3 + k, s], wh[:, k, :], wl[:, k, :],
                                  k == 0, k == KV_RANK_T - 1)
                    ins.then_inc(tile_done, 1)
            for g in range(2):
                for j in range(4):
                    feature_tile(unit_no[("mk", g)], tile_no[("mk", g, j)], a_hi, a_lo, kt=KV_RANK_T, k0=3, cols=T, c0=j * P)

            def project_q(a):
                for what in ("qn", "qr"):
                    for hh in range(2):
                        feature_tile(unit_no[(what, a)], tile_no[(what, a, hh)], h_hi, h_lo,
                                     h_ready if a == 0 else None, 3 * KD + 2, kt=Q_RANK_T, cols=2 * P, c0=hh * P)

            def scores(j):
                h, qb = divmod(j, 4)
                a, hh = divmod(h, 2)
                s = slice(qb * P, (qb + 1) * P)
                r = slice(hh * ROPE, (hh + 1) * ROPE)
                width = (qb + 1) * P
                dst = s_bank[j % 3]
                if j >= 3:
                    pe.wait_ge(prob_exp, j - 2)
                if qb == 0 and hh == 0:
                    pe.wait_ge(qr_ready, a + 1)
                    wait_read(pe, tile_no[("qn", a, 1)])
                nc.tensor.matmul(dst[:, 0:width], qr[r, a % 2, s], kr[r, 0:width], start=True, stop=False)
                nc.tensor.matmul(dst[:, 0:width], qn[:, a % 2, hh, s], y[:, h, 0:width], start=False, stop=False)
                nc.tensor.matmul(dst[:, width - P:width], mask_q[:, :], mask_k[:, :], start=False,
                                 stop=True).then_inc(s_done, 1)

            def transposes(j):
                pe.wait_ge(prob_ready, j + 1)
                if j >= 2:
                    pe.wait_ge(pt_ready, j - 1)
                for kb in range(j % 4 + 1):
                    ins = nc.tensor.transpose(t_bank[j % 2][:, kb, :], prob[:, j % 3, kb * P:(kb + 1) * P], ident[:, :])
                ins.then_inc(pt_done, 1)

            def values(h):
                pe.wait_ge(pt_ready, 4 * h + 4)
                if h >= 1:
                    pe.wait_ge(att_ready, h)
                for kb in range(NT):
                    ins = nc.tensor.matmul(po[:, kb * P:T], v_tok[:, kb, h * P:(h + 1) * P], p_t[:, kb, kb * P:T],
                                           start=(kb == 0), stop=(kb == NT - 1))
                ins.then_inc(pv_done, 1)

            project_q(0)
            pe.wait_ge(consts_ready, 6)
            pe.wait_ge(rope_ready, 1)
            pe.wait_ge(r_ready[8], 2)
            pe.wait_ge(ms_ready, 4)
            for j in range(4 * MLA_HEADS + 2):
                if j % 8 == 0 and j // 8 + 1 < MLA_HEADS // 2:
                    project_q(j // 8 + 1)
                if j < 4 * MLA_HEADS:
                    scores(j)
                if j >= 6 and j % 4 == 2:
                    values(j // 4 - 1)
                if 2 <= j:
                    transposes(j - 2)
            values(MLA_HEADS - 1)
            linear_out("oo", 5, att_ready)
            mlp(1, 7, 3 * KD + 5)

            for m in range(2 * NT):
                half, t = divmod(m, NT)
                n = tile_no[("out", m)]
                pe.wait_ge(x_new, 3 * KD + 2 * (half + 1))
                pe.wait_ge(x_odd, 2 * (half + 1))
                wait_bank(pe, n)
                for k in range(4):
                    ins = nc.tensor.transpose(bank[n % 2][:, k * P:(k + 1) * P],
                                              xT[:, 4 * half + k, t * P:(t + 1) * P], ident[:, :])
                ins.then_inc(tile_done, 1)


_INS = ["x", "positions", "norm_gains", "ev_w_in", "hg_lb_table", "gla_w_gate", "gla_b_gate", "hg_out_norm",
        "gla_out_norm", "ev_w_out", "od_w_in", "mla_q_norm", "mla_w_uq", "mla_kv_norm", "mla_w_ukv", "od_w_out",
        "mlp_w1", "mlp_w2"]


def kernel(**inputs):
    import numpy as np
    import concourse.bacc as _bacc
    from concourse.bass_utils import run_bass_kernel_spmd as _run

    inv_freq = np.float32(10000.0) ** (-np.arange(0, ROPE, 2, dtype=np.float32) / np.float32(ROPE))
    sign = np.repeat(np.array([-1.0, 1.0], np.float32), ROPE // 2)
    rope_const = np.stack([np.tile(inv_freq, 4), np.tile(sign, 2)], axis=1).astype(np.float32)

    nc = _bacc.Bacc("TRN2", target_bir_lowering=False, num_devices=1)
    arrays = {f"in_{n}": np.ascontiguousarray(inputs[n]) for n in _INS}
    arrays["rope_const"] = rope_const
    args = [nc.dram_tensor(n, a.shape, mybir.dt.from_np(a.dtype), kind="ExternalInput").ap() for n, a in arrays.items()]
    out = nc.dram_tensor("out_0", (1, T, D), F32, kind="ExternalOutput").ap()
    trunk(nc, *args, out)
    r = _run(nc, [arrays], core_ids=[0])
    return r.results[0]["out_0"]
```
